# Optimizing a Trainium2 kernel written in Bass

```python
import math
import jax, jax.numpy as jnp
from jax import lax
import numpy as np

D_MODEL = 1024
BATCH = 1
SEQ = 2048
DEPTH = 1

CHUNK = 64
Q_BLOCK = 128
EPS = 1e-6

MLA_HEADS = 8
MLA_NOPE = 64
MLA_ROPE = 32
MLA_V = 64
MLA_Q_RANK = 256
MLA_KV_RANK = 128
MLA_WIDTH = MLA_HEADS * MLA_V
MLA_QK_DIM = MLA_NOPE + MLA_ROPE
ROPE_THETA = 10000.0

FOX_HEADS = 8
FOX_HEAD_DIM = 64
FOX_WIDTH = FOX_HEADS * FOX_HEAD_DIM

S5_WIDTH = 512
S5_GROUP = 16
S5_GROUPS = S5_WIDTH // S5_GROUP
S5_STATE = 64
DT_MIN = 1e-3
DT_MAX = 1e-1

BRANCH_WIDTH = MLA_WIDTH + FOX_WIDTH + S5_WIDTH
IN_SPLITS = (MLA_Q_RANK, MLA_KV_RANK, MLA_ROPE,
             FOX_WIDTH, FOX_WIDTH, FOX_WIDTH, FOX_HEADS,
             S5_WIDTH,
             MLA_WIDTH, FOX_WIDTH, S5_WIDTH,
             D_MODEL, D_MODEL, D_MODEL)
IN_WIDTH = MLA_Q_RANK + MLA_KV_RANK + MLA_ROPE + 3 * FOX_WIDTH + FOX_HEADS + S5_WIDTH + BRANCH_WIDTH + 3 * D_MODEL

kernel_name = "hybrid_mla_fox_s5_gated_trunk"

def rmsnorm(x, g):
    xf = x.astype(jnp.float32)
    y = xf * lax.rsqrt(jnp.mean(xf * xf, axis=-1, keepdims=True) + EPS)
    return (y * g.astype(jnp.float32)).astype(x.dtype)

def rope_tables(positions, dtype):
    inv = 1.0 / (ROPE_THETA ** (jnp.arange(0, MLA_ROPE, 2, dtype=jnp.float32) / MLA_ROPE))
    ang = positions.astype(jnp.float32)[..., None] * inv
    return jnp.cos(ang).astype(dtype)[:, :, None, :], jnp.sin(ang).astype(dtype)[:, :, None, :]

def apply_rope(x, cos, sin):
    x1, x2 = jnp.split(x, 2, axis=-1)
    return jnp.concatenate([x1 * cos - x2 * sin, x1 * sin + x2 * cos], axis=-1)

def swept_attention(q, k, v, scale, chunk_causal, cum_logf=None):
    S = q.shape[1]
    outs = []
    for i in range(S // Q_BLOCK):
        q0, q1 = i * Q_BLOCK, (i + 1) * Q_BLOCK
        kv_end = q1
        logits = jnp.einsum('bqhd,bkhd->bhqk', q[:, q0:q1], k[:, :kv_end]).astype(jnp.float32) * scale
        qpos = jnp.arange(q0, q1)[:, None]
        kpos = jnp.arange(kv_end)[None, :]
        if chunk_causal:
            allowed = (kpos // CHUNK) <= (qpos // CHUNK)
        else:
            allowed = kpos <= qpos
        if cum_logf is not None:
            c_q = jnp.transpose(cum_logf[:, q0:q1], (0, 2, 1))[..., :, None]
            c_k = jnp.transpose(cum_logf[:, :kv_end], (0, 2, 1))[..., None, :]
            logits = logits + (c_q - c_k)
        logits = jnp.where(allowed, logits, -jnp.inf)
        p = jax.nn.softmax(logits, axis=-1).astype(v.dtype)
        outs.append(jnp.einsum('bhqk,bkhd->bqhd', p, v[:, :kv_end]))
    return jnp.concatenate(outs, axis=1)

def mla_branch(cq, ckv, kpe, cos, sin, q_a_norm, w_q_up, kv_a_norm, w_kv_up, q_norm, k_norm):
    Bsz, S, _ = cq.shape
    q = (rmsnorm(cq, q_a_norm) @ w_q_up).reshape(Bsz, S, MLA_HEADS, MLA_QK_DIM)
    q_nope, q_pe = jnp.split(q, [MLA_NOPE], axis=-1)
    kv = (rmsnorm(ckv, kv_a_norm) @ w_kv_up).reshape(Bsz, S, MLA_HEADS, MLA_NOPE + MLA_V)
    k_nope, v = jnp.split(kv, [MLA_NOPE], axis=-1)
    k_pe = apply_rope(kpe[:, :, None, :], cos, sin)
    q = jnp.concatenate([q_nope, apply_rope(q_pe, cos, sin)], axis=-1)
    k = jnp.concatenate([k_nope, jnp.broadcast_to(k_pe, (Bsz, S, MLA_HEADS, MLA_ROPE))], axis=-1)
    q = rmsnorm(q, q_norm)
    k = rmsnorm(k, k_norm)
    y = swept_attention(q, k, v, 1.0 / math.sqrt(MLA_QK_DIM), chunk_causal=True)
    return y.reshape(Bsz, S, MLA_WIDTH)

def fox_branch(fq, fk, fv, ff, b_f, q_norm, k_norm):
    Bsz, S, _ = fq.shape
    q = rmsnorm(fq.reshape(Bsz, S, FOX_HEADS, FOX_HEAD_DIM), q_norm)
    k = rmsnorm(fk.reshape(Bsz, S, FOX_HEADS, FOX_HEAD_DIM), k_norm)
    v = fv.reshape(Bsz, S, FOX_HEADS, FOX_HEAD_DIM)
    log_f = jax.nn.log_sigmoid(ff.astype(jnp.float32) + b_f.astype(jnp.float32))
    cum = jnp.cumsum(log_f, axis=1)
    y = swept_attention(q, k, v, 1.0 / math.sqrt(FOX_HEAD_DIM), chunk_causal=False, cum_logf=cum)
    return y.reshape(Bsz, S, FOX_WIDTH)

def _ssm_combine(e1, e2):
    a1r, a1i, b1r, b1i = e1
    a2r, a2i, b2r, b2i = e2
    return (a2r * a1r - a2i * a1i,
            a2r * a1i + a2i * a1r,
            a2r * b1r - a2i * b1i + b2r,
            a2r * b1i + a2i * b1r + b2i)

def s5_branch(u, lam_re, lam_im, log_dt, b_re, b_im, c_re, c_im, d_skip, w_glu, b_glu):
    Bsz, S, _ = u.shape
    uf = u.astype(jnp.float32).reshape(Bsz, S, S5_GROUPS, S5_GROUP)
    dt = jnp.exp(log_dt.astype(jnp.float32))[:, None]
    lr = lam_re.astype(jnp.float32)
    li = lam_im.astype(jnp.float32)
    mag = jnp.exp(lr * dt)
    a_re = mag * jnp.cos(li * dt)
    a_im = mag * jnp.sin(li * dt)
    den = lr * lr + li * li
    f_re = ((a_re - 1.0) * lr + a_im * li) / den
    f_im = (a_im * lr - (a_re - 1.0) * li) / den
    br = b_re.astype(jnp.float32)
    bi = b_im.astype(jnp.float32)
    bb_re = f_re[..., None] * br - f_im[..., None] * bi
    bb_im = f_re[..., None] * bi + f_im[..., None] * br
    bu_re = jnp.einsum('bsgc,gnc->bsgn', uf, bb_re)
    bu_im = jnp.einsum('bsgc,gnc->bsgn', uf, bb_im)
    a_re_full = jnp.broadcast_to(a_re, bu_re.shape)
    a_im_full = jnp.broadcast_to(a_im, bu_re.shape)
    _, _, x_re, x_im = lax.associative_scan(_ssm_combine, (a_re_full, a_im_full, bu_re, bu_im), axis=1)
    y = (jnp.einsum('bsgn,gcn->bsgc', x_re, c_re.astype(jnp.float32))
         - jnp.einsum('bsgn,gcn->bsgc', x_im, c_im.astype(jnp.float32)))
    y = (y + d_skip.astype(jnp.float32).reshape(S5_GROUPS, S5_GROUP) * uf).reshape(Bsz, S, S5_WIDTH)
    z = jax.nn.gelu(y)
    z = z * jax.nn.sigmoid(z @ w_glu.astype(jnp.float32) + b_glu.astype(jnp.float32))
    return z.astype(u.dtype)

def hybrid_layer(x, cos, sin, norm_g, w_in,
                 mla_q_a_norm, mla_w_q_up, mla_kv_a_norm, mla_w_kv_up, mla_q_norm, mla_k_norm,
                 fox_b_f, fox_q_norm, fox_k_norm,
                 s5_lambda_re, s5_lambda_im, s5_log_dt, s5_b_re, s5_b_im, s5_c_re, s5_c_im,
                 s5_d, s5_w_glu, s5_b_glu, w_branch_out, w_out):
    h = rmsnorm(x, norm_g)
    proj = h @ w_in
    offsets = np.cumsum(IN_SPLITS)[:-1].tolist()
    (cq, ckv, kpe, fq, fk, fv, ff, s5u,
     g_mla, g_fox, g_s5, m_mla, m_fox, m_s5) = jnp.split(proj, offsets, axis=-1)

    y_mla = mla_branch(cq, ckv, kpe, cos, sin, mla_q_a_norm, mla_w_q_up,
                       mla_kv_a_norm, mla_w_kv_up, mla_q_norm, mla_k_norm)
    y_fox = fox_branch(fq, fk, fv, ff, fox_b_f, fox_q_norm, fox_k_norm)
    y_s5 = s5_branch(s5u, s5_lambda_re, s5_lambda_im, s5_log_dt, s5_b_re, s5_b_im,
                     s5_c_re, s5_c_im, s5_d, s5_w_glu, s5_b_glu)

    wo_mla, wo_fox, wo_s5 = jnp.split(w_branch_out, [MLA_WIDTH, MLA_WIDTH + FOX_WIDTH], axis=0)
    o_mla = (y_mla * jax.nn.silu(g_mla)) @ wo_mla
    o_fox = (y_fox * jax.nn.silu(g_fox)) @ wo_fox
    o_s5 = (y_s5 * jax.nn.silu(g_s5)) @ wo_s5
    merged = jax.nn.sigmoid(m_mla) * o_mla + jax.nn.sigmoid(m_fox) * o_fox + jax.nn.sigmoid(m_s5) * o_s5
    return x + merged @ w_out

def setup_inputs(seed: int = 0) -> dict:
    key = jax.random.key(seed)
    ks = jax.random.split(key, 32)
    f32 = jnp.float32

    def nrm(k, shape, scale):
        return jax.random.normal(k, shape, f32) * scale

    def gain(k, shape):
        return 1.0 + 0.02 * jax.random.normal(k, shape, f32)

    L = DEPTH
    x = jax.random.normal(ks[0], (BATCH, SEQ, D_MODEL), f32)
    start = jax.random.randint(ks[1], (BATCH, 1), 0, 4096, dtype=jnp.int32)
    positions = start + jnp.arange(SEQ, dtype=jnp.int32)[None, :]
    n_idx = jnp.arange(S5_STATE, dtype=f32)
    log_dt = jax.random.uniform(ks[17], (L, S5_GROUPS), f32, math.log(DT_MIN), math.log(DT_MAX))
    return {
        "x": x,
        "positions": positions,
        "norm_g": gain(ks[2], (L, D_MODEL)),
        "w_in": nrm(ks[3], (L, D_MODEL, IN_WIDTH), D_MODEL ** -0.5),
        "mla_q_a_norm": gain(ks[4], (L, MLA_Q_RANK)),
        "mla_w_q_up": nrm(ks[5], (L, MLA_Q_RANK, MLA_HEADS * MLA_QK_DIM), MLA_Q_RANK ** -0.5),
        "mla_kv_a_norm": gain(ks[6], (L, MLA_KV_RANK)),
        "mla_w_kv_up": nrm(ks[7], (L, MLA_KV_RANK, MLA_HEADS * (MLA_NOPE + MLA_V)), MLA_KV_RANK ** -0.5),
        "mla_q_norm": gain(ks[8], (L, MLA_QK_DIM)),
        "mla_k_norm": gain(ks[9], (L, MLA_QK_DIM)),
        "fox_b_f": 1.0 + 0.5 * jax.random.normal(ks[10], (L, FOX_HEADS), f32),
        "fox_q_norm": gain(ks[11], (L, FOX_HEAD_DIM)),
        "fox_k_norm": gain(ks[12], (L, FOX_HEAD_DIM)),
        "s5_lambda_re": -0.5 * (1.0 + 0.02 * jax.random.normal(ks[13], (L, S5_GROUPS, S5_STATE), f32)),
        "s5_lambda_im": math.pi * n_idx + 0.01 * jax.random.normal(ks[14], (L, S5_GROUPS, S5_STATE), f32),
        "s5_log_dt": log_dt,
        "s5_b_re": nrm(ks[15], (L, S5_GROUPS, S5_STATE, S5_GROUP), (2.0 * S5_GROUP) ** -0.5),
        "s5_b_im": nrm(ks[16], (L, S5_GROUPS, S5_STATE, S5_GROUP), (2.0 * S5_GROUP) ** -0.5),
        "s5_c_re": nrm(ks[18], (L, S5_GROUPS, S5_GROUP, S5_STATE), (2.0 * S5_STATE) ** -0.5),
        "s5_c_im": nrm(ks[19], (L, S5_GROUPS, S5_GROUP, S5_STATE), (2.0 * S5_STATE) ** -0.5),
        "s5_d": nrm(ks[20], (L, S5_WIDTH), 1.0),
        "s5_w_glu": nrm(ks[21], (L, S5_WIDTH, S5_WIDTH), S5_WIDTH ** -0.5),
        "s5_b_glu": nrm(ks[22], (L, S5_WIDTH), 0.02),
        "w_branch_out": nrm(ks[23], (L, BRANCH_WIDTH, D_MODEL), MLA_WIDTH ** -0.5),
        "w_out": nrm(ks[24], (L, D_MODEL, D_MODEL), D_MODEL ** -0.5),
    }

def reference(x, positions, norm_g, w_in,
              mla_q_a_norm, mla_w_q_up, mla_kv_a_norm, mla_w_kv_up, mla_q_norm, mla_k_norm,
              fox_b_f, fox_q_norm, fox_k_norm,
              s5_lambda_re, s5_lambda_im, s5_log_dt, s5_b_re, s5_b_im, s5_c_re, s5_c_im,
              s5_d, s5_w_glu, s5_b_glu, w_branch_out, w_out):
    cos, sin = rope_tables(positions, x.dtype)
    h = x
    for l in range(DEPTH):
        h = hybrid_layer(h, cos, sin, norm_g[l], w_in[l],
                         mla_q_a_norm[l], mla_w_q_up[l], mla_kv_a_norm[l], mla_w_kv_up[l],
                         mla_q_norm[l], mla_k_norm[l],
                         fox_b_f[l], fox_q_norm[l], fox_k_norm[l],
                         s5_lambda_re[l], s5_lambda_im[l], s5_log_dt[l], s5_b_re[l], s5_b_im[l],
                         s5_c_re[l], s5_c_im[l], s5_d[l], s5_w_glu[l], s5_b_glu[l],
                         w_branch_out[l], w_out[l])
    return h


_drawn_inputs = setup_inputs


def setup_inputs(seed=0):
    import zlib

    import numpy as np

    out = dict(_drawn_inputs(seed))
    spreads = {}
    factors = {'norm_g': 8.0,
     'mla_q_a_norm': 8.0,
     'mla_kv_a_norm': 8.0,
     'mla_q_norm': 8.0,
     'mla_k_norm': 8.0,
     'fox_q_norm': 8.0,
     'fox_k_norm': 8.0,
     's5_lambda_re': 64.0,
     's5_lambda_im': 64.0,
     's5_log_dt': 64.0,
     's5_b_re': 64.0,
     's5_b_im': 64.0,
     's5_c_re': 64.0,
     's5_c_im': 64.0,
     's5_b_glu': 54.559}
    for name, (base, spread) in spreads.items():
        noise = np.random.default_rng([zlib.crc32(name.encode()), seed]).standard_normal(out[name].shape)
        drawn = base * np.exp(spread * noise) if base else spread * noise
        out[name] = __import__('jax').numpy.asarray(drawn.astype(out[name].dtype))
    for name, factor in factors.items():
        out[name] = (out[name] * factor).astype(out[name].dtype)
    return out
```

```python
import math
from contextlib import ExitStack

import numpy as np

import concourse.bass as bass
from concourse import mybir

P = 128
F32 = mybir.dt.float32
BF16 = mybir.dt.bfloat16
I32 = mybir.dt.int32
ALU = mybir.AluOpType
ACT = mybir.ActivationFunctionType
AX = mybir.AxisListType

D = 1024
S = 2048
KD = D // P
NT = S // P
H = 8
Q_RANK, KV_RANK, ROPE, NOPE, HD = 256, 128, 32, 64, 64
MQ = NOPE + ROPE
FQ = HD + 2
WIDTH = H * HD
GROUPS, GC, NS = 32, 16, 64
EPS = 1e-6
CH = 512
STEP = 8
NC_ = S // STEP
GB = 8
NB = GROUPS // GB
MAGIC = 1.5 * 2.0 ** 23
TWO_PI = 2.0 * math.pi
C1 = 6.28125
C2 = float(np.float32(math.floor((TWO_PI - C1) * 2 ** 20) / 2 ** 20))
C3 = TWO_PI - C1 - C2
PI_F32 = 3.1415925
MASKED = -1.0e30


class Steps:

    def __init__(self, eng, sem, base=0):
        self.eng, self.sem, self.base, self.n = eng, sem, base, 0

    def do(self, ins):
        ins.then_inc(self.sem, 1)
        self.n += 1

    def join(self):
        self.eng.wait_ge(self.sem, self.base + self.n)

    def then(self, ins):
        self.do(ins)
        self.join()


def wait_alone(eng, sem, value, tick):
    eng.wait_ge(sem, value)
    eng.sem_inc(tick, 1)


class Mem:

    def __init__(self, nc, ctx, tag):
        self.nc, self.ctx, self.tag = nc, ctx, tag

    def sb(self, name, shape, dt=F32):
        return self.ctx.enter_context(self.nc.sbuf_tensor(f"{self.tag}_{name}", shape, dt))

    def ps(self, name, shape, dt=F32):
        return self.ctx.enter_context(self.nc.psum_tensor(f"{self.tag}_{name}", shape, dt))

    def sem(self, name):
        return self.ctx.enter_context(self.nc.semaphore(f"{self.tag}_{name}"))


def norm_x(nc, a, keep):
    with ExitStack() as ctx:
        m = Mem(nc, ctx, "nx")
        x_in = m.sb("x_in", [P, 2, D])
        square = m.sb("square", [P, D])
        h = m.sb("h", [P, 2, D])
        hT = m.sb("hT", [P, 2, KD, P])
        gain = m.sb("gain", [P, KD])
        w_ff = m.sb("w_ff", [P, KD, H])
        ff = m.sb("ff", [P, NT, H])
        b_f = m.sb("b_f", [P, H])
        stat = m.sb("stat", [P, 2, 3])
        lf = m.sb("lf", [P, 4, NT * H])
        tri = m.sb("tri", [P, P])
        ones = m.sb("ones", [P, P])
        total = m.sb("total", [P, NT, H])
        ident = keep["ident"]
        t_ps = [m.ps(f"t{i}", [P, 4, P]) for i in range(4)]
        ff_ps = [m.ps(f"ff{i}", [P, CH]) for i in range(2)]
        cum_ps = m.ps("cum_ps", [P, NT * H])
        tot_ps = m.ps("tot_ps", [P, NT * H])

        params_in = m.sem("params_in")
        x_loaded = [m.sem(f"x_loaded{b}") for b in range(2)]
        consts_set = m.sem("consts_set")
        h_done = m.sem("h_done")
        squared = m.sem("squared")
        mean_ready = m.sem("mean_ready")
        root_ready = m.sem("root_ready")
        transposed = m.sem("transposed")
        hT_copied = m.sem("hT_copied")
        hT_stored = [m.sem(f"hT_stored{b}") for b in range(2)]
        ff_done = m.sem("ff_done")
        ff_copied = m.sem("ff_copied")
        logs = m.sem("logs")
        summed = m.sem("summed")
        own = m.sem("own")
        tick = m.sem("tick")

        with nc.Block() as block:
            @block.sync
            def _(sp):
                sp.dma_start(gain[:, :], a["norm_g"]).then_inc(params_in, 16)
                sp.dma_start(w_ff[:, :, :], a["w_ff"]).then_inc(params_in, 16)
                sp.dma_start(b_f[:, :], a["fox_b_f"].partition_broadcast(P)).then_inc(params_in, 16)
                for b in range(2):
                    sp.sem_inc(hT_stored[b], 1)
                with sp.Fori(0, NT // 2) as i:
                    for b in range(2):
                        wait_alone(sp, hT_copied, 4 * i + 2 * b + 3, tick)
                        sp.dma_start(a["hT"][2 * i + b], hT[:, b, :, :].rearrange("p k t -> p (k t)")).then_inc(hT_stored[b], 16)
                for b in range(2):
                    sp.wait_ge(hT_stored[b], 16 * (NT // 2) + 1)

            @block.gpsimd
            def _(pool):
                pool.memset(ones[:, :], 1.0).then_inc(consts_set, 1)
                pool.memset(ident[:, :], 0.0).then_inc(consts_set, 1)
                pool.wait_ge(consts_set, 2)
                pool.affine_select(out=ident[:, :], in_=ident[:, :], compare_op=ALU.not_equal, fill=1.0,
                                   base=0, pattern=[[-1, P]], channel_multiplier=1).then_inc(consts_set, 1)
                pool.affine_select(out=tri[:, :], in_=ones[:, :], compare_op=ALU.is_ge, fill=0.0,
                                   base=0, pattern=[[1, P]], channel_multiplier=-1).then_inc(consts_set, 1)
                with pool.Fori(0, NT // 2) as i:
                    for b in range(2):
                        wait_alone(pool, h_done, 2 * i + b + 1, tick)
                        pool.dma_start(x_in[:, b, :], a["x"][2 * i + b]).then_inc(x_loaded[b], 16)

            @block.scalar
            def _(act):
                with act.Fori(0, NT // 2) as i:
                    for b in range(2):
                        act.wait_ge(x_loaded[b], 16 * i + 16)
                        act.wait_ge(mean_ready, 2 * i + b + 1)
                        nc.scalar.activation(square[:, :], x_in[:, b, :], ACT.Square,
                                             accum_out=stat[:, b, 0:1]).then_inc(squared, 1)
                        act.wait_ge(mean_ready, 2 * i + b + 2)
                        nc.scalar.activation(stat[:, b, 2:3], stat[:, b, 1:2], ACT.Sqrt).then_inc(root_ready, 1)
                act.wait_ge(logs, 1)
                nc.scalar.activation(lf[:, 2, :], lf[:, 1, :], ACT.Exp, scale=-1.0).then_inc(logs, 1)
                act.wait_ge(logs, 3)
                nc.scalar.activation(lf[:, 3, :], lf[:, 2, :], ACT.Ln).then_inc(logs, 1)

            @block.vector
            def _(dve):
                dve.sem_inc(h_done, 2)
                dve.sem_inc(mean_ready, 1)
                dve.sem_inc(hT_copied, 1)
                dve.sem_inc(ff_copied, 2)
                dve.wait_ge(params_in, 48)
                with dve.Fori(0, NT // 2) as i:
                    st = Steps(nc.vector, own, base=i * 2)
                    for b in range(2):
                        t = 2 * i + b
                        dve.wait_ge(squared, t + 1)
                        nc.vector.tensor_scalar(stat[:, b, 1:2], stat[:, b, 0:1], 1.0 / D, EPS,
                                                ALU.mult, ALU.add).then_inc(mean_ready, 1)
                        dve.wait_ge(root_ready, t + 1)
                        st.then(nc.vector.reciprocal(stat[:, b, 1:2], stat[:, b, 2:3]))
                        dve.wait_ge(transposed, 2 * t + 2)
                        nc.vector.tensor_scalar(h[:, b, :], x_in[:, b, :], stat[:, b, 1:2], None,
                                                ALU.mult).then_inc(h_done, 1)
                        dve.wait_ge(hT_stored[b], 16 * i + 1)
                        dve.wait_ge(ff_done, t + 1)
                        for half in range(2):
                            dve.wait_ge(transposed, 2 * t + half + 5)
                            ks = slice(4 * half, 4 * half + 4)
                            nc.vector.tensor_tensor(hT[:, b, ks, :], t_ps[2 * b + half][:, :, :],
                                                    gain[:, ks].unsqueeze(2).to_broadcast([P, 4, P]),
                                                    ALU.mult).then_inc(hT_copied, 1)
                        dve.wait_ge(ff_done, t + 3)
                        nc.vector.tensor_tensor(ff[:, t, :], ff_ps[b][:, 0:H], b_f[:, :], ALU.add).then_inc(ff_copied, 1)
                dve.wait_ge(ff_copied, NT + 2)
                ff_all = ff[:, :, :].rearrange("p t h -> p (t h)")
                own2 = Steps(nc.vector, own, base=NT)
                own2.then(nc.vector.tensor_scalar(lf[:, 0, :], ff_all, -1.0, None, ALU.mult))
                nc.vector.tensor_tensor(lf[:, 1, :], lf[:, 0, :], ff_all, ALU.max).then_inc(logs, 1)
                dve.wait_ge(logs, 2)
                own2.do(nc.vector.tensor_scalar(lf[:, 0, :], ff_all, 0.0, None, ALU.min))
                nc.vector.tensor_scalar(lf[:, 2, :], lf[:, 2, :], 1.0, None, ALU.add).then_inc(logs, 1)
                dve.wait_ge(logs, 4)
                own2.join()
                nc.vector.tensor_tensor(lf[:, 0, :], lf[:, 0, :], lf[:, 3, :], ALU.subtract).then_inc(logs, 1)
                dve.wait_ge(summed, 1)
                own2.then(nc.vector.memset(total[:, 0, :], 0.0))
                for t in range(1, NT):
                    own2.then(nc.vector.tensor_tensor(total[:, t, :], total[:, t - 1, :],
                                                      tot_ps[:, (t - 1) * H:t * H], ALU.add))
                own2.then(nc.vector.tensor_tensor(keep["cum"][:, :, :].rearrange("p t h -> p (t h)"), cum_ps[:, :],
                                                  total[:, :, :].rearrange("p t h -> p (t h)"), ALU.add))

            @block.tensor
            def _(pe):
                pe.sem_inc(transposed, 4)
                pe.sem_inc(ff_done, 2)
                pe.wait_ge(consts_set, 4)
                pe.wait_ge(params_in, 48)
                with pe.Fori(0, NT // 2) as i:
                    for b in range(2):
                        t = 2 * i + b
                        pe.wait_ge(h_done, t + 3)
                        for half in range(2):
                            for k in range(4 * half, 4 * half + 4):
                                last = nc.tensor.transpose(t_ps[2 * b + half][:, k % 4, :],
                                                           h[:, b, k * P:(k + 1) * P], ident[:, :])
                            last.then_inc(transposed, 1)
                        pe.wait_ge(hT_copied, 2 * t + 3)
                        pe.wait_ge(ff_copied, t + 1)
                        for k in range(KD):
                            last = nc.tensor.matmul(ff_ps[b][:, 0:H], hT[:, b, k, :], w_ff[:, k, :],
                                                    start=(k == 0), stop=(k == KD - 1))
                        last.then_inc(ff_done, 1)
                pe.wait_ge(logs, 5)
                nc.tensor.matmul(cum_ps[:, :], tri[:, :], lf[:, 0, :], start=True, stop=True)
                nc.tensor.matmul(tot_ps[:, :], ones[:, :], lf[:, 0, :], start=True, stop=True).then_inc(summed, 1)


def reduce_angle(nc, st, angle, k):
    st.then(nc.vector.tensor_scalar(k, angle, 1.0 / TWO_PI, MAGIC, ALU.mult, ALU.add))
    st.then(nc.vector.tensor_scalar(k, k, MAGIC, None, ALU.subtract))
    for part in (C1, C2, C3):
        st.then(nc.vector.scalar_tensor_tensor(out=angle, in0=k, scalar=-part, in1=angle,
                                               op0=ALU.mult, op1=ALU.add))
    st.then(nc.vector.tensor_scalar(angle, angle, PI_F32, -PI_F32, ALU.min, ALU.max))


def project(nc, a, keep):
    with ExitStack() as ctx:
        m = Mem(nc, ctx, "pr")
        w_lora = m.sb("w_lora", [P, KD, 416])
        w_fox = m.sb("w_fox", [P, KD, 3 * WIDTH])
        w_u = m.sb("w_u", [P, KD, WIDTH])
        w_q_up = m.sb("w_q_up", [P, 2, H * MQ])
        w_kv_up = m.sb("w_kv_up", [P, H * P])
        hT = m.sb("hT", [P, 2, KD * P])
        lora = m.sb("lora", [P, 416])
        lora_n = m.sb("lora_n", [P, 384])
        loraT = m.sb("loraT", [P, 3, P])
        gain_lora = m.sb("gain_lora", [P, 3])
        fox = m.sb("fox", [P, 2 * WIDTH])
        q_raw = m.sb("q_raw", [P, H * MQ])
        kv_raw = m.sb("kv_raw", [P, H * P])
        fv_out = m.sb("fv_out", [P, 2, WIDTH])
        mv_out = m.sb("mv_out", [P, 2, WIDTH])
        u_out = m.sb("u_out", [P, 2, WIDTH])
        junk = m.sb("junk", [P, 2 * WIDTH])
        rope = m.sb("rope", [P, 4, H * ROPE // 2])
        kpe = m.sb("kpe", [P, ROPE])
        fqk = m.sb("fqk", [P, 2 * H, FQ])
        mqk = m.sb("mqk", [P, 2 * H, MQ])
        gain_f = m.sb("gain_f", [FQ, 2])
        gain_m = m.sb("gain_m", [MQ, 2])
        st_l = m.sb("st_l", [P, 7])
        st_f = m.sb("st_f", [P, 3, 2 * H])
        st_m = m.sb("st_m", [P, 3, 2 * H])
        stage_f = m.sb("stage_f", [FQ, 2, 2 * H, P])
        stage_m = m.sb("stage_m", [MQ, 2, 2 * H, P])
        pos_i = m.sb("pos_i", [P, NT], I32)
        pos = m.sb("pos", [P, NT])
        inv = m.sb("inv", [P, ROPE // 2])
        sin_t = m.sb("sin_t", [P, NT, ROPE // 2])
        cos_t = m.sb("cos_t", [P, NT, ROPE // 2])
        angle = m.sb("angle", [P, NT * ROPE // 2])
        turns = m.sb("turns", [P, NT * ROPE // 2])
        ident, cum = keep["ident"], keep["cum"]
        pj = [m.ps(f"pj{i}", [P, CH]) for i in range(3)]
        tp = [m.ps(f"tp{i}", [P, 4, P]) for i in range(3)]

        weights_in = m.sem("weights_in")
        small_in = m.sem("small_in")
        hT_in = [m.sem(f"hT_in{b}") for b in range(2)]
        hT_used = m.sem("hT_used")
        projected = m.sem("projected")
        evacuated = m.sem("evacuated")
        turned = m.sem("turned")
        turn_out = m.sem("turn_out")
        sums = m.sem("sums")
        roots = m.sem("roots")
        lora_ready = m.sem("lora_ready")
        heads_ready = m.sem("heads_ready")
        raw_used = m.sem("raw_used")
        mv_ready = m.sem("mv_ready")
        stored = [m.sem(f"stored{b}") for b in range(2)]
        tables = m.sem("tables")
        own = m.sem("own")
        tick = m.sem("tick")
        OUTS = 7

        with nc.Block() as block:
            @block.sync
            def _(sp):
                sp.dma_start(w_lora[:, :, :], a["w_lora"]).then_inc(weights_in, 16)
                for k in range(0, KD, 2):
                    sp.dma_start(w_fox[:, k:k + 2, :], a["w_fox"][:, k:k + 2, :]).then_inc(weights_in, 16)
                sp.dma_start(w_u[:, :, :], a["w_u"]).then_inc(weights_in, 16)
                sp.dma_start(w_q_up[:, :, :], a["w_q_up"]).then_inc(weights_in, 16)
                sp.dma_start(w_kv_up[:, :], a["w_kv_up"]).then_inc(weights_in, 16)
                for b in range(2):
                    sp.sem_inc(stored[b], 1)
                with sp.Fori(0, NT // 2) as i:
                    for b in range(2):
                        t = 2 * i + b
                        tok = bass.ds(t * P, P)
                        wait_alone(sp, evacuated, 9 * t + 9 + 3, tick)
                        wait_alone(sp, mv_ready, t + 1, tick)
                        sp.dma_start(a["u"][t], u_out[:, b, :]).then_inc(stored[b], 16)
                        sp.dma_start(a["fv"][t], fv_out[:, b, :]).then_inc(stored[b], 16)
                        sp.dma_start(a["mv"][t], mv_out[:, b, :]).then_inc(stored[b], 16)
                        wait_alone(sp, turn_out, 9 * t + 5 + 3, tick)
                        for j, name in enumerate(("fqT", "fkT")):
                            sp.dma_start(a[name][:, :, tok].rearrange("h d t -> d h t"),
                                         stage_f[:, b, j * H:(j + 1) * H, :]).then_inc(stored[b], 16)
                        wait_alone(sp, turn_out, 9 * t + 9 + 3, tick)
                        for j, name in enumerate(("mqT", "mkT")):
                            sp.dma_start(a[name][:, :, tok].rearrange("h d t -> d h t"),
                                         stage_m[:, b, j * H:(j + 1) * H, :]).then_inc(stored[b], 16)
                for b in range(2):
                    sp.wait_ge(stored[b], 16 * OUTS * (NT // 2) + 1)

            @block.gpsimd
            def _(pool):
                pool.memset(gain_f[:, :], 1.0).then_inc(tables, 1)
                pool.memset(fqk[:, :, HD:FQ], 1.0).then_inc(tables, 1)
                pool.wait_ge(tables, 1)
                for dst, name in ((pos_i[:, :], "positions"), (inv[:, :], "inv_freq"), (gain_lora[:, :], "gain_lora"),
                                  (gain_f[0:HD, 0:1], "fox_q_norm"), (gain_f[0:HD, 1:2], "fox_k_norm"),
                                  (gain_m[:, 0:1], "mla_q_norm"), (gain_m[:, 1:2], "mla_k_norm")):
                    pool.dma_start(dst, a[name]).then_inc(small_in, 16)
                with pool.Fori(0, NT // 2) as i:
                    for b in range(2):
                        wait_alone(pool, hT_used, 2 * i + b + 1, tick)
                        pool.dma_start(hT[:, b, :], a["hT"][2 * i + b]).then_inc(hT_in[b], 16)

            @block.tensor
            def _(pe):
                pe.sem_inc(hT_used, 2)
                pe.wait_ge(weights_in, 16 * 8)
                with pe.Fori(0, NT // 2) as i:
                    for b in range(2):
                        t = 2 * i + b
                        use = {"pj": 0, "tp": 0}

                        def bank():
                            n = use["pj"]
                            use["pj"] += 1
                            pe.wait_ge(evacuated, 9 * t + n + 1)
                            return pj[n % 3]

                        def from_h(w, width):
                            out = bank()
                            for k in range(KD):
                                last = nc.tensor.matmul(out[:, 0:width], hT[:, b, k * P:(k + 1) * P], w(k),
                                                        start=(k == 0), stop=(k == KD - 1))
                            return last.then_inc(projected, 1)

                        def turn(blocks, rows):
                            n = use["tp"]
                            use["tp"] += 1
                            pe.wait_ge(turn_out, 9 * t + n + 1)
                            for j, src in enumerate(blocks):
                                last = nc.tensor.transpose(tp[n % 3][0:rows, j, :], src, ident[:, :])
                            last.then_inc(turned, 1)

                        pe.wait_ge(hT_in[b], 16 * i + 16)
                        from_h(lambda k: w_lora[:, k, :], 416)
                        from_h(lambda k: w_fox[:, k, 0:WIDTH], WIDTH)
                        from_h(lambda k: w_fox[:, k, WIDTH:2 * WIDTH], WIDTH)
                        pe.wait_ge(lora_ready, t + 1)
                        turn([lora_n[:, j * P:(j + 1) * P] for j in range(3)], P)
                        pe.wait_ge(turn_out, 9 * t + 4)
                        for lo, hi in ((0, CH), (CH, H * MQ)):
                            out = bank()
                            for k in range(2):
                                last = nc.tensor.matmul(out[:, 0:hi - lo], loraT[:, k, :], w_q_up[:, k, lo:hi],
                                                        start=(k == 0), stop=(k == 1))
                            last.then_inc(projected, 1)
                        for lo in (0, CH):
                            nc.tensor.matmul(bank()[:, :], loraT[:, 2, :], w_kv_up[:, lo:lo + CH],
                                             start=True, stop=True).then_inc(projected, 1)
                        from_h(lambda k: w_fox[:, k, 2 * WIDTH:3 * WIDTH], WIDTH)
                        out = bank()
                        for k in range(KD):
                            last = nc.tensor.matmul(out[:, :], hT[:, b, k * P:(k + 1) * P], w_u[:, k, :],
                                                    start=(k == 0), stop=(k == KD - 1))
                        last.then_inc(projected, 1)
                        pe.wait_ge(projected, 9 * t + 9)
                        pe.sem_inc(hT_used, 1)
                        for kind, (src, rows) in enumerate(((fqk, FQ), (mqk, MQ))):
                            pe.wait_ge(heads_ready, 2 * t + kind + 1)
                            for lo in range(0, 2 * H, 4):
                                turn([src[:, lo + j, :] for j in range(4)], rows)

            @block.scalar
            def _(act):
                act.wait_ge(tables, 3)
                nc.scalar.activation(sin_t[:, :, :].rearrange("p t f -> p (t f)"), angle[:, :], ACT.Sin).then_inc(tables, 1)
                nc.scalar.activation(cos_t[:, :, :].rearrange("p t f -> p (t f)"), angle[:, :], ACT.Sin,
                                     scale=0.5).then_inc(tables, 1)
                act.sem_inc(evacuated, 3)
                with act.Fori(0, NT // 2) as i:
                    for b in range(2):
                        t = 2 * i + b
                        use = [0]

                        def evacuate(dst, width, ready=None):
                            n = use[0]
                            use[0] += 1
                            act.wait_ge(projected, 9 * t + n + 1)
                            nc.scalar.activation(dst, pj[n % 3][:, 0:width], ACT.Copy).then_inc(evacuated, 1)

                        def root(st, n):
                            act.wait_ge(sums, 3 * t + n + 1)
                            nc.scalar.activation(st[1], st[0], ACT.Sqrt).then_inc(roots, 1)

                        act.wait_ge(raw_used, t + 1)
                        evacuate(lora[:, :], 416)
                        evacuate(fox[:, 0:WIDTH], WIDTH)
                        evacuate(fox[:, WIDTH:], WIDTH)
                        root((st_l[:, 2:4], st_l[:, 4:6]), 0)
                        evacuate(q_raw[:, 0:CH], CH)
                        evacuate(q_raw[:, CH:], H * MQ - CH)
                        evacuate(kv_raw[:, 0:CH], CH)
                        evacuate(kv_raw[:, CH:], CH)
                        root((st_f[:, 1, :], st_f[:, 2, :]), 1)
                        act.wait_ge(stored[b], 16 * OUTS * i + 1)
                        evacuate(fv_out[:, b, :], WIDTH)
                        evacuate(u_out[:, b, :], WIDTH)
                        root((st_m[:, 1, :], st_m[:, 2, :]), 2)

            @block.vector
            def _(dve):
                st = Steps(nc.vector, own)
                dve.wait_ge(small_in, 16 * 7)
                dve.wait_ge(tables, 2)
                st.do(nc.vector.tensor_scalar(gain_f[0:HD, 0:1], gain_f[0:HD, 0:1], HD ** -0.5, None, ALU.mult))
                st.do(nc.vector.tensor_scalar(gain_m[:, 0:1], gain_m[:, 0:1], MQ ** -0.5, None, ALU.mult))
                st.then(nc.vector.tensor_copy(pos[:, :], pos_i[:, :]))
                st.then(nc.vector.tensor_tensor(
                    angle[:, :].rearrange("p (t f) -> p t f", t=NT), pos[:, :].unsqueeze(2).to_broadcast([P, NT, ROPE // 2]),
                    inv[:, :].unsqueeze(1).to_broadcast([P, NT, ROPE // 2]), ALU.mult))
                reduce_angle(nc, st, angle[:, :], turns[:, :])
                dve.sem_inc(tables, 1)
                dve.wait_ge(tables, 5)
                cos_flat = cos_t[:, :, :].rearrange("p t f -> p (t f)")
                st.then(nc.vector.tensor_tensor(cos_flat, cos_flat, cos_flat, ALU.mult))
                st.then(nc.vector.tensor_scalar(cos_flat, cos_flat, -2.0, 1.0, ALU.mult, ALU.add))
                before = st.n
                per_tile = 32
                dve.sem_inc(raw_used, 1)
                dve.sem_inc(turn_out, 3)
                with dve.Fori(0, NT // 2) as i:
                    for b in range(2):
                        t = 2 * i + b
                        st = Steps(nc.vector, own, base=t * per_tile + before)
                        use = [0]

                        def arrived(n):
                            dve.wait_ge(evacuated, 9 * t + n + 1 + 3)

                        def turn_to(dst, gain, rows):
                            n = use[0]
                            use[0] += 1
                            dve.wait_ge(turned, 9 * t + n + 1)
                            nc.vector.tensor_scalar(dst, tp[n % 3][0:rows, :, :], gain, None, ALU.mult).then_inc(turn_out, 1)

                        def sum_squares(lo, hi, out):
                            st.do(nc.vector.tensor_tensor_reduce(out=junk[:, lo:hi], in0=lora[:, lo:hi], in1=lora[:, lo:hi],
                                                                 scale=1.0, scalar=0.0, op0=ALU.mult, op1=ALU.add,
                                                                 accum_out=out))

                        arrived(0)
                        sum_squares(0, Q_RANK, st_l[:, 0:1])
                        sum_squares(Q_RANK, 384, st_l[:, 1:2])
                        sum_squares(384, 416, st_l[:, 6:7])
                        st.join()
                        st.do(nc.vector.tensor_scalar(st_l[:, 2:3], st_l[:, 0:1], 1.0 / Q_RANK, EPS, ALU.mult, ALU.add))
                        nc.vector.tensor_scalar(st_l[:, 3:4], st_l[:, 1:2], 1.0 / KV_RANK, EPS,
                                                ALU.mult, ALU.add).then_inc(sums, 1)
                        dve.wait_ge(roots, 3 * t + 1)
                        st.then(nc.vector.reciprocal(st_l[:, 4:6], st_l[:, 4:6]))
                        st.do(nc.vector.tensor_scalar(lora_n[:, 0:Q_RANK], lora[:, 0:Q_RANK], st_l[:, 4:5], None, ALU.mult))
                        nc.vector.tensor_scalar(lora_n[:, Q_RANK:], lora[:, Q_RANK:384], st_l[:, 5:6], None,
                                                ALU.mult).then_inc(lora_ready, 1)
                        dve.wait_ge(turned, 9 * t + 1)
                        use[0] = 1
                        nc.vector.tensor_tensor(loraT[:, :, :], tp[0][:, 0:3, :],
                                                gain_lora[:, :].unsqueeze(2).to_broadcast([P, 3, P]),
                                                ALU.mult).then_inc(turn_out, 1)
                        cos1, sin1 = cos_t[:, t, :], sin_t[:, t, :]
                        half = ROPE // 2
                        x1, x2 = lora[:, 384:384 + half], lora[:, 384 + half:416]
                        for j, (x, w) in enumerate(((x1, cos1), (x2, sin1), (x1, sin1), (x2, cos1))):
                            st.do(nc.vector.tensor_tensor(rope[:, j, 0:half], x, w, ALU.mult))
                        st.join()
                        st.do(nc.vector.tensor_tensor(kpe[:, 0:half], rope[:, 0, 0:half], rope[:, 1, 0:half], ALU.subtract))
                        st.do(nc.vector.tensor_tensor(kpe[:, half:], rope[:, 2, 0:half], rope[:, 3, 0:half], ALU.add))
                        arrived(2)
                        st.then(nc.vector.tensor_tensor(junk[:, :], fox[:, :], fox[:, :], ALU.mult))
                        st.then(nc.vector.tensor_reduce(st_f[:, 0, :], junk[:, :].rearrange("p (h d) -> p h d", d=HD),
                                                        AX.X, ALU.add))
                        nc.vector.tensor_scalar(st_f[:, 1, :], st_f[:, 0, :], 1.0 / HD, EPS, ALU.mult, ALU.add).then_inc(sums, 1)
                        dve.wait_ge(roots, 3 * t + 2)
                        st.then(nc.vector.reciprocal(st_f[:, 2, :], st_f[:, 2, :]))
                        st.do(nc.vector.tensor_tensor(fqk[:, :, 0:HD], fox[:, :].rearrange("p (h d) -> p h d", d=HD),
                                                      st_f[:, 2, :].unsqueeze(2).to_broadcast([P, 2 * H, HD]), ALU.mult))
                        st.do(nc.vector.tensor_copy(fqk[:, 0:H, HD + 1], cum[:, t, :]))
                        nc.vector.tensor_scalar(fqk[:, H:2 * H, HD], cum[:, t, :], -1.0, None, ALU.mult).then_inc(heads_ready, 1)
                        dve.wait_ge(heads_ready, 2 * t + 1)
                        st.join()
                        arrived(6)
                        q3 = q_raw[:, :].rearrange("p (h d) -> p h d", d=MQ)
                        kv3 = kv_raw[:, :].rearrange("p (h d) -> p h d", d=P)
                        st.then(nc.vector.tensor_tensor(junk[:, 0:H * MQ], q_raw[:, :], q_raw[:, :], ALU.mult))
                        st.then(nc.vector.tensor_reduce(st_m[:, 0, 0:H], junk[:, 0:H * MQ].rearrange("p (h d) -> p h d", d=MQ),
                                                        AX.X, ALU.add))
                        jk = junk[:, 0:WIDTH].rearrange("p (h d) -> p h d", d=NOPE)
                        st.then(nc.vector.tensor_tensor(jk, kv3[:, :, 0:NOPE], kv3[:, :, 0:NOPE], ALU.mult))
                        st.then(nc.vector.tensor_reduce(st_m[:, 0, H:], jk, AX.X, ALU.add))
                        st.then(nc.vector.tensor_scalar(st_m[:, 0, H:], st_m[:, 0, H:], st_l[:, 6:7], None, ALU.add))
                        nc.vector.tensor_scalar(st_m[:, 1, :], st_m[:, 0, :], 1.0 / MQ, EPS, ALU.mult, ALU.add).then_inc(sums, 1)
                        cosb = cos1.unsqueeze(1).to_broadcast([P, H, half])
                        sinb = sin1.unsqueeze(1).to_broadcast([P, H, half])
                        r3 = [rope[:, j, :].rearrange("p (h d) -> p h d", d=half) for j in range(4)]
                        x1, x2 = q3[:, :, NOPE:NOPE + half], q3[:, :, NOPE + half:]
                        for j, (x, w) in enumerate(((x1, cosb), (x2, sinb), (x1, sinb), (x2, cosb))):
                            st.do(nc.vector.tensor_tensor(r3[j], x, w, ALU.mult))
                        st.join()
                        st.do(nc.vector.tensor_tensor(x1, r3[0], r3[1], ALU.subtract))
                        st.do(nc.vector.tensor_tensor(x2, r3[2], r3[3], ALU.add))
                        dve.wait_ge(roots, 3 * t + 3)
                        st.then(nc.vector.reciprocal(st_m[:, 2, :], st_m[:, 2, :]))
                        st.do(nc.vector.tensor_tensor(mqk[:, 0:H, :], q3,
                                                      st_m[:, 2, 0:H].unsqueeze(2).to_broadcast([P, H, MQ]), ALU.mult))
                        st.do(nc.vector.tensor_tensor(mqk[:, H:, 0:NOPE], kv3[:, :, 0:NOPE],
                                                      st_m[:, 2, H:].unsqueeze(2).to_broadcast([P, H, NOPE]), ALU.mult))
                        st.do(nc.vector.tensor_tensor(mqk[:, H:, NOPE:], kpe[:, :].unsqueeze(1).to_broadcast([P, H, ROPE]),
                                                      st_m[:, 2, H:].unsqueeze(2).to_broadcast([P, H, ROPE]), ALU.mult))
                        dve.wait_ge(stored[b], 16 * OUTS * i + 1)
                        nc.vector.tensor_copy(mv_out[:, b, :].rearrange("p (h d) -> p h d", d=HD),
                                              kv3[:, :, NOPE:]).then_inc(mv_ready, 1)
                        st.join()
                        dve.sem_inc(heads_ready, 1)
                        dve.wait_ge(mv_ready, t + 1)
                        dve.sem_inc(raw_used, 1)
                        for lo in range(0, 2 * H, 4):
                            turn_to(stage_f[:, b, lo:lo + 4, :], gain_f[:, lo // H:lo // H + 1], FQ)
                        for lo in range(0, 2 * H, 4):
                            turn_to(stage_m[:, b, lo:lo + 4, :], gain_m[:, lo // H:lo // H + 1], MQ)
                        assert st.n == per_tile, st.n



def attend(nc, a, keep):
    with ExitStack() as ctx:
        m = Mem(nc, ctx, "at")
        widths = (MQ, FQ)
        qT = [m.sb(f"qT{x}", [widths[x], S]) for x in range(2)]
        kT = [m.sb(f"kT{x}", [widths[x], S]) for x in range(2)]
        v = [m.sb(f"v{x}", [P, NT, HD]) for x in range(2)]
        y = [m.sb(f"y{x}", [P, NT, HD]) for x in range(2)]
        logits = m.sb("logits", [P, 2, S])
        probs = m.sb("probs", [P, 2, S])
        probsT = m.sb("probsT", [P, 4, 4, P])
        chunk_max = m.sb("chunk_max", [P, 2, 4])
        neg_max = m.sb("neg_max", [P, 2])
        row_sum = m.sb("row_sum", [P, 2])
        inv_sum = m.sb("inv_sum", [P, 2])
        ident = keep["ident"]
        ident_b = m.sb("ident_b", [P, P], BF16)
        mask = [m.sb(f"mask{x}", [P, P], BF16) for x in range(2)]
        s_ps = [m.ps(f"s{i}", [P, CH]) for i in range(4)]
        t_ps = [m.ps(f"t{i}", [P, 4, P]) for i in range(2)]
        o_ps = [m.ps(f"o{i}", [P, HD]) for i in range(2)]

        head_in = [m.sem(f"head_in{x}") for x in range(2)]
        head_used = [m.sem(f"head_used{x}") for x in range(2)]
        y_done = m.sem("y_done")
        y_stored = [m.sem(f"y_stored{x}") for x in range(2)]
        masks_set = m.sem("masks_set")
        scored = m.sem("scored")
        score_out = m.sem("score_out")
        max_ready = m.sem("max_ready")
        exped = m.sem("exped")
        turned = m.sem("turned")
        turn_out = m.sem("turn_out")
        weighted = m.sem("weighted")
        own = m.sem("own")
        tick = m.sem("tick")

        units = [(x, t, [(c, min(c + 4, t + 1)) for c in range(0, t + 1, 4)]) for x in range(2) for t in range(NT)]
        U = len(units)
        start = np.cumsum([0] + [len(u[2]) for u in units]).tolist()
        CHUNKS = start[-1]
        assert CHUNKS % 4 == 0
        EARLY = 8

        def turned_by(i, u):
            n = start[u + 1] if u >= 0 else start[u + 1 + U] - CHUNKS
            return i * CHUNKS + n + EARLY

        with nc.Block() as block:
            @block.sync
            def _(sp):
                for x in range(2):
                    sp.sem_inc(y_stored[x], 1)
                with sp.Fori(0, H) as i:
                    for x in range(2):
                        wait_alone(sp, y_done, U * i + NT * (x + 1) + 2, tick)
                        sp.dma_start(a["y"][:, :, bass.ds(i * HD + x * WIDTH, HD)].rearrange("t p d -> p t d"),
                                     y[x][:, :, :]).then_inc(y_stored[x], 16)
                for x in range(2):
                    sp.wait_ge(y_stored[x], 16 * H + 1)

            @block.gpsimd
            def _(pool):
                pool.memset(ident_b[:, :], 0.0).then_inc(masks_set, 1)
                for x in range(2):
                    pool.memset(mask[x][:, :], 0.0).then_inc(masks_set, 1)
                pool.wait_ge(masks_set, 3)
                pool.affine_select(out=ident_b[:, :], in_=ident_b[:, :], compare_op=ALU.not_equal, fill=1.0,
                                   base=0, pattern=[[-1, P]], channel_multiplier=1).then_inc(masks_set, 1)
                pool.memset(mask[0][0:P // 2, P // 2:P], MASKED).then_inc(masks_set, 1)
                pool.affine_select(out=mask[1][:, :], in_=mask[1][:, :], compare_op=ALU.is_ge, fill=MASKED,
                                   base=0, pattern=[[-1, P]], channel_multiplier=1).then_inc(masks_set, 1)
                with pool.Fori(0, H) as i:
                    for x, (qn, kn, vn) in enumerate((("mqT", "mkT", "mv"), ("fqT", "fkT", "fv"))):
                        wait_alone(pool, head_used[x], i + 1, tick)
                        pool.dma_start(qT[x][:, :], a[qn][i]).then_inc(head_in[x], 16)
                        pool.dma_start(kT[x][:, :], a[kn][i]).then_inc(head_in[x], 16)
                        pool.dma_start(v[x][:, :, :], a[vn][:, :, bass.ds(i * HD, HD)].rearrange("t p d -> p t d")).then_inc(head_in[x], 16)

            @block.tensor
            def _(pe):
                pe.sem_inc(turned, EARLY)
                pe.sem_inc(weighted, 4)
                for x in range(2):
                    pe.sem_inc(head_used[x], 1)
                pe.wait_ge(masks_set, 6)
                with pe.Fori(0, H) as i:
                    def score(u):
                        x, t, chunks = units[u]
                        if t == 0:
                            pe.wait_ge(head_in[x], 48 * i + 48)
                        for c, (lo, hi) in enumerate(chunks):
                            n = start[u] + c
                            out = s_ps[n % 4]
                            diagonal = hi == t + 1
                            pe.wait_ge(score_out, i * CHUNKS + n + 1)
                            last = nc.tensor.matmul(out[:, 0:(hi - lo) * P], qT[x][:, t * P:(t + 1) * P],
                                                    kT[x][:, lo * P:hi * P], start=True, stop=not diagonal)
                            if diagonal:
                                last = nc.tensor.matmul(out[:, (t - lo) * P:(hi - lo) * P], ident_b[:, :], mask[x][:, :],
                                                        start=False, stop=True)
                            last.then_inc(scored, 1)

                    def turn(u, c):
                        lo, hi = units[u][2][c]
                        n = start[u] + c
                        pe.wait_ge(turn_out, i * CHUNKS + n + 1)
                        for kt in range(lo, hi):
                            last = nc.tensor.transpose(t_ps[n % 2][:, kt - lo, :], probs[:, u % 2, kt * P:(kt + 1) * P],
                                                       ident[:, :])
                        last.then_inc(turned, 1)

                    def weigh(u, c):
                        x, t, chunks = units[u]
                        lo, hi = chunks[c]
                        n = start[u] + c
                        pe.wait_ge(turn_out, i * CHUNKS + n + 1 + 2)
                        if c == 0:
                            pe.wait_ge(y_done, U * i + u + 1)
                        for kt in range(lo, hi):
                            last = nc.tensor.matmul(o_ps[u % 2][:, :], probsT[:, n % 4, kt - lo, :], v[x][:, kt, :],
                                                    start=(kt == 0), stop=(kt == t))
                        last.then_inc(weighted, 1)

                    score(0)
                    for u in range(U):
                        x, t, chunks = units[u]
                        if u + 1 < U:
                            score(u + 1)
                        pe.wait_ge(exped, U * i + u + 1 + 2)
                        turn(u, 0)
                        for c in range(len(chunks)):
                            if c + 1 < len(chunks):
                                turn(u, c + 1)
                            weigh(u, c)
                        if t == NT - 1:
                            pe.wait_ge(weighted, i * CHUNKS + start[u + 1] + 4)
                            pe.sem_inc(head_used[x], 1)

            @block.scalar
            def _(act):
                act.sem_inc(exped, 2)
                act.sem_inc(turn_out, 2)
                with act.Fori(0, H) as i:
                    def exponentiate(u):
                        t = units[u][1]
                        act.wait_ge(max_ready, U * i + u + 1)
                        act.wait_ge(turned, turned_by(i, u - 2))
                        act.wait_ge(y_done, U * i + u + 1)
                        nc.scalar.activation(probs[:, u % 2, 0:(t + 1) * P], logits[:, u % 2, 0:(t + 1) * P], ACT.Exp,
                                             bias=neg_max[:, u % 2:u % 2 + 1],
                                             accum_out=row_sum[:, u % 2:u % 2 + 1]).then_inc(exped, 1)

                    exponentiate(0)
                    for u in range(U):
                        for c, (lo, hi) in enumerate(units[u][2]):
                            n = start[u] + c
                            act.wait_ge(turned, i * CHUNKS + n + 1 + EARLY)
                            act.wait_ge(weighted, i * CHUNKS + n + 1)
                            nc.scalar.activation(probsT[:, n % 4, 0:hi - lo, :], t_ps[n % 2][:, 0:hi - lo, :],
                                                 ACT.Copy).then_inc(turn_out, 1)
                        if u + 1 < U:
                            exponentiate(u + 1)

            @block.vector
            def _(dve):
                dve.sem_inc(score_out, 4)
                dve.sem_inc(y_done, 2)
                with dve.Fori(0, H) as i:
                    st = Steps(nc.vector, own, base=i * U)

                    def copy_scores(u):
                        x, t, chunks = units[u]
                        b = u % 2
                        dve.wait_ge(exped, U * i + u + 1)
                        for c, (lo, hi) in enumerate(chunks):
                            n = start[u] + c
                            dve.wait_ge(scored, i * CHUNKS + n + 1)
                            nc.vector.tensor_scalar(logits[:, b, lo * P:hi * P], s_ps[n % 4][:, 0:(hi - lo) * P], 1.0, None,
                                                    ALU.mult, ALU.max, accum_out=chunk_max[:, b, c:c + 1]).then_inc(score_out, 1)
                        dve.wait_ge(score_out, i * CHUNKS + start[u + 1] + 4)
                        nc.vector.tensor_reduce(neg_max[:, b:b + 1], chunk_max[:, b, 0:len(chunks)], AX.X, ALU.max,
                                                negate=True).then_inc(max_ready, 1)

                    def normalise(u):
                        x, t, chunks = units[u]
                        b = u % 2
                        dve.wait_ge(weighted, i * CHUNKS + start[u + 1] + 4)
                        if t == 0:
                            dve.wait_ge(y_stored[x], 16 * i + 1)
                        st.then(nc.vector.reciprocal(inv_sum[:, b:b + 1], row_sum[:, b:b + 1]))
                        nc.vector.tensor_scalar(y[x][:, t, :], o_ps[b][:, :], inv_sum[:, b:b + 1], None,
                                                ALU.mult).then_inc(y_done, 1)

                    copy_scores(0)
                    for u in range(U):
                        if u + 1 < U:
                            copy_scores(u + 1)
                        normalise(u)


def s5(nc, a, keep):
    TC = NC_ + 1
    with ExitStack() as ctx:
        m = Mem(nc, ctx, "s5")
        lr = m.sb("lr", [P, GROUPS])
        li = m.sb("li", [P, GROUPS])
        dt = m.sb("dt", [P, GROUPS])
        w = m.sb("w", [P, 12, GROUPS])
        pr = m.sb("pr", [P, GROUPS, STEP + 1])
        pi = m.sb("pi", [P, GROUPS, STEP + 1])
        back_r = m.sb("back_r", [P, GROUPS, STEP])
        back_i = m.sb("back_i", [P, GROUPS, STEP])
        mag8 = m.sb("mag8", [P, GROUPS])
        turn8 = m.sb("turn8", [P, GROUPS])
        b1 = m.sb("b1", [P, GROUPS, GC])
        b2 = m.sb("b2", [P, GROUPS, GC])
        c1 = m.sb("c1", [P, GROUPS, GC])
        c2 = m.sb("c2", [P, GROUPS, GC])
        bb1 = m.sb("bb1", [P, GROUPS, GC])
        bb2 = m.sb("bb2", [P, GROUPS, GC])
        skip = m.sb("skip", [GC, GROUPS, GC])
        step_i = m.sb("step_i", [P, TC], I32)
        step_no = m.sb("step_no", [P, TC])
        u_in = m.sb("u_in", [P, 2, STEP, P])
        u_grp = m.sb("u_grp", [P, 2, GB, P])
        uT = m.sb("uT", [P, GB, 2, P])
        tmp = m.sb("tmp", [P, GB, (STEP + 1) * GC])
        tmp2 = m.sb("tmp2", [P, GB, (STEP + 1) * GC])
        h_rows = m.sb("h_rows", [P, 2, GB, P])
        hT = m.sb("hT", [P, 2, GB, P])
        ca1 = m.sb("ca1", [P, GB, (STEP + 1) * GC])
        g2 = m.sb("g2", [P, GB, STEP * GC])
        k_out = m.sb("k_out", [GC, GB, P])
        toep = m.sb("toep", [P, GB, P])
        arg = m.sb("arg", [P, GB, TC])
        whole = m.sb("whole", [P, GB, TC])
        sin_t = m.sb("sin_t", [P, GB, TC])
        cos_t = m.sb("cos_t", [P, GB, TC])
        drive = m.sb("drive", [P, NC_])
        drive2 = m.sb("drive2", [P, NC_])
        z = m.sb("z", [P, NC_ + 1])
        xc = m.sb("xc", [P, 2, GB, NC_])
        y_tok = m.sb("y_tok", [P, 2, STEP, P])
        gel = m.sb("gel", [P, WIDTH // P, S])
        ident = keep["ident"]
        q = [m.ps(f"q{i}", [P, CH]) for i in range(8)]

        params_in = m.sem("params_in")
        consts = m.sem("consts")
        params_act = m.sem("params_act")
        params_ready = m.sem("params_ready")
        batch_done = m.sem("batch_done")
        u_loaded = m.sem("u_loaded")
        u_grouped = m.sem("u_grouped")
        u_turned = m.sem("u_turned")
        u_ready = m.sem("u_ready")
        rows_ready = m.sem("rows_ready")
        angles_ready = m.sem("angles_ready")
        waves_ready = m.sem("waves_ready")
        h_turned = m.sem("h_turned")
        h_ready = m.sem("h_ready")
        k_done = m.sem("k_done")
        k_copied = m.sem("k_copied")
        k_ready = m.sem("k_ready")
        shifted = m.sem("shifted")
        driven = m.sem("driven")
        drive_used = m.sem("drive_used")
        x_ready = m.sem("x_ready")
        y_done = m.sem("y_done")
        y_copied = m.sem("y_copied")
        y_turned = m.sem("y_turned")
        gelu_done = m.sem("gelu_done")
        own = m.sem("own")
        tick = m.sem("tick")

        with nc.Block() as block:
            @block.gpsimd
            def _(pool):
                pool.iota(step_i[:, :], pattern=[[1, TC]], base=-1, channel_multiplier=0).then_inc(consts, 1)
                pool.memset(toep[:, :, :], 0.0).then_inc(consts, 1)
                pool.memset(z[:, 0:1], 0.0).then_inc(consts, 1)
                for dst, name in ((lr[:, :], "s5_lr"), (li[:, :], "s5_li"), (dt[:, :], "s5_log_dt"),
                                  (b1[:, :, :], "s5_b_ri"), (b2[:, :, :], "s5_b_ir"),
                                  (c1[:, :, :], "s5_c_ri"), (c2[:, :, :], "s5_c_ir")):
                    pool.dma_start(dst, a[name]).then_inc(params_in, 16)
                pool.dma_start(skip[:, :, :].rearrange("c g o -> c (g o)"), a["s5_d"].partition_broadcast(GC)).then_inc(params_in, 16)
                pool.wait_ge(params_in, 16 * 8)
                pool.affine_select(out=skip[:, :, :], in_=skip[:, :, :], compare_op=ALU.is_equal, fill=0.0, base=0,
                                   pattern=[[0, GROUPS], [-1, GC]], channel_multiplier=1).then_inc(consts, 1)
                with pool.Fori(0, NB) as i:
                    wait_alone(pool, batch_done, i + 1, tick)
                    for half in range(2):
                        src = a["u"].rearrange("(h t) p n -> h (t p) n", h=2)[half].rearrange("(c s) n -> c s n", s=STEP)
                        pool.dma_start(u_in[:, half, :, :], src[:, :, bass.ds(i * P, P)]).then_inc(u_loaded, 16)
                    wait_alone(pool, u_loaded, 32 * i + 32, tick)
                    for half in range(2):
                        pool.tensor_copy(u_grp[:, half, :, :].rearrange("c g (s o) -> c g s o", o=GC),
                                         u_in[:, half, :, :].rearrange("c s (g o) -> c g s o", o=GC)).then_inc(u_grouped, 1)

            @block.sync
            def _(sp):
                sp.wait_ge(consts, 4)
                sp.sem_inc(shifted, 1)
                with sp.Fori(0, NB) as i:
                    wait_alone(sp, k_ready, i + 1, tick)
                    for s in range(STEP):
                        sp.dma_start(toep[s * GC:(s + 1) * GC, :, s * GC:P], k_out[:, :, 0:P - s * GC]).then_inc(shifted, 16)

            @block.scalar
            def _(act):
                act.sem_inc(batch_done, 1)
                act.wait_ge(params_in, 16 * 8)
                nc.scalar.activation(dt[:, :], dt[:, :], ACT.Exp).then_inc(params_act, 1)
                act.wait_ge(params_ready, 1)
                nc.scalar.activation(w[:, 0, :], w[:, 4, :], ACT.Exp).then_inc(params_act, 1)
                nc.scalar.activation(mag8[:, :], w[:, 4, :], ACT.Exp, scale=float(STEP)).then_inc(params_act, 1)
                nc.scalar.activation(w[:, 1, :], w[:, 5, :], ACT.Sin).then_inc(params_act, 1)
                nc.scalar.activation(w[:, 2, :], w[:, 5, :], ACT.Sin, scale=0.5).then_inc(params_act, 1)
                with act.Fori(0, NB) as i:
                    act.wait_ge(angles_ready, i + 1)
                    nc.scalar.activation(sin_t[:, :, :], arg[:, :, :], ACT.Sin, scale=6.283185).then_inc(waves_ready, 1)
                    nc.scalar.activation(cos_t[:, :, :], arg[:, :, :], ACT.Sin, scale=3.1415925).then_inc(waves_ready, 1)
                    for j in range(4):
                        act.wait_ge(h_turned, 4 * i + j + 1)
                        nc.scalar.activation(hT[:, j // 2, 4 * (j % 2):4 * (j % 2) + 4, :].rearrange("p g n -> p (g n)"),
                                             q[4 + j][:, :], ACT.Copy).then_inc(h_ready, 1)
                    act.wait_ge(k_done, i + 1)
                    for j in range(2):
                        nc.scalar.activation(k_out[:, 4 * j:4 * j + 4, :].rearrange("p g n -> p (g n)"), q[j][0:GC, :],
                                             ACT.Copy).then_inc(k_copied, 1)
                    for j in range(4):
                        half, g4 = divmod(j, 2)
                        act.wait_ge(y_done, 4 * i + j + 1)
                        nc.scalar.activation(
                            y_tok[:, half, :, 64 * g4:64 * g4 + 64].rearrange("p s (g o) -> p g s o", o=GC),
                            q[j][:, :].rearrange("p (g s o) -> p g s o", g=4, o=GC), ACT.Copy).then_inc(y_copied, 1)
                    gel_b = gel[:, i, :].rearrange("p (h c s) -> p h s c", h=2, s=STEP)
                    for j in range(4):
                        half, s4 = divmod(j, 2)
                        act.wait_ge(y_turned, 4 * i + j + 1)
                        nc.scalar.activation(gel_b[:, half, 4 * s4:4 * s4 + 4, :],
                                             q[4 + j][:, :].rearrange("p (s c) -> p s c", s=4),
                                             ACT.Gelu_apprx_tanh).then_inc(gelu_done, 1)
                    act.wait_ge(gelu_done, 4 * i + 4)
                    act.sem_inc(batch_done, 1)

            @block.tensor
            def _(pe):
                pe.sem_inc(drive_used, 4)
                with pe.Fori(0, NB) as i:
                    pe.wait_ge(batch_done, i + 1)
                    pe.wait_ge(u_grouped, 2 * i + 2)
                    for g in range(GB):
                        for half in range(2):
                            last = nc.tensor.transpose(q[g // 2][:, (g % 2) * 256 + half * P:(g % 2) * 256 + half * P + P],
                                                       u_grp[:, half, g, :], ident[:, :])
                        if g % 2:
                            last.then_inc(u_turned, 1)
                    pe.wait_ge(rows_ready, 2 * i + 1)
                    for j in range(4):
                        for g in range(4):
                            last = nc.tensor.transpose(q[4 + j][:, g * P:(g + 1) * P], h_rows[:, j // 2, 4 * (j % 2) + g, :],
                                                       ident[:, :])
                        last.then_inc(h_turned, 1)
                    pe.wait_ge(rows_ready, 2 * i + 2)
                    pe.wait_ge(u_ready, 4 * i + 4)
                    for g in range(GB):
                        last = nc.tensor.matmul(q[g // 4][0:GC, (g % 4) * P:(g % 4 + 1) * P], h_rows[:, 0, g, P - GC:P],
                                                ca1[:, g, 0:P], start=True, stop=True)
                    last.then_inc(k_done, 1)
                    pe.wait_ge(h_ready, 4 * i + 4)
                    for g in range(GB):
                        pe.wait_ge(drive_used, GB * i + g + 1)
                        for j in range(2):
                            last = nc.tensor.matmul(q[4 + g % 4][:, j * NC_:(j + 1) * NC_], hT[:, j, g, :],
                                                    uT[:, g, :, :].rearrange("p h c -> p (h c)"), start=True, stop=True)
                        last.then_inc(driven, 1)
                    pe.wait_ge(shifted, 16 * STEP * i + 16 * STEP + 1)
                    pe.wait_ge(x_ready, 2 * GB * i + 2 * GB)
                    for half in range(2):
                        cs = slice(half * P, half * P + P)
                        for g in range(GB):
                            out = q[2 * half + g // 4][:, (g % 4) * P:(g % 4 + 1) * P]
                            nc.tensor.matmul(out, uT[:, g, half, :], toep[:, g, :], start=True, stop=False)
                            nc.tensor.matmul(out, xc[:, 0, g, cs], ca1[:, g, GC:P + GC], start=False, stop=False)
                            last = nc.tensor.matmul(out, xc[:, 1, g, cs], g2[:, g, :], start=False, stop=True)
                            if g % 4 == 3:
                                last.then_inc(y_done, 1)
                    pe.wait_ge(y_copied, 4 * i + 4)
                    for j in range(4):
                        half, s4 = divmod(j, 2)
                        for s in range(4):
                            last = nc.tensor.transpose(q[4 + j][:, s * P:(s + 1) * P], y_tok[:, half, 4 * s4 + s, :], ident[:, :])
                        last.then_inc(y_turned, 1)

            @block.vector
            def _(dve):
                st = Steps(nc.vector, own)
                v, tt, ts = nc.vector, nc.vector.tensor_tensor, nc.vector.tensor_scalar
                W = lambda n: w[:, n, :]
                dve.wait_ge(consts, 4)
                dve.wait_ge(params_in, 16 * 8)
                dve.wait_ge(params_act, 1)
                st.do(ts(b2[0:NS, :, :], b2[0:NS, :, :], -1.0, None, ALU.mult))
                st.do(ts(c1[NS:P, :, :], c1[NS:P, :, :], -1.0, None, ALU.mult))
                st.do(ts(c2[:, :, :], c2[:, :, :], -1.0, None, ALU.mult))
                st.do(v.tensor_copy(step_no[:, :], step_i[:, :]))
                st.do(tt(W(4), lr[:, :], dt[:, :], ALU.mult))
                st.then(tt(W(5), li[:, :], dt[:, :], ALU.mult))
                reduce_angle(nc, st, W(5), W(6))
                dve.sem_inc(params_ready, 1)
                st.then(ts(turn8[:, :], W(5), STEP / TWO_PI, None, ALU.mult))
                st.then(ts(W(6), turn8[:, :], MAGIC, None, ALU.add))
                st.then(ts(W(6), W(6), MAGIC, None, ALU.subtract))
                st.do(tt(turn8[:, :], turn8[:, :], W(6), ALU.subtract))
                st.do(tt(W(7), lr[:, :], lr[:, :], ALU.mult))
                st.then(tt(W(8), li[:, :], li[:, :], ALU.mult))
                st.then(tt(W(7), W(7), W(8), ALU.add))
                st.do(v.reciprocal(W(7), W(7)))
                dve.wait_ge(params_act, 5)
                st.then(tt(W(2), W(2), W(2), ALU.mult))
                st.then(ts(W(2), W(2), -2.0, 1.0, ALU.mult, ALU.add))
                a_re, a_im = pr[:, :, 1], pi[:, :, 1]
                st.do(tt(a_re, W(0), W(2), ALU.mult))
                st.do(tt(a_im, W(0), W(1), ALU.mult))
                st.do(v.memset(pr[:, :, 0], 1.0))
                st.then(v.memset(pi[:, :, 0], 0.0))
                st.then(ts(W(3), a_re, 1.0, None, ALU.subtract))
                for n, (x, y) in enumerate(((W(3), lr), (a_im, li), (a_im, lr), (W(3), li))):
                    st.do(tt(W(8 + n), x, y[:, :], ALU.mult))
                st.join()
                st.do(tt(W(8), W(8), W(9), ALU.add))
                st.then(tt(W(10), W(10), W(11), ALU.subtract))
                st.do(tt(W(8), W(8), W(7), ALU.mult))
                st.then(tt(W(10), W(10), W(7), ALU.mult))
                for d in range(2, STEP + 1):
                    for n, (x, y) in enumerate(((pr, a_re), (pi, a_im), (pr, a_im), (pi, a_re))):
                        st.do(tt(W((0, 1, 2, 4)[n]), x[:, :, d - 1], y, ALU.mult))
                    st.join()
                    st.do(tt(pr[:, :, d], W(0), W(1), ALU.subtract))
                    st.then(tt(pi[:, :, d], W(2), W(4), ALU.add))
                for d in range(STEP):
                    st.do(v.tensor_copy(back_r[:, :, STEP - 1 - d], pr[:, :, d]))
                    st.do(v.tensor_copy(back_i[:, :, STEP - 1 - d], pi[:, :, d]))
                wide = lambda x: x.unsqueeze(2).to_broadcast([P, GROUPS, GC])
                flat = lambda x: x[:, :, :].rearrange("p g c -> p (g c)")
                ta = tmp[:, 0:4, :].rearrange("p g c -> p (g c)")[:, 0:GROUPS * GC].rearrange("p (g c) -> p g c", c=GC)
                tb = tmp2[:, 0:4, :].rearrange("p g c -> p (g c)")[:, 0:GROUPS * GC].rearrange("p (g c) -> p g c", c=GC)
                for out, x, y, op in ((bb1, b1, b2, ALU.add), (bb2, b2, b1, ALU.subtract)):
                    st.do(tt(ta, x[:, :, :], wide(W(8)), ALU.mult))
                    st.then(tt(tb, y[:, :, :], wide(W(10)), ALU.mult))
                    st.then(tt(out[:, :, :], ta, tb, op))
                before = st.n
                per_batch = 39
                with dve.Fori(0, NB) as i:
                    st = Steps(nc.vector, own, base=i * per_batch + before)
                    gs = bass.ds(i * GB, GB)
                    dve.wait_ge(batch_done, i + 1)
                    full = [P, GB, TC]
                    st.then(tt(arg[:, :, :], turn8[:, gs].unsqueeze(2).to_broadcast(full),
                               step_no[:, :].unsqueeze(1).to_broadcast(full), ALU.mult))
                    st.then(ts(whole[:, :, :], arg[:, :, :], MAGIC, None, ALU.add))
                    st.then(ts(whole[:, :, :], whole[:, :, :], MAGIC, None, ALU.subtract))
                    tt(arg[:, :, :], arg[:, :, :], whole[:, :, :], ALU.subtract).then_inc(angles_ready, 1)
                    for j in range(4):
                        dve.wait_ge(u_turned, 4 * i + j + 1)
                        v.tensor_copy(uT[:, 2 * j:2 * j + 2, :, :].rearrange("p g h c -> p (g h c)"), q[j][:, :]).then_inc(u_ready, 1)

                    def rows(out, powers_r, powers_i, n, x, y, op, done=None):
                        shape = [P, GB, n, GC]
                        sr, si = (s[:, :, :].unsqueeze(3).to_broadcast(shape) for s in (powers_r, powers_i))
                        bx, by = (s[:, gs, :].unsqueeze(2).to_broadcast(shape) for s in (x, y))
                        t1, t2 = (s[:, :, 0:n * GC].rearrange("p g (s c) -> p g s c", c=GC) for s in (tmp, tmp2))
                        st.do(tt(t1, sr, bx, ALU.mult))
                        st.then(tt(t2, si, by, ALU.mult))
                        ins = tt(out.rearrange("p g (s c) -> p g s c", c=GC), t1, t2, op)
                        if done is None:
                            st.then(ins)
                        else:
                            ins.then_inc(done, 1)

                    br, bi = back_r[:, gs, :], back_i[:, gs, :]
                    rows(h_rows[:, 0, :, :], br, bi, STEP, bb1, bb2, ALU.add)
                    rows(h_rows[:, 1, :, :], bi, br, STEP, bb1, bb2, ALU.subtract, rows_ready)
                    dve.wait_ge(rows_ready, 2 * i + 1)
                    rows(g2[:, :, :], pr[:, gs, 1:], pi[:, gs, 1:], STEP, c2, c1, ALU.subtract)
                    rows(ca1[:, :, :], pr[:, gs, :], pi[:, gs, :], STEP + 1, c1, c2, ALU.add, rows_ready)
                    dve.wait_ge(waves_ready, 2 * i + 2)
                    st.then(tt(cos_t[:, :, :], cos_t[:, :, :], cos_t[:, :, :], ALU.mult))
                    st.then(ts(cos_t[:, :, :], cos_t[:, :, :], -2.0, 1.0, ALU.mult, ALU.add))
                    dve.wait_ge(k_copied, 2 * i + 2)
                    tt(k_out[:, :, 0:GC], k_out[:, :, 0:GC], skip[:, gs, :], ALU.add).then_inc(k_ready, 1)
                    for g in range(GB):
                        dve.wait_ge(driven, GB * i + g + 1)
                        st.do(tt(drive[:, :], q[4 + g % 4][:, 0:NC_], cos_t[:, g, 1:TC], ALU.mult))
                        tt(drive2[:, :], q[4 + g % 4][:, NC_:], sin_t[:, g, 1:TC], ALU.mult).then_inc(drive_used, 1)
                        dve.wait_ge(drive_used, GB * i + g + 1 + 4)
                        st.join()
                        st.then(tt(drive[:, :], drive[:, :], drive2[:, :], ALU.add))
                        st.then(v.tensor_tensor_scan(z[:, 1:NC_ + 1], mag8[:, bass.ds(i * GB + g, 1)].to_broadcast([P, NC_]),
                                                     drive[:, :], 0.0, ALU.mult, ALU.add))
                        tt(xc[:, 0, g, :], z[:, 0:NC_], cos_t[:, g, 0:NC_], ALU.mult).then_inc(x_ready, 1)
                        tt(xc[:, 1, g, :], z[:, 0:NC_], sin_t[:, g, 0:NC_], ALU.mult).then_inc(x_ready, 1)
                    assert st.n == per_batch, st.n

        with ExitStack() as glu_ctx:
            m = Mem(nc, glu_ctx, "gl")
            w_glu = m.sb("w_glu", [P, WIDTH // P, WIDTH])
            b_glu = m.sb("b_glu", [P, WIDTH // P])
            gate = m.sb("gate", [P, 2, CH])
            out = m.sb("out", [P, 4, CH])
            loaded, mixed, gated, multiplied = m.sem("loaded"), m.sem("mixed"), m.sem("gated"), m.sem("multiplied")
            z_stored = [m.sem(f"z_stored{i}") for i in range(4)]
            NJ = WIDTH // P
            with nc.Block() as block:
                @block.sync
                def _(sp):
                    sp.dma_start(w_glu[:, :, :], a["s5_w_glu"]).then_inc(loaded, 16)
                    sp.dma_start(b_glu[:, :], a["s5_b_glu"]).then_inc(loaded, 16)
                    for n in range(4 * NJ):
                        j, c = divmod(n, 4)
                        sp.wait_ge(multiplied, n + 1)
                        sp.dma_start(a["zT"][j, :, c * CH:(c + 1) * CH], out[:, n % 4, :]).then_inc(z_stored[n % 4], 16)
                    for i in range(4):
                        sp.wait_ge(z_stored[i], 16 * NJ)

                @block.tensor
                def _(pe):
                    pe.wait_ge(loaded, 32)
                    for n in range(4 * NJ):
                        j, c = divmod(n, 4)
                        if n >= 4:
                            pe.wait_ge(gated, n - 3)
                        for k in range(NJ):
                            last = nc.tensor.matmul(q[n % 4][:, :], w_glu[:, k, j * P:(j + 1) * P],
                                                    gel[:, k, c * CH:(c + 1) * CH], start=(k == 0), stop=(k == NJ - 1))
                        last.then_inc(mixed, 1)

                @block.scalar
                def _(act):
                    act.wait_ge(loaded, 32)
                    for n in range(4 * NJ):
                        j, c = divmod(n, 4)
                        act.wait_ge(mixed, n + 1)
                        if n >= 2:
                            act.wait_ge(multiplied, n - 1)
                        nc.scalar.activation(gate[:, n % 2, :], q[n % 4][:, :], ACT.Sigmoid,
                                             bias=b_glu[:, j:j + 1]).then_inc(gated, 1)

                @block.vector
                def _(dve):
                    for n in range(4 * NJ):
                        j, c = divmod(n, 4)
                        dve.wait_ge(gated, n + 1)
                        if n >= 4:
                            dve.wait_ge(z_stored[n % 4], 16 * (n // 4))
                        nc.vector.tensor_tensor(out[:, n % 4, :], gel[:, j, c * CH:(c + 1) * CH], gate[:, n % 2, :],
                                                ALU.mult).then_inc(multiplied, 1)


def merge(nc, a, keep):
    HT = NT // 2
    HS = S // 2
    NY = 3 * WIDTH // P
    BR = 3
    SLOTS = 6
    with ExitStack() as ctx:
        m = Mem(nc, ctx, "me")
        hT = m.sb("hT", [P, KD, HS])
        yg = m.sb("yg", [P, NY, HS])
        both = m.sb("both", [P, KD, HS])
        w_out = m.sb("w_out", [P, KD, D])
        ring = m.sb("ring", [P, SLOTS, KD, P])
        gate = m.sb("gate", [P, 2, CH])
        part = m.sb("part", [P, CH])
        x_in = m.sb("x_in", [P, D])
        out = m.sb("out", [P, D])
        ident = keep["ident"]
        y_tok = both[:, :, :]
        a_ps = [m.ps(f"a{i}", [P, CH]) for i in range(4)]
        m_ps = [m.ps(f"m{i}", [P, CH]) for i in range(2)]
        o_ps = [m.ps(f"o{i}", [P, CH]) for i in range(2)]

        w_out_in = m.sem("w_out_in")
        half_in = m.sem("half_in")
        z_in = m.sem("z_in")
        half_done = m.sem("half_done")
        w_in = [m.sem(f"w_in{i}") for i in range(SLOTS)]
        w_used = m.sem("w_used")
        a_full = m.sem("a_full")
        a_free = m.sem("a_free")
        g_sig = m.sem("g_sig")
        gate_used = m.sem("gate_used")
        m_full = m.sem("m_full")
        m_free = m.sem("m_free")
        o_full = m.sem("o_full")
        o_free = m.sem("o_free")
        x_loaded = m.sem("x_loaded")
        x_free = m.sem("x_free")
        stored = m.sem("stored")
        own = m.sem("own")
        tick = m.sem("tick")
        NA = 16 + 2 * NY + 2 * HT
        NW = NY + 2 * BR * KD
        NM = 2 * BR * KD
        assert NA % 4 == 0 and NW % SLOTS == 0 and NM % 2 == 0
        PER_SLOT = NW // SLOTS

        with nc.Block() as block:
            @block.sync
            def _(sp):
                sp.sem_inc(w_used, SLOTS)
                for k in range(0, KD, 2):
                    sp.dma_start(w_out[:, k:k + 2, :], a["w_out"][:, k:k + 2, :]).then_inc(w_out_in, 16)
                with sp.Fori(0, 2) as i:
                    tile = 0

                    def weight(src, width):
                        n = tile
                        wait_alone(sp, w_used, NW * i + n + 1, tick)
                        sp.dma_start(ring[:, n % SLOTS, 0:width, :], src).then_inc(w_in[n % SLOTS], 16)

                    for j in range(NY):
                        weight(a["w_gate"][j], KD)
                        tile += 1
                    for j in range(KD):
                        for br in range(BR):
                            weight(a["w_merge"][j, br], KD)
                            tile += 1
                            weight(a["w_branch"][j, br], 4)
                            tile += 1

            @block.gpsimd
            def _(pool):
                with pool.Fori(0, 2) as i:
                    wait_alone(pool, half_done, i + 1, tick)
                    for t in range(HT):
                        pool.dma_start(y_tok[:, t, :], a["y"][i * HT + t]).then_inc(half_in, 16)
                        pool.dma_start(hT[:, :, t * P:(t + 1) * P], a["hT"][i * HT + t].rearrange("p (k t) -> p k t", t=P)).then_inc(half_in, 16)
                    for j in range(4):
                        pool.dma_start(yg[:, 8 + j, :], a["zT"][j][:, bass.ds(i * HS, HS)]).then_inc(z_in, 16)
                    for t in range(HT):
                        wait_alone(pool, x_free, i * HT + t + 1, tick)
                        pool.dma_start(x_in[:, :], a["x"][i * HT + t]).then_inc(x_loaded, 16)

            @block.tensor
            def _(pe):
                with pe.Fori(0, 2) as i:
                    n_a = n_m = n_w = 0

                    def fill_a():
                        pe.wait_ge(a_free, NA * i + n_a + 1)
                        return a_ps[n_a % 4]

                    def weights_of(n):
                        pe.wait_ge(w_in[n % SLOTS], 16 * PER_SLOT * i + 16 * (n // SLOTS) + 16)
                        return ring[:, n % SLOTS, :, :]

                    pe.wait_ge(half_in, 16 * 2 * HT * i + 16 * 2 * HT)
                    for j in range(8):
                        for c in range(2):
                            bank = fill_a()
                            for t in range(4):
                                last = nc.tensor.transpose(bank[:, t * P:(t + 1) * P], y_tok[:, 4 * c + t, j * P:(j + 1) * P],
                                                           ident[:, :])
                            last.then_inc(a_full, 1)
                            n_a += 1
                    for j in range(NY):
                        w = weights_of(n_w)
                        for c in range(2):
                            bank = fill_a()
                            for k in range(KD):
                                last = nc.tensor.matmul(bank[:, :], w[:, k, :], hT[:, k, c * CH:(c + 1) * CH],
                                                        start=(k == 0), stop=(k == KD - 1))
                            last.then_inc(a_full, 1)
                            n_a += 1
                        pe.wait_ge(a_full, NA * i + n_a)
                        pe.sem_inc(w_used, 1)
                        n_w += 1
                    pe.wait_ge(a_free, NA * i + n_a + 4)
                    for j in range(KD):
                        for br in range(BR):
                            wm, wb = weights_of(n_w), weights_of(n_w + 1)
                            for c in range(2):
                                cs = slice(c * CH, (c + 1) * CH)
                                pe.wait_ge(m_free, NM * i + n_m + 1)
                                for k in range(KD):
                                    last = nc.tensor.matmul(m_ps[n_m % 2][:, :], wm[:, k, :], hT[:, k, cs],
                                                            start=(k == 0), stop=(k == KD - 1))
                                last.then_inc(m_full, 1)
                                pe.wait_ge(o_free, NM * i + n_m + 1)
                                for k in range(4):
                                    last = nc.tensor.matmul(o_ps[n_m % 2][:, :], wb[:, k, :], yg[:, 4 * br + k, cs],
                                                            start=(k == 0), stop=(k == 3))
                                last.then_inc(o_full, 1)
                                n_m += 1
                            pe.wait_ge(o_full, NM * i + n_m)
                            pe.sem_inc(w_used, 2)
                            n_w += 2
                    pe.wait_ge(o_free, NM * i + n_m + 2)
                    pe.wait_ge(w_out_in, 64)
                    for t in range(HT):
                        for c in range(2):
                            bank = fill_a()
                            for k in range(KD):
                                last = nc.tensor.matmul(bank[:, :], both[:, k, t * P:(t + 1) * P], w_out[:, k, c * CH:(c + 1) * CH],
                                                        start=(k == 0), stop=(k == KD - 1))
                            last.then_inc(a_full, 1)
                            n_a += 1

            @block.scalar
            def _(act):
                act.sem_inc(m_free, 2)
                act.sem_inc(stored, 1)
                with act.Fori(0, 2) as i:
                    n_g = 0
                    NG = 2 * NY + NM

                    def sigmoid(src, done):
                        act.wait_ge(gate_used, NG * i + n_g + 1)
                        nc.scalar.activation(gate[:, n_g % 2, :], src, ACT.Sigmoid).then_inc(done, 1)

                    for n in range(2 * NY):
                        act.wait_ge(a_full, NA * i + 16 + n + 1)
                        sigmoid(a_ps[n % 4][:, :], g_sig)
                        n_g += 1
                    for n in range(NM):
                        act.wait_ge(m_full, NM * i + n + 1)
                        sigmoid(m_ps[n % 2][:, :], m_free)
                        n_g += 1
                    for t in range(HT):
                        act.wait_ge(a_free, NA * i + 16 + 2 * NY + 2 * t + 2 + 4)
                        act.dma_start(a["out"][i * HT + t], out[:, :]).then_inc(stored, 16)
                act.wait_ge(stored, 16 * NT + 1)

            @block.vector
            def _(dve):
                dve.sem_inc(a_free, 4)
                dve.sem_inc(o_free, 2)
                dve.sem_inc(gate_used, 2)
                dve.sem_inc(half_done, 1)
                dve.sem_inc(x_free, 1)
                tt = nc.vector.tensor_tensor
                PER_TURN = 2 * NY
                with dve.Fori(0, 2) as i:
                    st = Steps(nc.vector, own, base=i * PER_TURN)
                    n_a = 0
                    for j in range(8):
                        for c in range(2):
                            dve.wait_ge(a_full, NA * i + n_a + 1)
                            nc.vector.tensor_copy(yg[:, j, c * CH:(c + 1) * CH], a_ps[n_a % 4][:, :]).then_inc(a_free, 1)
                            n_a += 1
                    dve.wait_ge(a_free, NA * i + 16 + 4)
                    dve.wait_ge(z_in, 64 * i + 64)
                    for n in range(2 * NY):
                        j, c = divmod(n, 2)
                        dve.wait_ge(g_sig, 2 * NY * i + n + 1)
                        g, ys = gate[:, n % 2, :], yg[:, j, c * CH:(c + 1) * CH]
                        st.then(tt(g, a_ps[n % 4][:, :], g, ALU.mult))
                        tt(ys, ys, g, ALU.mult).then_inc(a_free, 1)
                        dve.wait_ge(a_free, NA * i + n_a + 1 + 4)
                        dve.sem_inc(gate_used, 1)
                        n_a += 1
                    n_m = 0
                    for j in range(KD):
                        for br in range(BR):
                            for c in range(2):
                                dve.wait_ge(m_free, NM * i + n_m + 1 + 2)
                                dve.wait_ge(o_full, NM * i + n_m + 1)
                                dst = both[:, j, c * CH:(c + 1) * CH]
                                g, o = gate[:, n_m % 2, :], o_ps[n_m % 2][:, :]
                                if br == 0:
                                    tt(dst, o, g, ALU.mult).then_inc(o_free, 1)
                                    dve.wait_ge(o_free, NM * i + n_m + 1 + 2)
                                    dve.sem_inc(gate_used, 1)
                                else:
                                    dve.wait_ge(o_free, NM * i + n_m + 2)
                                    tt(part[:, :], o, g, ALU.mult).then_inc(gate_used, 1)
                                    dve.wait_ge(gate_used, (2 * NY + NM) * i + 2 * NY + n_m + 1 + 2)
                                    tt(dst, dst, part[:, :], ALU.add).then_inc(o_free, 1)
                                n_m += 1
                    for t in range(HT):
                        dve.wait_ge(x_loaded, 16 * (i * HT) + 16 * t + 16)
                        dve.wait_ge(stored, 16 * (i * HT) + 16 * t + 1)
                        for c in range(2):
                            dve.wait_ge(a_full, NA * i + n_a + 1)
                            tt(out[:, c * CH:(c + 1) * CH], a_ps[n_a % 4][:, :], x_in[:, c * CH:(c + 1) * CH],
                               ALU.add).then_inc(a_free, 1)
                            n_a += 1
                        dve.wait_ge(a_free, NA * i + n_a + 4)
                        dve.sem_inc(x_free, 1)
                    dve.sem_inc(half_done, 1)
                    assert st.n == PER_TURN, st.n


def build(nc, a):
    scratch = {"hT": (NT, P, D), "mqT": (H, MQ, S), "mkT": (H, MQ, S), "fqT": (H, FQ, S), "fkT": (H, FQ, S),
               "mv": (NT, P, WIDTH), "fv": (NT, P, WIDTH), "u": (NT, P, WIDTH), "y": (NT, P, 2 * WIDTH),
               "zT": (WIDTH // P, P, S)}
    a = dict(a)
    for name, shape in scratch.items():
        a[name] = nc.dram_tensor(f"scratch_{name}", shape, F32).ap()
    with ExitStack() as ctx:
        keep = {"ident": ctx.enter_context(nc.sbuf_tensor("ident", [P, P], F32)),
                "cum": ctx.enter_context(nc.sbuf_tensor("cum", [P, NT, H], F32))}
        norm_x(nc, a, keep)
        project(nc, a, keep)
        s5(nc, a, keep)
        attend(nc, a, keep)
        merge(nc, a, keep)


def layout(inputs):
    f = {k: np.asarray(v) for k, v in inputs.items()}
    one = {k: v[0] for k, v in f.items() if k not in ("positions",)}
    rows = lambda w: w.reshape(-1, P, w.shape[-1]).transpose(1, 0, 2)
    w = one["w_in"]
    cut = np.cumsum([0, Q_RANK, KV_RANK, ROPE, WIDTH, WIDTH, WIDTH, H, WIDTH, WIDTH, WIDTH, WIDTH, D, D, D])
    cols = lambda i, j: w[:, cut[i]:cut[j]]

    def tiles(w):
        k, j = w.shape[0] // P, w.shape[1] // P
        return w.reshape(k, P, j, P).transpose(2, 1, 0, 3)

    stack = lambda x, y: np.concatenate([x, y], axis=0)
    state = lambda x: x.transpose(1, 0)
    br, bi = (one[k].transpose(1, 0, 2) for k in ("s5_b_re", "s5_b_im"))
    cr, ci = (one[k].transpose(2, 0, 1) for k in ("s5_c_re", "s5_c_im"))
    merge_w = tiles(cols(11, 14)).reshape(3, KD, P, KD, P).transpose(1, 0, 2, 3, 4)
    branch_w = np.stack([tiles(one["w_branch_out"][b * WIDTH:(b + 1) * WIDTH]) for b in range(3)], axis=1)
    col = lambda v: v.reshape(-1, 1)
    out = {
        "x": one["x"].reshape(NT, P, D),
        "positions": f["positions"].reshape(NT, P).transpose(1, 0),
        "inv_freq": np.broadcast_to((1.0 / (np.float32(10000.0) ** (np.arange(0, ROPE, 2, dtype=np.float32) / np.float32(ROPE)))).astype(np.float32), (P, ROPE // 2)),
        "norm_g": one["norm_g"].reshape(KD, P).transpose(1, 0),
        "w_ff": rows(cols(6, 7)), "fox_b_f": one["fox_b_f"],
        "w_lora": rows(cols(0, 3)), "w_fox": rows(cols(3, 6)), "w_u": rows(cols(7, 8)),
        "w_q_up": rows(one["mla_w_q_up"]), "w_kv_up": one["mla_w_kv_up"],
        "gain_lora": np.concatenate([one["mla_q_a_norm"], one["mla_kv_a_norm"]]).reshape(3, P).transpose(1, 0),
        "fox_q_norm": col(one["fox_q_norm"]), "fox_k_norm": col(one["fox_k_norm"]),
        "mla_q_norm": col(one["mla_q_norm"]), "mla_k_norm": col(one["mla_k_norm"]),
        "s5_lr": stack(state(one["s5_lambda_re"]), state(one["s5_lambda_re"])),
        "s5_li": stack(state(one["s5_lambda_im"]), state(one["s5_lambda_im"])),
        "s5_log_dt": np.broadcast_to(one["s5_log_dt"], (P, GROUPS)),
        "s5_b_ri": stack(br, bi), "s5_b_ir": stack(bi, br), "s5_c_ri": stack(cr, ci), "s5_c_ir": stack(ci, cr),
        "s5_d": one["s5_d"], "s5_w_glu": rows(one["s5_w_glu"]), "s5_b_glu": one["s5_b_glu"].reshape(-1, P).transpose(1, 0),
        "w_gate": tiles(cols(8, 11)), "w_merge": merge_w, "w_branch": branch_w, "w_out": rows(one["w_out"]),
    }
    return {k: np.ascontiguousarray(v) for k, v in out.items()}


def kernel(**inputs):
    import concourse.bacc as bacc
    from concourse.bass_utils import run_bass_kernel_spmd

    nc = bacc.Bacc("TRN2", target_bir_lowering=False, num_devices=1)
    arrays = {f"in_{k}": v for k, v in layout(inputs).items()}
    a = {k[3:]: nc.dram_tensor(k, v.shape, mybir.dt.from_np(v.dtype), kind="ExternalInput").ap() for k, v in arrays.items()}
    a["out"] = nc.dram_tensor("out", (NT, P, D), F32, kind="ExternalOutput").ap()
    build(nc, a)
    result = run_bass_kernel_spmd(nc, [arrays], core_ids=[0])
    return result.results[0]["out"].reshape(1, S, D)
```

```python
import math
from contextlib import ExitStack

import numpy as np

import concourse.bass as bass
from concourse import mybir

P = 128
F32 = mybir.dt.float32
F32R = mybir.dt.float32r
BF16 = mybir.dt.bfloat16
I32 = mybir.dt.int32
ALU = mybir.AluOpType
ACT = mybir.ActivationFunctionType
AX = mybir.AxisListType

D = 1024
S = 2048
KD = D // P
NT = S // P
H = 8
Q_RANK, KV_RANK, ROPE, NOPE, HD = 256, 128, 32, 64, 64
MQ = NOPE + ROPE
FQ = HD + 5
WIDTH = H * HD
GROUPS, GC, NS = 32, 16, 64
EPS = 1e-6
CH = 512
STEP = 8
NC_ = S // STEP
GB = 8
NB = GROUPS // GB
MAGIC = 1.5 * 2.0 ** 23
TWO_PI = 2.0 * math.pi
C1 = 6.28125
C2 = float(np.float32(math.floor((TWO_PI - C1) * 2 ** 20) / 2 ** 20))
C3 = TWO_PI - C1 - C2
PI_F32 = 3.1415925
MASKED = -1.0e30


class Steps:

    def __init__(self, eng, sem, base=0):
        self.eng, self.sem, self.base, self.n = eng, sem, base, 0

    def do(self, ins):
        ins.then_inc(self.sem, 1)
        self.n += 1

    def join(self):
        self.eng.wait_ge(self.sem, self.base + self.n)

    def then(self, ins):
        self.do(ins)
        self.join()


def wait_alone(eng, sem, value, tick):
    eng.wait_ge(sem, value)
    eng.sem_inc(tick, 1)


class Mem:

    def __init__(self, nc, ctx, tag):
        self.nc, self.ctx, self.tag = nc, ctx, tag

    def sb(self, name, shape, dt=F32):
        return self.ctx.enter_context(self.nc.sbuf_tensor(f"{self.tag}_{name}", shape, dt))

    def ps(self, name, shape, dt=F32):
        return self.ctx.enter_context(self.nc.psum_tensor(f"{self.tag}_{name}", shape, dt))

    def sem(self, name):
        return self.ctx.enter_context(self.nc.semaphore(f"{self.tag}_{name}"))


def norm_x(nc, a, keep):
    with ExitStack() as ctx:
        m = Mem(nc, ctx, "nx")
        x_in = m.sb("x_in", [P, 2, D])
        square = m.sb("square", [P, D])
        h = m.sb("h", [P, 2, D])
        hT = m.sb("hT", [P, 2, KD, P])
        gain = m.sb("gain", [P, KD])
        w_ff = m.sb("w_ff", [P, KD, H])
        ff = m.sb("ff", [P, NT, H])
        b_f = m.sb("b_f", [P, H])
        stat = m.sb("stat", [P, 2, 3])
        lf = m.sb("lf", [P, 4, NT * H])
        tri = m.sb("tri", [P, P])
        ones = m.sb("ones", [P, P])
        total = m.sb("total", [P, NT, H])
        cum_lead = m.sb("cum_lead", [P, NT * H], F32R)
        ident = keep["ident"]
        t_ps = [m.ps(f"t{i}", [P, 4, P]) for i in range(4)]
        ff_ps = [m.ps(f"ff{i}", [P, CH]) for i in range(2)]
        cum_ps = m.ps("cum_ps", [P, NT * H])
        tot_ps = m.ps("tot_ps", [P, NT * H])

        params_in = m.sem("params_in")
        x_loaded = [m.sem(f"x_loaded{b}") for b in range(2)]
        consts_set = m.sem("consts_set")
        h_done = m.sem("h_done")
        squared = m.sem("squared")
        mean_ready = m.sem("mean_ready")
        root_ready = m.sem("root_ready")
        transposed = m.sem("transposed")
        hT_copied = m.sem("hT_copied")
        hT_stored = [m.sem(f"hT_stored{b}") for b in range(2)]
        ff_done = m.sem("ff_done")
        ff_copied = m.sem("ff_copied")
        logs = m.sem("logs")
        summed = m.sem("summed")
        own = m.sem("own")
        tick = m.sem("tick")

        with nc.Block() as block:
            @block.sync
            def _(sp):
                sp.dma_start(gain[:, :], a["norm_g"]).then_inc(params_in, 16)
                sp.dma_start(w_ff[:, :, :], a["w_ff"]).then_inc(params_in, 16)
                sp.dma_start(b_f[:, :], a["fox_b_f"].partition_broadcast(P)).then_inc(params_in, 16)
                for b in range(2):
                    sp.sem_inc(hT_stored[b], 1)
                with sp.Fori(0, NT // 2) as i:
                    for b in range(2):
                        wait_alone(sp, hT_copied, 4 * i + 2 * b + 3, tick)
                        sp.dma_start(a["hT"][2 * i + b], hT[:, b, :, :].rearrange("p k t -> p (k t)")).then_inc(hT_stored[b], 16)
                for b in range(2):
                    sp.wait_ge(hT_stored[b], 16 * (NT // 2) + 1)

            @block.gpsimd
            def _(pool):
                pool.memset(ones[:, :], 1.0).then_inc(consts_set, 1)
                pool.memset(ident[:, :], 0.0).then_inc(consts_set, 1)
                pool.wait_ge(consts_set, 2)
                pool.affine_select(out=ident[:, :], in_=ident[:, :], compare_op=ALU.not_equal, fill=1.0,
                                   base=0, pattern=[[-1, P]], channel_multiplier=1).then_inc(consts_set, 1)
                pool.affine_select(out=tri[:, :], in_=ones[:, :], compare_op=ALU.is_ge, fill=0.0,
                                   base=0, pattern=[[1, P]], channel_multiplier=-1).then_inc(consts_set, 1)
                with pool.Fori(0, NT // 2) as i:
                    for b in range(2):
                        wait_alone(pool, h_done, 2 * i + b + 1, tick)
                        pool.dma_start(x_in[:, b, :], a["x"][2 * i + b]).then_inc(x_loaded[b], 16)

            @block.scalar
            def _(act):
                with act.Fori(0, NT // 2) as i:
                    for b in range(2):
                        act.wait_ge(x_loaded[b], 16 * i + 16)
                        act.wait_ge(mean_ready, 2 * i + b + 1)
                        nc.scalar.activation(square[:, :], x_in[:, b, :], ACT.Square,
                                             accum_out=stat[:, b, 0:1]).then_inc(squared, 1)
                        act.wait_ge(mean_ready, 2 * i + b + 2)
                        nc.scalar.activation(stat[:, b, 2:3], stat[:, b, 1:2], ACT.Sqrt).then_inc(root_ready, 1)
                act.wait_ge(logs, 1)
                nc.scalar.activation(lf[:, 2, :], lf[:, 1, :], ACT.Exp, scale=-1.0).then_inc(logs, 1)
                act.wait_ge(logs, 3)
                nc.scalar.activation(lf[:, 3, :], lf[:, 2, :], ACT.Ln).then_inc(logs, 1)

            @block.vector
            def _(dve):
                dve.sem_inc(h_done, 2)
                dve.sem_inc(mean_ready, 1)
                dve.sem_inc(hT_copied, 1)
                dve.sem_inc(ff_copied, 2)
                dve.wait_ge(params_in, 48)
                with dve.Fori(0, NT // 2) as i:
                    st = Steps(nc.vector, own, base=i * 2)
                    for b in range(2):
                        t = 2 * i + b
                        dve.wait_ge(squared, t + 1)
                        nc.vector.tensor_scalar(stat[:, b, 1:2], stat[:, b, 0:1], 1.0 / D, EPS,
                                                ALU.mult, ALU.add).then_inc(mean_ready, 1)
                        dve.wait_ge(root_ready, t + 1)
                        st.then(nc.vector.reciprocal(stat[:, b, 1:2], stat[:, b, 2:3]))
                        dve.wait_ge(transposed, 2 * t + 2)
                        nc.vector.tensor_scalar(h[:, b, :], x_in[:, b, :], stat[:, b, 1:2], None,
                                                ALU.mult).then_inc(h_done, 1)
                        dve.wait_ge(hT_stored[b], 16 * i + 1)
                        dve.wait_ge(ff_done, t + 1)
                        for half in range(2):
                            dve.wait_ge(transposed, 2 * t + half + 5)
                            ks = slice(4 * half, 4 * half + 4)
                            nc.vector.tensor_tensor(hT[:, b, ks, :], t_ps[2 * b + half][:, :, :],
                                                    gain[:, ks].unsqueeze(2).to_broadcast([P, 4, P]),
                                                    ALU.mult).then_inc(hT_copied, 1)
                        dve.wait_ge(ff_done, t + 3)
                        nc.vector.tensor_tensor(ff[:, t, :], ff_ps[b][:, 0:H], b_f[:, :], ALU.add).then_inc(ff_copied, 1)
                dve.wait_ge(ff_copied, NT + 2)
                ff_all = ff[:, :, :].rearrange("p t h -> p (t h)")
                own2 = Steps(nc.vector, own, base=NT)
                own2.then(nc.vector.tensor_scalar(lf[:, 0, :], ff_all, -1.0, None, ALU.mult))
                nc.vector.tensor_tensor(lf[:, 1, :], lf[:, 0, :], ff_all, ALU.max).then_inc(logs, 1)
                dve.wait_ge(logs, 2)
                own2.do(nc.vector.tensor_scalar(lf[:, 0, :], ff_all, 0.0, None, ALU.min))
                nc.vector.tensor_scalar(lf[:, 2, :], lf[:, 2, :], 1.0, None, ALU.add).then_inc(logs, 1)
                dve.wait_ge(logs, 4)
                own2.join()
                nc.vector.tensor_tensor(lf[:, 0, :], lf[:, 0, :], lf[:, 3, :], ALU.subtract).then_inc(logs, 1)
                dve.wait_ge(summed, 1)
                own2.then(nc.vector.memset(total[:, 0, :], 0.0))
                for t in range(1, NT):
                    own2.then(nc.vector.tensor_tensor(total[:, t, :], total[:, t - 1, :],
                                                      tot_ps[:, (t - 1) * H:t * H], ALU.add))
                flat = total[:, :, :].rearrange("p t h -> p (t h)")
                lead, rest = (keep["cum"][:, :, :, n].rearrange("p t h -> p (t h)") for n in range(2))
                own2.then(nc.vector.tensor_tensor(flat, cum_ps[:, :], flat, ALU.add))
                own2.then(nc.vector.tensor_copy(cum_lead[:, :], flat))
                own2.do(nc.vector.tensor_copy(lead, cum_lead[:, :].bitcast(F32)))
                own2.then(nc.vector.tensor_tensor(rest, flat, cum_lead[:, :].bitcast(F32), ALU.subtract))

            @block.tensor
            def _(pe):
                pe.sem_inc(transposed, 4)
                pe.sem_inc(ff_done, 2)
                pe.wait_ge(consts_set, 4)
                pe.wait_ge(params_in, 48)
                with pe.Fori(0, NT // 2) as i:
                    for b in range(2):
                        t = 2 * i + b
                        pe.wait_ge(h_done, t + 3)
                        for half in range(2):
                            for k in range(4 * half, 4 * half + 4):
                                last = nc.tensor.transpose(t_ps[2 * b + half][:, k % 4, :],
                                                           h[:, b, k * P:(k + 1) * P], ident[:, :])
                            last.then_inc(transposed, 1)
                        pe.wait_ge(hT_copied, 2 * t + 3)
                        pe.wait_ge(ff_copied, t + 1)
                        for k in range(KD):
                            last = nc.tensor.matmul(ff_ps[b][:, 0:H], hT[:, b, k, :], w_ff[:, k, :],
                                                    start=(k == 0), stop=(k == KD - 1))
                        last.then_inc(ff_done, 1)
                pe.wait_ge(logs, 5)
                nc.tensor.matmul(cum_ps[:, :], tri[:, :], lf[:, 0, :], start=True, stop=True)
                nc.tensor.matmul(tot_ps[:, :], ones[:, :], lf[:, 0, :], start=True, stop=True).then_inc(summed, 1)


def reduce_angle(nc, st, angle, k):
    st.then(nc.vector.tensor_scalar(k, angle, 1.0 / TWO_PI, MAGIC, ALU.mult, ALU.add))
    st.then(nc.vector.tensor_scalar(k, k, MAGIC, None, ALU.subtract))
    for part in (C1, C2, C3):
        st.then(nc.vector.scalar_tensor_tensor(out=angle, in0=k, scalar=-part, in1=angle,
                                               op0=ALU.mult, op1=ALU.add))
    st.then(nc.vector.tensor_scalar(angle, angle, PI_F32, -PI_F32, ALU.min, ALU.max))


def project(nc, a, keep):
    with ExitStack() as ctx:
        m = Mem(nc, ctx, "pr")
        w_lora = m.sb("w_lora", [P, KD, 416])
        w_fox = m.sb("w_fox", [P, KD, 3 * WIDTH])
        w_u = m.sb("w_u", [P, KD, WIDTH])
        w_q_up = m.sb("w_q_up", [P, 2, H * MQ])
        w_kv_up = m.sb("w_kv_up", [P, H * P])
        hT = m.sb("hT", [P, 2, KD * P])
        lora = m.sb("lora", [P, 416])
        lora_n = m.sb("lora_n", [P, 384])
        loraT = m.sb("loraT", [P, 3, P])
        gain_lora = m.sb("gain_lora", [P, 3])
        fox = m.sb("fox", [P, 2 * WIDTH])
        q_raw = m.sb("q_raw", [P, H * MQ])
        kv_raw = m.sb("kv_raw", [P, H * P])
        fv_out = m.sb("fv_out", [P, 2, WIDTH])
        mv_out = m.sb("mv_out", [P, 2, WIDTH])
        u_out = m.sb("u_out", [P, 2, WIDTH])
        junk = m.sb("junk", [P, 2 * WIDTH])
        rope = m.sb("rope", [P, 4, H * ROPE // 2])
        kpe = m.sb("kpe", [P, ROPE])
        fqk = m.sb("fqk", [P, 2 * H, FQ])
        mqk = m.sb("mqk", [P, 2 * H, MQ])
        gain_f = m.sb("gain_f", [FQ, 2])
        gain_m = m.sb("gain_m", [MQ, 2])
        st_l = m.sb("st_l", [P, 7])
        st_f = m.sb("st_f", [P, 3, 2 * H])
        st_m = m.sb("st_m", [P, 3, 2 * H])
        stage_f = m.sb("stage_f", [FQ, 2, 2 * H, P])
        stage_m = m.sb("stage_m", [MQ, 2, 2 * H, P])
        pos_i = m.sb("pos_i", [P, NT], I32)
        pos = m.sb("pos", [P, NT])
        inv = m.sb("inv", [P, ROPE // 2])
        sin_t = m.sb("sin_t", [P, NT, ROPE // 2])
        cos_t = m.sb("cos_t", [P, NT, ROPE // 2])
        angle = m.sb("angle", [P, NT * ROPE // 2])
        turns = m.sb("turns", [P, NT * ROPE // 2])
        ident, cum = keep["ident"], keep["cum"]
        pj = [m.ps(f"pj{i}", [P, CH]) for i in range(3)]
        tp = [m.ps(f"tp{i}", [P, 4, P]) for i in range(3)]

        weights_in = m.sem("weights_in")
        small_in = m.sem("small_in")
        hT_in = [m.sem(f"hT_in{b}") for b in range(2)]
        hT_used = m.sem("hT_used")
        projected = m.sem("projected")
        evacuated = m.sem("evacuated")
        turned = m.sem("turned")
        turn_out = m.sem("turn_out")
        sums = m.sem("sums")
        roots = m.sem("roots")
        lora_ready = m.sem("lora_ready")
        heads_ready = m.sem("heads_ready")
        raw_used = m.sem("raw_used")
        mv_ready = m.sem("mv_ready")
        stored = [m.sem(f"stored{b}") for b in range(2)]
        tables = m.sem("tables")
        own = m.sem("own")
        tick = m.sem("tick")
        OUTS = 7

        with nc.Block() as block:
            @block.sync
            def _(sp):
                sp.dma_start(w_lora[:, :, :], a["w_lora"]).then_inc(weights_in, 16)
                for k in range(0, KD, 2):
                    sp.dma_start(w_fox[:, k:k + 2, :], a["w_fox"][:, k:k + 2, :]).then_inc(weights_in, 16)
                sp.dma_start(w_u[:, :, :], a["w_u"]).then_inc(weights_in, 16)
                sp.dma_start(w_q_up[:, :, :], a["w_q_up"]).then_inc(weights_in, 16)
                sp.dma_start(w_kv_up[:, :], a["w_kv_up"]).then_inc(weights_in, 16)
                for b in range(2):
                    sp.sem_inc(stored[b], 1)
                with sp.Fori(0, NT // 2) as i:
                    for b in range(2):
                        t = 2 * i + b
                        tok = bass.ds(t * P, P)
                        wait_alone(sp, evacuated, 9 * t + 9 + 3, tick)
                        wait_alone(sp, mv_ready, t + 1, tick)
                        sp.dma_start(a["u"][t], u_out[:, b, :]).then_inc(stored[b], 16)
                        sp.dma_start(a["fv"][t], fv_out[:, b, :]).then_inc(stored[b], 16)
                        sp.dma_start(a["mv"][t], mv_out[:, b, :]).then_inc(stored[b], 16)
                        wait_alone(sp, turn_out, 9 * t + 5 + 3, tick)
                        for j, name in enumerate(("fqT", "fkT")):
                            sp.dma_start(a[name][:, :, tok].rearrange("h d t -> d h t"),
                                         stage_f[:, b, j * H:(j + 1) * H, :]).then_inc(stored[b], 16)
                        wait_alone(sp, turn_out, 9 * t + 9 + 3, tick)
                        for j, name in enumerate(("mqT", "mkT")):
                            sp.dma_start(a[name][:, :, tok].rearrange("h d t -> d h t"),
                                         stage_m[:, b, j * H:(j + 1) * H, :]).then_inc(stored[b], 16)
                for b in range(2):
                    sp.wait_ge(stored[b], 16 * OUTS * (NT // 2) + 1)

            @block.gpsimd
            def _(pool):
                pool.memset(gain_f[:, :], 1.0).then_inc(tables, 1)
                pool.memset(fqk[:, :, HD:FQ], 1.0).then_inc(tables, 1)
                pool.wait_ge(tables, 1)
                for dst, name in ((pos_i[:, :], "positions"), (inv[:, :], "inv_freq"), (gain_lora[:, :], "gain_lora"),
                                  (gain_f[0:HD, 0:1], "fox_q_norm"), (gain_f[0:HD, 1:2], "fox_k_norm"),
                                  (gain_m[:, 0:1], "mla_q_norm"), (gain_m[:, 1:2], "mla_k_norm")):
                    pool.dma_start(dst, a[name]).then_inc(small_in, 16)
                with pool.Fori(0, NT // 2) as i:
                    for b in range(2):
                        wait_alone(pool, hT_used, 2 * i + b + 1, tick)
                        pool.dma_start(hT[:, b, :], a["hT"][2 * i + b]).then_inc(hT_in[b], 16)

            @block.tensor
            def _(pe):
                pe.sem_inc(hT_used, 2)
                pe.wait_ge(weights_in, 16 * 8)
                with pe.Fori(0, NT // 2) as i:
                    for b in range(2):
                        t = 2 * i + b
                        use = {"pj": 0, "tp": 0}

                        def bank():
                            n = use["pj"]
                            use["pj"] += 1
                            pe.wait_ge(evacuated, 9 * t + n + 1)
                            return pj[n % 3]

                        def from_h(w, width):
                            out = bank()
                            for k in range(KD):
                                last = nc.tensor.matmul(out[:, 0:width], hT[:, b, k * P:(k + 1) * P], w(k),
                                                        start=(k == 0), stop=(k == KD - 1))
                            return last.then_inc(projected, 1)

                        def turn(blocks, rows):
                            n = use["tp"]
                            use["tp"] += 1
                            pe.wait_ge(turn_out, 9 * t + n + 1)
                            for j, src in enumerate(blocks):
                                last = nc.tensor.transpose(tp[n % 3][0:rows, j, :], src, ident[:, :])
                            last.then_inc(turned, 1)

                        pe.wait_ge(hT_in[b], 16 * i + 16)
                        from_h(lambda k: w_lora[:, k, :], 416)
                        from_h(lambda k: w_fox[:, k, 0:WIDTH], WIDTH)
                        from_h(lambda k: w_fox[:, k, WIDTH:2 * WIDTH], WIDTH)
                        pe.wait_ge(lora_ready, t + 1)
                        turn([lora_n[:, j * P:(j + 1) * P] for j in range(3)], P)
                        pe.wait_ge(turn_out, 9 * t + 4)
                        for lo, hi in ((0, CH), (CH, H * MQ)):
                            out = bank()
                            for k in range(2):
                                last = nc.tensor.matmul(out[:, 0:hi - lo], loraT[:, k, :], w_q_up[:, k, lo:hi],
                                                        start=(k == 0), stop=(k == 1))
                            last.then_inc(projected, 1)
                        for lo in (0, CH):
                            nc.tensor.matmul(bank()[:, :], loraT[:, 2, :], w_kv_up[:, lo:lo + CH],
                                             start=True, stop=True).then_inc(projected, 1)
                        from_h(lambda k: w_fox[:, k, 2 * WIDTH:3 * WIDTH], WIDTH)
                        out = bank()
                        for k in range(KD):
                            last = nc.tensor.matmul(out[:, :], hT[:, b, k * P:(k + 1) * P], w_u[:, k, :],
                                                    start=(k == 0), stop=(k == KD - 1))
                        last.then_inc(projected, 1)
                        pe.wait_ge(projected, 9 * t + 9)
                        pe.sem_inc(hT_used, 1)
                        for kind, (src, rows) in enumerate(((fqk, FQ), (mqk, MQ))):
                            pe.wait_ge(heads_ready, 2 * t + kind + 1)
                            for lo in range(0, 2 * H, 4):
                                turn([src[:, lo + j, :] for j in range(4)], rows)

            @block.scalar
            def _(act):
                act.wait_ge(tables, 3)
                nc.scalar.activation(sin_t[:, :, :].rearrange("p t f -> p (t f)"), angle[:, :], ACT.Sin).then_inc(tables, 1)
                nc.scalar.activation(cos_t[:, :, :].rearrange("p t f -> p (t f)"), angle[:, :], ACT.Sin,
                                     scale=0.5).then_inc(tables, 1)
                act.sem_inc(evacuated, 3)
                with act.Fori(0, NT // 2) as i:
                    for b in range(2):
                        t = 2 * i + b
                        use = [0]

                        def evacuate(dst, width, ready=None):
                            n = use[0]
                            use[0] += 1
                            act.wait_ge(projected, 9 * t + n + 1)
                            nc.scalar.activation(dst, pj[n % 3][:, 0:width], ACT.Copy).then_inc(evacuated, 1)

                        def root(st, n):
                            act.wait_ge(sums, 3 * t + n + 1)
                            nc.scalar.activation(st[1], st[0], ACT.Sqrt).then_inc(roots, 1)

                        act.wait_ge(raw_used, t + 1)
                        evacuate(lora[:, :], 416)
                        evacuate(fox[:, 0:WIDTH], WIDTH)
                        evacuate(fox[:, WIDTH:], WIDTH)
                        root((st_l[:, 2:4], st_l[:, 4:6]), 0)
                        evacuate(q_raw[:, 0:CH], CH)
                        evacuate(q_raw[:, CH:], H * MQ - CH)
                        evacuate(kv_raw[:, 0:CH], CH)
                        evacuate(kv_raw[:, CH:], CH)
                        root((st_f[:, 1, :], st_f[:, 2, :]), 1)
                        act.wait_ge(stored[b], 16 * OUTS * i + 1)
                        evacuate(fv_out[:, b, :], WIDTH)
                        evacuate(u_out[:, b, :], WIDTH)
                        root((st_m[:, 1, :], st_m[:, 2, :]), 2)

            @block.vector
            def _(dve):
                st = Steps(nc.vector, own)
                dve.wait_ge(small_in, 16 * 7)
                dve.wait_ge(tables, 2)
                st.do(nc.vector.memset(fqk[:, 0:H, HD:HD + 1], 0.0))
                st.do(nc.vector.tensor_scalar(gain_f[0:HD, 0:1], gain_f[0:HD, 0:1], HD ** -0.5, None, ALU.mult))
                st.do(nc.vector.tensor_scalar(gain_m[:, 0:1], gain_m[:, 0:1], MQ ** -0.5, None, ALU.mult))
                st.then(nc.vector.tensor_copy(pos[:, :], pos_i[:, :]))
                st.then(nc.vector.tensor_tensor(
                    angle[:, :].rearrange("p (t f) -> p t f", t=NT), pos[:, :].unsqueeze(2).to_broadcast([P, NT, ROPE // 2]),
                    inv[:, :].unsqueeze(1).to_broadcast([P, NT, ROPE // 2]), ALU.mult))
                reduce_angle(nc, st, angle[:, :], turns[:, :])
                dve.sem_inc(tables, 1)
                dve.wait_ge(tables, 5)
                cos_flat = cos_t[:, :, :].rearrange("p t f -> p (t f)")
                st.then(nc.vector.tensor_tensor(cos_flat, cos_flat, cos_flat, ALU.mult))
                st.then(nc.vector.tensor_scalar(cos_flat, cos_flat, -2.0, 1.0, ALU.mult, ALU.add))
                before = st.n
                per_tile = 32
                dve.sem_inc(raw_used, 1)
                dve.sem_inc(turn_out, 3)
                with dve.Fori(0, NT // 2) as i:
                    for b in range(2):
                        t = 2 * i + b
                        st = Steps(nc.vector, own, base=t * per_tile + before)
                        use = [0]

                        def arrived(n):
                            dve.wait_ge(evacuated, 9 * t + n + 1 + 3)

                        def turn_to(dst, gain, rows):
                            n = use[0]
                            use[0] += 1
                            dve.wait_ge(turned, 9 * t + n + 1)
                            nc.vector.tensor_scalar(dst, tp[n % 3][0:rows, :, :], gain, None, ALU.mult).then_inc(turn_out, 1)

                        def sum_squares(lo, hi, out):
                            st.do(nc.vector.tensor_tensor_reduce(out=junk[:, lo:hi], in0=lora[:, lo:hi], in1=lora[:, lo:hi],
                                                                 scale=1.0, scalar=0.0, op0=ALU.mult, op1=ALU.add,
                                                                 accum_out=out))

                        arrived(0)
                        sum_squares(0, Q_RANK, st_l[:, 0:1])
                        sum_squares(Q_RANK, 384, st_l[:, 1:2])
                        sum_squares(384, 416, st_l[:, 6:7])
                        st.join()
                        st.do(nc.vector.tensor_scalar(st_l[:, 2:3], st_l[:, 0:1], 1.0 / Q_RANK, EPS, ALU.mult, ALU.add))
                        nc.vector.tensor_scalar(st_l[:, 3:4], st_l[:, 1:2], 1.0 / KV_RANK, EPS,
                                                ALU.mult, ALU.add).then_inc(sums, 1)
                        dve.wait_ge(roots, 3 * t + 1)
                        st.then(nc.vector.reciprocal(st_l[:, 4:6], st_l[:, 4:6]))
                        st.do(nc.vector.tensor_scalar(lora_n[:, 0:Q_RANK], lora[:, 0:Q_RANK], st_l[:, 4:5], None, ALU.mult))
                        nc.vector.tensor_scalar(lora_n[:, Q_RANK:], lora[:, Q_RANK:384], st_l[:, 5:6], None,
                                                ALU.mult).then_inc(lora_ready, 1)
                        dve.wait_ge(turned, 9 * t + 1)
                        use[0] = 1
                        nc.vector.tensor_tensor(loraT[:, :, :], tp[0][:, 0:3, :],
                                                gain_lora[:, :].unsqueeze(2).to_broadcast([P, 3, P]),
                                                ALU.mult).then_inc(turn_out, 1)
                        cos1, sin1 = cos_t[:, t, :], sin_t[:, t, :]
                        half = ROPE // 2
                        x1, x2 = lora[:, 384:384 + half], lora[:, 384 + half:416]
                        for j, (x, w) in enumerate(((x1, cos1), (x2, sin1), (x1, sin1), (x2, cos1))):
                            st.do(nc.vector.tensor_tensor(rope[:, j, 0:half], x, w, ALU.mult))
                        st.join()
                        st.do(nc.vector.tensor_tensor(kpe[:, 0:half], rope[:, 0, 0:half], rope[:, 1, 0:half], ALU.subtract))
                        st.do(nc.vector.tensor_tensor(kpe[:, half:], rope[:, 2, 0:half], rope[:, 3, 0:half], ALU.add))
                        arrived(2)
                        st.then(nc.vector.tensor_tensor(junk[:, :], fox[:, :], fox[:, :], ALU.mult))
                        st.then(nc.vector.tensor_reduce(st_f[:, 0, :], junk[:, :].rearrange("p (h d) -> p h d", d=HD),
                                                        AX.X, ALU.add))
                        nc.vector.tensor_scalar(st_f[:, 1, :], st_f[:, 0, :], 1.0 / HD, EPS, ALU.mult, ALU.add).then_inc(sums, 1)
                        dve.wait_ge(roots, 3 * t + 2)
                        st.then(nc.vector.reciprocal(st_f[:, 2, :], st_f[:, 2, :]))
                        st.do(nc.vector.tensor_tensor(fqk[:, :, 0:HD], fox[:, :].rearrange("p (h d) -> p h d", d=HD),
                                                      st_f[:, 2, :].unsqueeze(2).to_broadcast([P, 2 * H, HD]), ALU.mult))
                        st.do(nc.vector.tensor_copy(fqk[:, 0:H, HD + 3:FQ], cum[:, t, :, :]))
                        nc.vector.tensor_scalar(fqk[:, H:2 * H, HD + 1:HD + 3], cum[:, t, :, :], -1.0, None,
                                                ALU.mult).then_inc(heads_ready, 1)
                        dve.wait_ge(heads_ready, 2 * t + 1)
                        st.join()
                        arrived(6)
                        q3 = q_raw[:, :].rearrange("p (h d) -> p h d", d=MQ)
                        kv3 = kv_raw[:, :].rearrange("p (h d) -> p h d", d=P)
                        st.then(nc.vector.tensor_tensor(junk[:, 0:H * MQ], q_raw[:, :], q_raw[:, :], ALU.mult))
                        st.then(nc.vector.tensor_reduce(st_m[:, 0, 0:H], junk[:, 0:H * MQ].rearrange("p (h d) -> p h d", d=MQ),
                                                        AX.X, ALU.add))
                        jk = junk[:, 0:WIDTH].rearrange("p (h d) -> p h d", d=NOPE)
                        st.then(nc.vector.tensor_tensor(jk, kv3[:, :, 0:NOPE], kv3[:, :, 0:NOPE], ALU.mult))
                        st.then(nc.vector.tensor_reduce(st_m[:, 0, H:], jk, AX.X, ALU.add))
                        st.then(nc.vector.tensor_scalar(st_m[:, 0, H:], st_m[:, 0, H:], st_l[:, 6:7], None, ALU.add))
                        nc.vector.tensor_scalar(st_m[:, 1, :], st_m[:, 0, :], 1.0 / MQ, EPS, ALU.mult, ALU.add).then_inc(sums, 1)
                        cosb = cos1.unsqueeze(1).to_broadcast([P, H, half])
                        sinb = sin1.unsqueeze(1).to_broadcast([P, H, half])
                        r3 = [rope[:, j, :].rearrange("p (h d) -> p h d", d=half) for j in range(4)]
                        x1, x2 = q3[:, :, NOPE:NOPE + half], q3[:, :, NOPE + half:]
                        for j, (x, w) in enumerate(((x1, cosb), (x2, sinb), (x1, sinb), (x2, cosb))):
                            st.do(nc.vector.tensor_tensor(r3[j], x, w, ALU.mult))
                        st.join()
                        st.do(nc.vector.tensor_tensor(x1, r3[0], r3[1], ALU.subtract))
                        st.do(nc.vector.tensor_tensor(x2, r3[2], r3[3], ALU.add))
                        dve.wait_ge(roots, 3 * t + 3)
                        st.then(nc.vector.reciprocal(st_m[:, 2, :], st_m[:, 2, :]))
                        st.do(nc.vector.tensor_tensor(mqk[:, 0:H, :], q3,
                                                      st_m[:, 2, 0:H].unsqueeze(2).to_broadcast([P, H, MQ]), ALU.mult))
                        st.do(nc.vector.tensor_tensor(mqk[:, H:, 0:NOPE], kv3[:, :, 0:NOPE],
                                                      st_m[:, 2, H:].unsqueeze(2).to_broadcast([P, H, NOPE]), ALU.mult))
                        st.do(nc.vector.tensor_tensor(mqk[:, H:, NOPE:], kpe[:, :].unsqueeze(1).to_broadcast([P, H, ROPE]),
                                                      st_m[:, 2, H:].unsqueeze(2).to_broadcast([P, H, ROPE]), ALU.mult))
                        dve.wait_ge(stored[b], 16 * OUTS * i + 1)
                        nc.vector.tensor_copy(mv_out[:, b, :].rearrange("p (h d) -> p h d", d=HD),
                                              kv3[:, :, NOPE:]).then_inc(mv_ready, 1)
                        st.join()
                        dve.sem_inc(heads_ready, 1)
                        dve.wait_ge(mv_ready, t + 1)
                        dve.sem_inc(raw_used, 1)
                        for lo in range(0, 2 * H, 4):
                            turn_to(stage_f[:, b, lo:lo + 4, :], gain_f[:, lo // H:lo // H + 1], FQ)
                        for lo in range(0, 2 * H, 4):
                            turn_to(stage_m[:, b, lo:lo + 4, :], gain_m[:, lo // H:lo // H + 1], MQ)
                        assert st.n == per_tile, st.n



def attend(nc, a, keep):
    G = 4
    NG = NT // G
    with ExitStack() as ctx:
        m = Mem(nc, ctx, "at")
        widths = (MQ + 1, FQ)
        max_row = (MQ, HD)
        raw = [[m.sb(f"raw_{n}{x}", [widths[x], S]) for n in "qk"] for x in range(2)]
        lead = [[m.sb(f"lead_{n}{x}", [widths[x], S], F32R) for n in "qk"] for x in range(2)]
        rest = [[m.sb(f"rest_{n}{x}", [widths[x], S], F32R) for n in "qk"] for x in range(2)]
        v_raw = [m.sb(f"v_raw{x}", [P, NT, HD]) for x in range(2)]
        v_lead = [m.sb(f"v_lead{x}", [P, NT, 2 * HD], F32R) for x in range(2)]
        v_rest = [m.sb(f"v_rest{x}", [P, NT, 2 * HD], F32R) for x in range(2)]
        y = [m.sb(f"y{x}", [HD + 1, S]) for x in range(2)]
        sums = [m.sb(f"sums{x}", [P, S // P]) for x in range(2)]
        inv = [m.sb(f"inv{x}", [P, S // P]) for x in range(2)]
        inv_all = m.sb("inv_all", [HD, S])
        probs = m.sb("probs", [P, 4, CH])
        p_lead = m.sb("p_lead", [P, 4, CH], F32R)
        p_rest = m.sb("p_rest", [P, 4, CH], F32R)
        chunk_max = m.sb("chunk_max", [P, 2, G, NG])
        neg_max = m.sb("neg_max", [P, 2, G], F32R)
        ident_r = m.sb("ident_r", [P, P], F32R)
        ident_b = m.sb("ident_b", [P, P], BF16)
        mask = [m.sb(f"mask{x}", [P, P], BF16) for x in range(2)]
        maskT = [m.sb(f"maskT{x}", [P, P], BF16) for x in range(2)]
        s_ps = [m.ps(f"s{i}", [P, CH]) for i in range(2)]
        st_ps = [m.ps(f"st{i}", [P, CH]) for i in range(4)]
        o_ps = [m.ps(f"o{i}", [P, CH]) for i in range(2)]

        raw_in = [m.sem(f"raw_in{x}") for x in range(2)]
        raw_used = [m.sem(f"raw_used{x}") for x in range(2)]
        split = [m.sem(f"split{x}") for x in range(2)]
        head_used = [m.sem(f"head_used{x}") for x in range(2)]
        y_done = m.sem("y_done")
        row_out = [m.sem(f"row_out{x}") for x in range(2)]
        sums_in = [m.sem(f"sums_in{x}") for x in range(2)]
        inverted = [m.sem(f"inverted{x}") for x in range(2)]
        inv_out = [m.sem(f"inv_out{x}") for x in range(2)]
        inv_in = m.sem("inv_in")
        normalised = m.sem("normalised")
        y_stored = [m.sem(f"y_stored{x}") for x in range(2)]
        masks_set = m.sem("masks_set")
        scored = m.sem("scored")
        score_out = m.sem("score_out")
        max_ready = m.sem("max_ready")
        scoredT = m.sem("scoredT")
        exped = m.sem("exped")
        lead_ready = m.sem("lead_ready")
        rest_ready = m.sem("rest_ready")
        weighted = m.sem("weighted")
        own = m.sem("own")
        tick = m.sem("tick")

        steps = [(x, g) for x in range(2) for g in range(NG)]
        order = []

        ROW_AHEAD = 2

        def max_jobs(n):
            return [("max", n, r, c) for r in range(G) for c in range(steps[n][1] + 1)] + [("row", n, 0, 0)]

        blocks = [(n, kt) for n, (x, g) in enumerate(steps) for kt in range(G * (g + 1))]
        LAG = 3
        for b in range(len(blocks) + LAG):
            if b < len(blocks):
                n, kt = blocks[b]
                KT = G * (steps[n][1] + 1)
                order.append(("score", n, kt, 0))
                ahead = max_jobs((n + 1) % len(steps))
                jobs = len(ahead) - 1
                at = [-(-jobs * min(k, KT - 2) // (KT - 2)) for k in (kt, kt + 1)]
                order += ahead[at[0]:at[1]]
                if kt == KT - ROW_AHEAD:
                    order.append(ahead[-1])
            if 1 <= b <= len(blocks):
                order.append(("rest", *blocks[b - 1], 0))
            if b >= LAG:
                order.append(("weigh", *blocks[b - LAG], 0))
        S_USES = sum(o[0] in ("max", "row") for o in order)
        ST_USES = sum(o[0] == "score" for o in order)
        assert S_USES % 2 == 0 and ST_USES % 4 == 0
        s_jobs = [o for o in order if o[0] in ("max", "row")]
        row_done = {o[1]: s_jobs.index(o) + 1 for o in s_jobs if o[0] == "row"}
        row_done[0] -= S_USES
        S_FIRST = len(max_jobs(0))

        PARTS = 10

        def block(n, kt):
            g = steps[n][1]
            lo = max(kt, G * g) - G * g
            return lo, G - lo

        with nc.Block() as program:
            @program.sync
            def _(sp):
                def load(i, x):
                    wait_alone(sp, raw_used[x], i + 1, tick)
                    for t, name in zip(raw[x], (("mqT", "mkT"), ("fqT", "fkT"))[x]):
                        rows = (MQ, FQ)[x]
                        sp.dma_start(t[0:rows, :], a[name][i]).then_inc(raw_in[x], 16)
                    sp.dma_start(v_raw[x][:, :, :], a[("mv", "fv")[x]][:, :, bass.ds(i * HD, HD)].rearrange("t p d -> p t d")).then_inc(raw_in[x], 16)

                def sums_of(i, x):
                    wait_alone(sp, y_done, len(steps) * i + NG * (x + 1) + 2, tick)
                    sp.dma_start(a["row_sum"][x, i], y[x][HD:HD + 1, :]).then_inc(row_out[x], 16)

                def store(i, x):
                    wait_alone(sp, row_out[x], 16 * i + 16, tick)
                    if x == 1:
                        wait_alone(sp, inverted[1], i + 1, tick)
                    sp.dma_start(sums[x][:, :], a["row_sum"][x, i].rearrange("r (p c) -> (r p) c", p=P)).then_inc(sums_in[x], 16)
                    wait_alone(sp, inverted[x], i + 1 + x, tick)
                    sp.dma_start(a["row_inv"][x, i].rearrange("r (p c) -> (r p) c", p=P), inv[x][:, :]).then_inc(inv_out[x], 16)
                    wait_alone(sp, inv_out[x], 16 * i + 16, tick)
                    wait_alone(sp, normalised, 2 * i + x + 1, tick)
                    sp.dma_start(inv_all[:, :], a["row_inv"][x, i].to_broadcast([HD, S])).then_inc(inv_in, 16)
                    wait_alone(sp, normalised, 2 * i + x + 2, tick)
                    sp.dma_start(a["yT"][x, i], y[x][0:HD, :]).then_inc(y_stored[x], 16)

                for x in range(2):
                    sp.sem_inc(y_stored[x], 1)
                sp.wait_ge(masks_set, 16)
                for x in range(2):
                    load(0, x)
                with sp.Fori(0, H - 1) as i:
                    for x in range(2):
                        sums_of(i, x)
                        load(i + 1, x)
                        store(i, x)
                for x in range(2):
                    sums_of(H - 1, x)
                    store(H - 1, x)
                for x in range(2):
                    sp.wait_ge(y_stored[x], 16 * H + 1)

            @program.gpsimd
            def _(pool):
                for x in range(2):
                    pool.sem_inc(raw_used[x], 1)
                pool.memset(ident_b[:, :], 0.0).then_inc(masks_set, 1)
                for x in range(2):
                    pool.memset(mask[x][:, :], 0.0).then_inc(masks_set, 1)
                    pool.memset(maskT[x][:, :], 0.0).then_inc(masks_set, 1)
                    any_finite = keep["ident"][:, 0:HD].unsqueeze(1).to_broadcast([P, NT, HD])
                    pool.tensor_scalar(v_lead[x][:, :, HD:], any_finite, 0.0, 1.0, ALU.mult, ALU.add).then_inc(masks_set, 1)
                    pool.tensor_scalar(v_rest[x][:, :, HD:], any_finite, 0.0, 0.0, ALU.mult, ALU.add).then_inc(masks_set, 1)
                pool.wait_ge(masks_set, 9)
                pool.memset(raw[0][0][MQ:MQ + 1, :], 0.0).then_inc(masks_set, 1)
                pool.wait_ge(masks_set, 10)
                pool.memset(raw[0][1][MQ:MQ + 1, :], 1.0).then_inc(masks_set, 1)
                pool.wait_ge(masks_set, 11)
                pool.affine_select(out=ident_b[:, :], in_=ident_b[:, :], compare_op=ALU.not_equal, fill=1.0,
                                   base=0, pattern=[[-1, P]], channel_multiplier=1).then_inc(masks_set, 1)
                pool.wait_ge(masks_set, 12)
                pool.memset(mask[0][0:P // 2, P // 2:P], MASKED).then_inc(masks_set, 1)
                pool.wait_ge(masks_set, 13)
                pool.memset(maskT[0][P // 2:P, 0:P // 2], MASKED).then_inc(masks_set, 1)
                pool.wait_ge(masks_set, 14)
                pool.affine_select(out=mask[1][:, :], in_=mask[1][:, :], compare_op=ALU.is_ge, fill=MASKED,
                                   base=0, pattern=[[-1, P]], channel_multiplier=1).then_inc(masks_set, 1)
                pool.affine_select(out=maskT[1][:, :], in_=maskT[1][:, :], compare_op=ALU.is_ge, fill=MASKED,
                                   base=0, pattern=[[1, P]], channel_multiplier=-1).then_inc(masks_set, 1)
                def split_head(i, x):
                    wait_alone(pool, raw_in[x], 48 * i + 48, tick)
                    wait_alone(pool, head_used[x], i + 1, tick)
                    parts = [(raw[x][n][:, c:c + CH], lead[x][n][:, c:c + CH], rest[x][n][:, c:c + CH])
                             for n in range(2) for c in range(0, S, CH)]
                    parts += [(v_raw[x][:, c:c + 8, :], v_lead[x][:, c:c + 8, 0:HD], v_rest[x][:, c:c + 8, 0:HD])
                              for c in range(0, NT, 8)]
                    assert len(parts) == PARTS
                    for whole, first, second in parts:
                        pool.tensor_scalar(first, whole, 1.0, 0.0, ALU.mult, ALU.add).then_inc(split[x], 1)
                    wait_alone(pool, split[x], 2 * PARTS * i + PARTS, tick)
                    for whole, first, second in parts:
                        pool.tensor_tensor(second, whole, first.bitcast(F32), ALU.subtract).then_inc(split[x], 1)
                    wait_alone(pool, split[x], 2 * PARTS * (i + 1), tick)
                    pool.sem_inc(raw_used[x], 1)

                def normalise(i, x):
                    wait_alone(pool, inv_in, 16 * (2 * i + x + 1), tick)
                    pool.tensor_tensor(y[x][0:HD, :], y[x][0:HD, :], inv_all[:, :], ALU.mult).then_inc(normalised, 1)

                pool.sem_inc(normalised, 1)
                for x in range(2):
                    split_head(0, x)
                with pool.Fori(0, H - 1) as i:
                    for x in range(2):
                        split_head(i + 1, x)
                        normalise(i, x)
                pool.sem_inc(split[0], 2 * PARTS)
                for x in range(2):
                    normalise(H - 1, x)

            @program.tensor
            def _(pe):
                pe.sem_inc(weighted, 4)
                for x in range(2):
                    pe.sem_inc(head_used[x], 1)
                pe.wait_ge(masks_set, 18)
                def maximum(head, n, r, c, at):
                    x, g = steps[n]
                    t, lo = G * g + r, G * c
                    hi = min(lo + 4, t + 1)
                    if g == 0 and r == 0:
                        pe.wait_ge(split[x], 2 * PARTS * head + PARTS)
                    pe.wait_ge(score_out, at[0] + 1)
                    bank = s_ps[at[1] % 2]
                    diagonal = hi == t + 1
                    last = nc.tensor.matmul(bank[:, 0:(hi - lo) * P], lead[x][0][:, t * P:(t + 1) * P],
                                            lead[x][1][:, lo * P:hi * P], start=True, stop=not diagonal)
                    if diagonal:
                        last = nc.tensor.matmul(bank[:, (t - lo) * P:(hi - lo) * P], ident_b[:, :], mask[x][:, :],
                                                start=False, stop=True)
                    last.then_inc(scored, 1)

                def row(step_number, n, at):
                    pe.wait_ge(score_out, at[0] + 1)
                    pe.wait_ge(max_ready, G * step_number + G)
                    for r in range(G):
                        last = nc.tensor.matmul(s_ps[at[1] % 2][:, r * P:(r + 1) * P],
                                                neg_max[:, n % 2, r:r + 1].to_broadcast([P, P]), ident_r[:, :],
                                                start=True, stop=True)
                    last.then_inc(scored, 1)

                for n_s, (kind, n, p1, p2) in enumerate(max_jobs(0)):
                    if kind == "max":
                        maximum(0, n, p1, p2, (n_s, n_s))
                    else:
                        row(0, n, (n_s, n_s))
                with pe.Fori(0, H) as i:
                    n_s, n_st, n_w = S_FIRST, 0, 0
                    for kind, n, p1, p2 in order:
                        x, g = steps[n]
                        (q_lead, k_lead), (q_rest, k_rest) = lead[x], rest[x]
                        if kind == "max":
                            maximum(i + (1 if n == 0 else 0), n, p1, p2, (S_USES * i + n_s, n_s))
                            n_s += 1
                        elif kind == "row":
                            row(len(steps) * (i + (1 if n == 0 else 0)) + n, n, (S_USES * i + n_s, n_s))
                            n_s += 1
                        elif kind == "score":
                            kt = p1
                            lo, width = block(n, kt)
                            if g == 0 and kt == 0:
                                pe.wait_ge(split[x], 2 * PARTS * (i + 1))
                            if kt == 0:
                                pe.wait_ge(score_out, S_USES * i + S_FIRST + row_done[n] + 2)
                            pe.wait_ge(exped, ST_USES * i + n_st + 1)
                            bank = st_ps[n_st % 4][:, 0:width * P]
                            ks = slice(kt * P, (kt + 1) * P)
                            qs = slice((G * g + lo) * P, (G * g + G) * P)
                            nc.tensor.matmul(bank, k_lead[:, ks], q_rest[:, qs], start=True, stop=False)
                            nc.tensor.matmul(bank, k_rest[:, ks], q_lead[:, qs], start=False, stop=False)
                            diagonal = kt >= G * g
                            last = nc.tensor.matmul(bank, k_lead[:, ks], q_lead[:, qs], start=False, stop=not diagonal)
                            if diagonal:
                                last = nc.tensor.matmul(st_ps[n_st % 4][:, 0:P], ident_b[:, :], maskT[x][:, :],
                                                        start=False, stop=True)
                            last.then_inc(scoredT, 1)
                            n_st += 1
                        elif kind == "weigh":
                            kt = p1
                            lo, width = block(n, kt)
                            pe.wait_ge(rest_ready, ST_USES * i + n_w + 1)
                            if kt == 0:
                                pe.wait_ge(y_done, len(steps) * i + n + 1)
                            out = o_ps[n % 2][:, lo * P:CH]
                            ws = slice(0, width * P)
                            last_kt = kt == G * g + G - 1
                            nc.tensor.matmul(out, v_rest[x][:, kt, :], p_lead[:, n_w % 4, ws], start=kt == 0, stop=False)
                            nc.tensor.matmul(out, v_lead[x][:, kt, :], p_rest[:, n_w % 4, ws], start=False, stop=False)
                            last = nc.tensor.matmul(out, v_lead[x][:, kt, :], p_lead[:, n_w % 4, ws], start=False, stop=last_kt)
                            last.then_inc(weighted, 1)
                            n_w += 1
                            if g == NG - 1 and kt == NT - 1:
                                pe.wait_ge(weighted, ST_USES * i + n_w + 4)
                                pe.sem_inc(head_used[x], 1)

            @program.scalar
            def _(act):
                act.sem_inc(exped, 4)
                with act.Fori(0, H) as i:
                    def lead_of(b):
                        width = block(*blocks[b])[1] * P
                        act.wait_ge(exped, ST_USES * i + b + 1 + 4)
                        nc.scalar.activation(p_lead[:, b % 4, 0:width], probs[:, b % 4, 0:width], ACT.Copy).then_inc(lead_ready, 1)

                    for b, (n, kt) in enumerate(blocks):
                        width = block(n, kt)[1] * P
                        act.wait_ge(scoredT, ST_USES * i + b + 1)
                        act.wait_ge(weighted, ST_USES * i + b + 1)
                        nc.scalar.activation(probs[:, b % 4, 0:width], st_ps[b % 4][:, 0:width], ACT.Exp).then_inc(exped, 1)
                        if b >= 1:
                            lead_of(b - 1)
                    lead_of(len(blocks) - 1)

            @program.vector
            def _(dve):
                dve.sem_inc(score_out, 2)
                dve.sem_inc(y_done, 2)
                dve.sem_inc(sums_in[1], 1)
                dve.wait_ge(masks_set, 16)
                nc.vector.tensor_copy(ident_r[:, :], keep["ident"][:, :]).then_inc(masks_set, 1)
                nc.vector.memset(sums[1][:, :], 1.0).then_inc(masks_set, 1)
                dve.wait_ge(masks_set, 18)
                def maximum(n, r, c, at):
                    g = steps[n][1]
                    t, lo = G * g + r, G * c
                    hi = min(lo + 4, t + 1)
                    dve.wait_ge(scored, at[0] + 1)
                    nc.vector.tensor_reduce(chunk_max[:, n % 2, r, c:c + 1], s_ps[at[1] % 2][:, 0:(hi - lo) * P],
                                            AX.X, ALU.max).then_inc(score_out, 1)
                    if hi == t + 1:
                        dve.wait_ge(score_out, at[0] + 1 + 2)
                        nc.vector.tensor_reduce(neg_max[:, n % 2, r:r + 1], chunk_max[:, n % 2, r, 0:g + 1],
                                                AX.X, ALU.max, negate=True).then_inc(max_ready, 1)

                def row_to_q(head, n, at):
                    x, g = steps[n]
                    dve.wait_ge(scored, at[0] + 1)
                    if g == 0:
                        dve.wait_ge(split[x], 2 * PARTS * (head + 1))
                    rows = slice(max_row[x], max_row[x] + 1)
                    nc.vector.tensor_copy(lead[x][0][rows, g * CH:(g + 1) * CH], s_ps[at[1] % 2][rows, :]).then_inc(score_out, 1)

                def invert(x, value):
                    dve.wait_ge(sums_in[x], value)
                    nc.vector.reciprocal(inv[x][:, :], sums[x][:, :]).then_inc(inverted[x], 1)

                for n_s, (kind, n, p1, p2) in enumerate(max_jobs(0)):
                    if kind == "max":
                        maximum(n, p1, p2, (n_s, n_s))
                    else:
                        row_to_q(0, n, (n_s, n_s))
                with dve.Fori(0, H) as i:
                    n_s, n_w, n_r = S_FIRST, 0, 0
                    for kind, n, p1, p2 in order:
                        x, g = steps[n]
                        if kind == "max":
                            maximum(n, p1, p2, (S_USES * i + n_s, n_s))
                            n_s += 1
                        elif kind == "row":
                            row_to_q(i + (1 if n == 0 else 0), n, (S_USES * i + n_s, n_s))
                            n_s += 1
                        elif kind == "rest":
                            width = block(n, p1)[1] * P
                            dve.wait_ge(lead_ready, ST_USES * i + n_r + 1)
                            nc.vector.tensor_tensor(p_rest[:, n_r % 4, 0:width], probs[:, n_r % 4, 0:width],
                                                    p_lead[:, n_r % 4, 0:width].bitcast(F32), ALU.subtract).then_inc(rest_ready, 1)
                            n_r += 1
                            if (n, p1) == (2, 8):
                                invert(1, 16 * i + 1)
                            if (n, p1) == (6, 8):
                                invert(0, 16 * i + 16)
                        elif kind == "weigh":
                            n_w += 1
                            if p1 == G * (g + 1) - 1:
                                b = n % 2
                                dve.wait_ge(weighted, ST_USES * i + n_w + 4)
                                if g == 0:
                                    dve.wait_ge(y_stored[x], 16 * i + 1)
                                nc.vector.tensor_copy(y[x][:, g * CH:(g + 1) * CH], o_ps[b][0:HD + 1, :]).then_inc(y_done, 1)
                invert(1, 16 * H + 1)


def s5(nc, a, keep):
    TC = NC_ + 1
    with ExitStack() as ctx:
        m = Mem(nc, ctx, "s5")
        lr = m.sb("lr", [P, GROUPS])
        li = m.sb("li", [P, GROUPS])
        dt = m.sb("dt", [P, GROUPS])
        w = m.sb("w", [P, 12, GROUPS])
        pr = m.sb("pr", [P, GROUPS, STEP + 1])
        pi = m.sb("pi", [P, GROUPS, STEP + 1])
        back_r = m.sb("back_r", [P, GROUPS, STEP])
        back_i = m.sb("back_i", [P, GROUPS, STEP])
        mag8 = m.sb("mag8", [P, GROUPS])
        turn8 = m.sb("turn8", [P, GROUPS])
        b1 = m.sb("b1", [P, GROUPS, GC])
        b2 = m.sb("b2", [P, GROUPS, GC])
        c1 = m.sb("c1", [P, GROUPS, GC])
        c2 = m.sb("c2", [P, GROUPS, GC])
        bb1 = m.sb("bb1", [P, GROUPS, GC])
        bb2 = m.sb("bb2", [P, GROUPS, GC])
        skip = m.sb("skip", [GC, GROUPS, GC])
        step_i = m.sb("step_i", [P, TC], I32)
        step_no = m.sb("step_no", [P, TC])
        u_in = m.sb("u_in", [P, 2, STEP, P])
        u_grp = m.sb("u_grp", [P, 2, GB, P])
        uT = m.sb("uT", [P, GB, 2, P])
        tmp = m.sb("tmp", [P, GB, (STEP + 1) * GC])
        tmp2 = m.sb("tmp2", [P, GB, (STEP + 1) * GC])
        h_rows = m.sb("h_rows", [P, 2, GB, P])
        hT = m.sb("hT", [P, 2, GB, P])
        ca1 = m.sb("ca1", [P, GB, (STEP + 1) * GC])
        g2 = m.sb("g2", [P, GB, STEP * GC])
        k_out = m.sb("k_out", [GC, GB, P])
        toep = m.sb("toep", [P, GB, P])
        arg = m.sb("arg", [P, GB, TC])
        whole = m.sb("whole", [P, GB, TC])
        sin_t = m.sb("sin_t", [P, GB, TC])
        cos_t = m.sb("cos_t", [P, GB, TC])
        drive = m.sb("drive", [P, NC_])
        drive2 = m.sb("drive2", [P, NC_])
        z = m.sb("z", [P, NC_ + 1])
        xc = m.sb("xc", [P, 2, GB, NC_])
        y_tok = m.sb("y_tok", [P, 2, STEP, P])
        gel = m.sb("gel", [P, WIDTH // P, S])
        ident = keep["ident"]
        q = [m.ps(f"q{i}", [P, CH]) for i in range(8)]

        params_in = m.sem("params_in")
        consts = m.sem("consts")
        params_act = m.sem("params_act")
        params_ready = m.sem("params_ready")
        batch_done = m.sem("batch_done")
        u_loaded = m.sem("u_loaded")
        u_grouped = m.sem("u_grouped")
        u_turned = m.sem("u_turned")
        u_ready = m.sem("u_ready")
        rows_ready = m.sem("rows_ready")
        angles_ready = m.sem("angles_ready")
        waves_ready = m.sem("waves_ready")
        h_turned = m.sem("h_turned")
        h_ready = m.sem("h_ready")
        k_done = m.sem("k_done")
        k_copied = m.sem("k_copied")
        k_ready = m.sem("k_ready")
        shifted = m.sem("shifted")
        driven = m.sem("driven")
        drive_used = m.sem("drive_used")
        x_ready = m.sem("x_ready")
        y_done = m.sem("y_done")
        y_copied = m.sem("y_copied")
        y_turned = m.sem("y_turned")
        gelu_done = m.sem("gelu_done")
        own = m.sem("own")
        tick = m.sem("tick")

        with nc.Block() as block:
            @block.gpsimd
            def _(pool):
                pool.iota(step_i[:, :], pattern=[[1, TC]], base=-1, channel_multiplier=0).then_inc(consts, 1)
                pool.memset(toep[:, :, :], 0.0).then_inc(consts, 1)
                pool.memset(z[:, 0:1], 0.0).then_inc(consts, 1)
                for dst, name in ((lr[:, :], "s5_lr"), (li[:, :], "s5_li"), (dt[:, :], "s5_log_dt"),
                                  (b1[:, :, :], "s5_b_ri"), (b2[:, :, :], "s5_b_ir"),
                                  (c1[:, :, :], "s5_c_ri"), (c2[:, :, :], "s5_c_ir")):
                    pool.dma_start(dst, a[name]).then_inc(params_in, 16)
                pool.dma_start(skip[:, :, :].rearrange("c g o -> c (g o)"), a["s5_d"].partition_broadcast(GC)).then_inc(params_in, 16)
                pool.wait_ge(params_in, 16 * 8)
                pool.affine_select(out=skip[:, :, :], in_=skip[:, :, :], compare_op=ALU.is_equal, fill=0.0, base=0,
                                   pattern=[[0, GROUPS], [-1, GC]], channel_multiplier=1).then_inc(consts, 1)
                with pool.Fori(0, NB) as i:
                    wait_alone(pool, batch_done, i + 1, tick)
                    for half in range(2):
                        src = a["u"].rearrange("(h t) p n -> h (t p) n", h=2)[half].rearrange("(c s) n -> c s n", s=STEP)
                        pool.dma_start(u_in[:, half, :, :], src[:, :, bass.ds(i * P, P)]).then_inc(u_loaded, 16)
                    wait_alone(pool, u_loaded, 32 * i + 32, tick)
                    for half in range(2):
                        pool.tensor_copy(u_grp[:, half, :, :].rearrange("c g (s o) -> c g s o", o=GC),
                                         u_in[:, half, :, :].rearrange("c s (g o) -> c g s o", o=GC)).then_inc(u_grouped, 1)

            @block.sync
            def _(sp):
                sp.wait_ge(consts, 4)
                sp.sem_inc(shifted, 1)
                with sp.Fori(0, NB) as i:
                    wait_alone(sp, k_ready, i + 1, tick)
                    for s in range(STEP):
                        sp.dma_start(toep[s * GC:(s + 1) * GC, :, s * GC:P], k_out[:, :, 0:P - s * GC]).then_inc(shifted, 16)

            @block.scalar
            def _(act):
                act.sem_inc(batch_done, 1)
                act.wait_ge(params_in, 16 * 8)
                nc.scalar.activation(dt[:, :], dt[:, :], ACT.Exp).then_inc(params_act, 1)
                act.wait_ge(params_ready, 1)
                nc.scalar.activation(w[:, 0, :], w[:, 4, :], ACT.Exp).then_inc(params_act, 1)
                nc.scalar.activation(mag8[:, :], w[:, 4, :], ACT.Exp, scale=float(STEP)).then_inc(params_act, 1)
                nc.scalar.activation(w[:, 1, :], w[:, 5, :], ACT.Sin).then_inc(params_act, 1)
                nc.scalar.activation(w[:, 2, :], w[:, 5, :], ACT.Sin, scale=0.5).then_inc(params_act, 1)
                with act.Fori(0, NB) as i:
                    act.wait_ge(angles_ready, i + 1)
                    nc.scalar.activation(sin_t[:, :, :], arg[:, :, :], ACT.Sin, scale=6.283185).then_inc(waves_ready, 1)
                    nc.scalar.activation(cos_t[:, :, :], arg[:, :, :], ACT.Sin, scale=3.1415925).then_inc(waves_ready, 1)
                    for j in range(4):
                        act.wait_ge(h_turned, 4 * i + j + 1)
                        nc.scalar.activation(hT[:, j // 2, 4 * (j % 2):4 * (j % 2) + 4, :].rearrange("p g n -> p (g n)"),
                                             q[4 + j][:, :], ACT.Copy).then_inc(h_ready, 1)
                    act.wait_ge(k_done, i + 1)
                    for j in range(2):
                        nc.scalar.activation(k_out[:, 4 * j:4 * j + 4, :].rearrange("p g n -> p (g n)"), q[j][0:GC, :],
                                             ACT.Copy).then_inc(k_copied, 1)
                    for j in range(4):
                        half, g4 = divmod(j, 2)
                        act.wait_ge(y_done, 4 * i + j + 1)
                        nc.scalar.activation(
                            y_tok[:, half, :, 64 * g4:64 * g4 + 64].rearrange("p s (g o) -> p g s o", o=GC),
                            q[j][:, :].rearrange("p (g s o) -> p g s o", g=4, o=GC), ACT.Copy).then_inc(y_copied, 1)
                    gel_b = gel[:, i, :].rearrange("p (h c s) -> p h s c", h=2, s=STEP)
                    for j in range(4):
                        half, s4 = divmod(j, 2)
                        act.wait_ge(y_turned, 4 * i + j + 1)
                        nc.scalar.activation(gel_b[:, half, 4 * s4:4 * s4 + 4, :],
                                             q[4 + j][:, :].rearrange("p (s c) -> p s c", s=4),
                                             ACT.Gelu_apprx_tanh).then_inc(gelu_done, 1)
                    act.wait_ge(gelu_done, 4 * i + 4)
                    act.sem_inc(batch_done, 1)

            @block.tensor
            def _(pe):
                pe.sem_inc(drive_used, 4)
                with pe.Fori(0, NB) as i:
                    pe.wait_ge(batch_done, i + 1)
                    pe.wait_ge(u_grouped, 2 * i + 2)
                    for g in range(GB):
                        for half in range(2):
                            last = nc.tensor.transpose(q[g // 2][:, (g % 2) * 256 + half * P:(g % 2) * 256 + half * P + P],
                                                       u_grp[:, half, g, :], ident[:, :])
                        if g % 2:
                            last.then_inc(u_turned, 1)
                    pe.wait_ge(rows_ready, 2 * i + 1)
                    for j in range(4):
                        for g in range(4):
                            last = nc.tensor.transpose(q[4 + j][:, g * P:(g + 1) * P], h_rows[:, j // 2, 4 * (j % 2) + g, :],
                                                       ident[:, :])
                        last.then_inc(h_turned, 1)
                    pe.wait_ge(rows_ready, 2 * i + 2)
                    pe.wait_ge(u_ready, 4 * i + 4)
                    for g in range(GB):
                        last = nc.tensor.matmul(q[g // 4][0:GC, (g % 4) * P:(g % 4 + 1) * P], h_rows[:, 0, g, P - GC:P],
                                                ca1[:, g, 0:P], start=True, stop=True)
                    last.then_inc(k_done, 1)
                    pe.wait_ge(h_ready, 4 * i + 4)
                    for g in range(GB):
                        pe.wait_ge(drive_used, GB * i + g + 1)
                        for j in range(2):
                            last = nc.tensor.matmul(q[4 + g % 4][:, j * NC_:(j + 1) * NC_], hT[:, j, g, :],
                                                    uT[:, g, :, :].rearrange("p h c -> p (h c)"), start=True, stop=True)
                        last.then_inc(driven, 1)
                    pe.wait_ge(shifted, 16 * STEP * i + 16 * STEP + 1)
                    pe.wait_ge(x_ready, 2 * GB * i + 2 * GB)
                    for half in range(2):
                        cs = slice(half * P, half * P + P)
                        for g in range(GB):
                            out = q[2 * half + g // 4][:, (g % 4) * P:(g % 4 + 1) * P]
                            nc.tensor.matmul(out, uT[:, g, half, :], toep[:, g, :], start=True, stop=False)
                            nc.tensor.matmul(out, xc[:, 0, g, cs], ca1[:, g, GC:P + GC], start=False, stop=False)
                            last = nc.tensor.matmul(out, xc[:, 1, g, cs], g2[:, g, :], start=False, stop=True)
                            if g % 4 == 3:
                                last.then_inc(y_done, 1)
                    pe.wait_ge(y_copied, 4 * i + 4)
                    for j in range(4):
                        half, s4 = divmod(j, 2)
                        for s in range(4):
                            last = nc.tensor.transpose(q[4 + j][:, s * P:(s + 1) * P], y_tok[:, half, 4 * s4 + s, :], ident[:, :])
                        last.then_inc(y_turned, 1)

            @block.vector
            def _(dve):
                st = Steps(nc.vector, own)
                v, tt, ts = nc.vector, nc.vector.tensor_tensor, nc.vector.tensor_scalar
                W = lambda n: w[:, n, :]
                dve.wait_ge(consts, 4)
                dve.wait_ge(params_in, 16 * 8)
                dve.wait_ge(params_act, 1)
                st.do(ts(b2[0:NS, :, :], b2[0:NS, :, :], -1.0, None, ALU.mult))
                st.do(ts(c1[NS:P, :, :], c1[NS:P, :, :], -1.0, None, ALU.mult))
                st.do(ts(c2[:, :, :], c2[:, :, :], -1.0, None, ALU.mult))
                st.do(v.tensor_copy(step_no[:, :], step_i[:, :]))
                st.do(tt(W(4), lr[:, :], dt[:, :], ALU.mult))
                st.then(tt(W(5), li[:, :], dt[:, :], ALU.mult))
                reduce_angle(nc, st, W(5), W(6))
                dve.sem_inc(params_ready, 1)
                st.then(ts(turn8[:, :], W(5), STEP / TWO_PI, None, ALU.mult))
                st.then(ts(W(6), turn8[:, :], MAGIC, None, ALU.add))
                st.then(ts(W(6), W(6), MAGIC, None, ALU.subtract))
                st.do(tt(turn8[:, :], turn8[:, :], W(6), ALU.subtract))
                st.do(tt(W(7), lr[:, :], lr[:, :], ALU.mult))
                st.then(tt(W(8), li[:, :], li[:, :], ALU.mult))
                st.then(tt(W(7), W(7), W(8), ALU.add))
                st.do(v.reciprocal(W(7), W(7)))
                dve.wait_ge(params_act, 5)
                st.then(tt(W(2), W(2), W(2), ALU.mult))
                st.then(ts(W(2), W(2), -2.0, 1.0, ALU.mult, ALU.add))
                a_re, a_im = pr[:, :, 1], pi[:, :, 1]
                st.do(tt(a_re, W(0), W(2), ALU.mult))
                st.do(tt(a_im, W(0), W(1), ALU.mult))
                st.do(v.memset(pr[:, :, 0], 1.0))
                st.then(v.memset(pi[:, :, 0], 0.0))
                st.then(ts(W(3), a_re, 1.0, None, ALU.subtract))
                for n, (x, y) in enumerate(((W(3), lr), (a_im, li), (a_im, lr), (W(3), li))):
                    st.do(tt(W(8 + n), x, y[:, :], ALU.mult))
                st.join()
                st.do(tt(W(8), W(8), W(9), ALU.add))
                st.then(tt(W(10), W(10), W(11), ALU.subtract))
                st.do(tt(W(8), W(8), W(7), ALU.mult))
                st.then(tt(W(10), W(10), W(7), ALU.mult))
                for d in range(2, STEP + 1):
                    for n, (x, y) in enumerate(((pr, a_re), (pi, a_im), (pr, a_im), (pi, a_re))):
                        st.do(tt(W((0, 1, 2, 4)[n]), x[:, :, d - 1], y, ALU.mult))
                    st.join()
                    st.do(tt(pr[:, :, d], W(0), W(1), ALU.subtract))
                    st.then(tt(pi[:, :, d], W(2), W(4), ALU.add))
                for d in range(STEP):
                    st.do(v.tensor_copy(back_r[:, :, STEP - 1 - d], pr[:, :, d]))
                    st.do(v.tensor_copy(back_i[:, :, STEP - 1 - d], pi[:, :, d]))
                wide = lambda x: x.unsqueeze(2).to_broadcast([P, GROUPS, GC])
                flat = lambda x: x[:, :, :].rearrange("p g c -> p (g c)")
                ta = tmp[:, 0:4, :].rearrange("p g c -> p (g c)")[:, 0:GROUPS * GC].rearrange("p (g c) -> p g c", c=GC)
                tb = tmp2[:, 0:4, :].rearrange("p g c -> p (g c)")[:, 0:GROUPS * GC].rearrange("p (g c) -> p g c", c=GC)
                for out, x, y, op in ((bb1, b1, b2, ALU.add), (bb2, b2, b1, ALU.subtract)):
                    st.do(tt(ta, x[:, :, :], wide(W(8)), ALU.mult))
                    st.then(tt(tb, y[:, :, :], wide(W(10)), ALU.mult))
                    st.then(tt(out[:, :, :], ta, tb, op))
                before = st.n
                per_batch = 39
                with dve.Fori(0, NB) as i:
                    st = Steps(nc.vector, own, base=i * per_batch + before)
                    gs = bass.ds(i * GB, GB)
                    dve.wait_ge(batch_done, i + 1)
                    full = [P, GB, TC]
                    st.then(tt(arg[:, :, :], turn8[:, gs].unsqueeze(2).to_broadcast(full),
                               step_no[:, :].unsqueeze(1).to_broadcast(full), ALU.mult))
                    st.then(ts(whole[:, :, :], arg[:, :, :], MAGIC, None, ALU.add))
                    st.then(ts(whole[:, :, :], whole[:, :, :], MAGIC, None, ALU.subtract))
                    tt(arg[:, :, :], arg[:, :, :], whole[:, :, :], ALU.subtract).then_inc(angles_ready, 1)
                    for j in range(4):
                        dve.wait_ge(u_turned, 4 * i + j + 1)
                        v.tensor_copy(uT[:, 2 * j:2 * j + 2, :, :].rearrange("p g h c -> p (g h c)"), q[j][:, :]).then_inc(u_ready, 1)

                    def rows(out, powers_r, powers_i, n, x, y, op, done=None):
                        shape = [P, GB, n, GC]
                        sr, si = (s[:, :, :].unsqueeze(3).to_broadcast(shape) for s in (powers_r, powers_i))
                        bx, by = (s[:, gs, :].unsqueeze(2).to_broadcast(shape) for s in (x, y))
                        t1, t2 = (s[:, :, 0:n * GC].rearrange("p g (s c) -> p g s c", c=GC) for s in (tmp, tmp2))
                        st.do(tt(t1, sr, bx, ALU.mult))
                        st.then(tt(t2, si, by, ALU.mult))
                        ins = tt(out.rearrange("p g (s c) -> p g s c", c=GC), t1, t2, op)
                        if done is None:
                            st.then(ins)
                        else:
                            ins.then_inc(done, 1)

                    br, bi = back_r[:, gs, :], back_i[:, gs, :]
                    rows(h_rows[:, 0, :, :], br, bi, STEP, bb1, bb2, ALU.add)
                    rows(h_rows[:, 1, :, :], bi, br, STEP, bb1, bb2, ALU.subtract, rows_ready)
                    dve.wait_ge(rows_ready, 2 * i + 1)
                    rows(g2[:, :, :], pr[:, gs, 1:], pi[:, gs, 1:], STEP, c2, c1, ALU.subtract)
                    rows(ca1[:, :, :], pr[:, gs, :], pi[:, gs, :], STEP + 1, c1, c2, ALU.add, rows_ready)
                    dve.wait_ge(waves_ready, 2 * i + 2)
                    st.then(tt(cos_t[:, :, :], cos_t[:, :, :], cos_t[:, :, :], ALU.mult))
                    st.then(ts(cos_t[:, :, :], cos_t[:, :, :], -2.0, 1.0, ALU.mult, ALU.add))
                    dve.wait_ge(k_copied, 2 * i + 2)
                    tt(k_out[:, :, 0:GC], k_out[:, :, 0:GC], skip[:, gs, :], ALU.add).then_inc(k_ready, 1)
                    for g in range(GB):
                        dve.wait_ge(driven, GB * i + g + 1)
                        st.do(tt(drive[:, :], q[4 + g % 4][:, 0:NC_], cos_t[:, g, 1:TC], ALU.mult))
                        tt(drive2[:, :], q[4 + g % 4][:, NC_:], sin_t[:, g, 1:TC], ALU.mult).then_inc(drive_used, 1)
                        dve.wait_ge(drive_used, GB * i + g + 1 + 4)
                        st.join()
                        st.then(tt(drive[:, :], drive[:, :], drive2[:, :], ALU.add))
                        st.then(v.tensor_tensor_scan(z[:, 1:NC_ + 1], mag8[:, bass.ds(i * GB + g, 1)].to_broadcast([P, NC_]),
                                                     drive[:, :], 0.0, ALU.mult, ALU.add))
                        tt(xc[:, 0, g, :], z[:, 0:NC_], cos_t[:, g, 0:NC_], ALU.mult).then_inc(x_ready, 1)
                        tt(xc[:, 1, g, :], z[:, 0:NC_], sin_t[:, g, 0:NC_], ALU.mult).then_inc(x_ready, 1)
                    assert st.n == per_batch, st.n

        with ExitStack() as glu_ctx:
            m = Mem(nc, glu_ctx, "gl")
            w_glu = m.sb("w_glu", [P, WIDTH // P, WIDTH])
            b_glu = m.sb("b_glu", [P, WIDTH // P])
            gate = m.sb("gate", [P, 2, CH])
            out = m.sb("out", [P, 4, CH])
            loaded, mixed, gated, multiplied = m.sem("loaded"), m.sem("mixed"), m.sem("gated"), m.sem("multiplied")
            z_stored = [m.sem(f"z_stored{i}") for i in range(4)]
            NJ = WIDTH // P
            with nc.Block() as block:
                @block.sync
                def _(sp):
                    sp.dma_start(w_glu[:, :, :], a["s5_w_glu"]).then_inc(loaded, 16)
                    sp.dma_start(b_glu[:, :], a["s5_b_glu"]).then_inc(loaded, 16)
                    for n in range(4 * NJ):
                        j, c = divmod(n, 4)
                        sp.wait_ge(multiplied, n + 1)
                        sp.dma_start(a["zT"][j, :, c * CH:(c + 1) * CH], out[:, n % 4, :]).then_inc(z_stored[n % 4], 16)
                    for i in range(4):
                        sp.wait_ge(z_stored[i], 16 * NJ)

                @block.tensor
                def _(pe):
                    pe.wait_ge(loaded, 32)
                    for n in range(4 * NJ):
                        j, c = divmod(n, 4)
                        if n >= 4:
                            pe.wait_ge(gated, n - 3)
                        for k in range(NJ):
                            last = nc.tensor.matmul(q[n % 4][:, :], w_glu[:, k, j * P:(j + 1) * P],
                                                    gel[:, k, c * CH:(c + 1) * CH], start=(k == 0), stop=(k == NJ - 1))
                        last.then_inc(mixed, 1)

                @block.scalar
                def _(act):
                    act.wait_ge(loaded, 32)
                    for n in range(4 * NJ):
                        j, c = divmod(n, 4)
                        act.wait_ge(mixed, n + 1)
                        if n >= 2:
                            act.wait_ge(multiplied, n - 1)
                        nc.scalar.activation(gate[:, n % 2, :], q[n % 4][:, :], ACT.Sigmoid,
                                             bias=b_glu[:, j:j + 1]).then_inc(gated, 1)

                @block.vector
                def _(dve):
                    for n in range(4 * NJ):
                        j, c = divmod(n, 4)
                        dve.wait_ge(gated, n + 1)
                        if n >= 4:
                            dve.wait_ge(z_stored[n % 4], 16 * (n // 4))
                        nc.vector.tensor_tensor(out[:, n % 4, :], gel[:, j, c * CH:(c + 1) * CH], gate[:, n % 2, :],
                                                ALU.mult).then_inc(multiplied, 1)


def split_on_pool(pool, whole, lead, rest, leads, done, count, tick):
    pool.tensor_scalar(lead, whole, 1.0, 0.0, ALU.mult, ALU.add).then_inc(leads, 1)
    wait_alone(pool, leads, count + 1, tick)
    pool.tensor_tensor(rest, whole, lead.bitcast(F32), ALU.subtract).then_inc(done, 1)


def merge(nc, a, keep):
    HT = NT // 2
    HC = HT // 2
    HS = S // 2
    BR = 3
    KB = WIDTH // P
    NY = BR * KB
    SLOTS = 3
    with ExitStack() as ctx:
        m = Mem(nc, ctx, "me")
        h_raw = m.sb("h_raw", [P, 2, KD, P])
        h_lead = m.sb("h_lead", [P, KD, HS], F32R)
        h_rest = m.sb("h_rest", [P, KD, HS], F32R)
        y_raw = m.sb("y_raw", [P, 2, HS])
        y_lead = m.sb("y_lead", [P, KB, HS], F32R)
        y_rest = m.sb("y_rest", [P, KB, HS], F32R)
        wm_raw = m.sb("wm_raw", [P, SLOTS, KD, P])
        wm_lead = m.sb("wm_lead", [P, SLOTS, KD, P], F32R)
        wm_rest = m.sb("wm_rest", [P, SLOTS, KD, P], F32R)
        wb_raw = m.sb("wb_raw", [P, SLOTS, KB, P])
        wb_lead = m.sb("wb_lead", [P, SLOTS, KB, P], F32R)
        wb_rest = m.sb("wb_rest", [P, SLOTS, KB, P], F32R)
        gate = m.sb("gate", [P, 2, CH])
        part = m.sb("part", [P, CH])
        both = m.sb("both", [P, KD, HS])
        a_ps = [m.ps(f"a{i}", [P, CH]) for i in range(4)]
        m_ps = [m.ps(f"m{i}", [P, CH]) for i in range(2)]
        o_ps = [m.ps(f"o{i}", [P, CH]) for i in range(2)]

        h_in = [m.sem(f"h_in{b}") for b in range(2)]
        y_in = [m.sem(f"y_in{b}") for b in range(2)]
        wm_in = [m.sem(f"wm_in{i}") for i in range(SLOTS)]
        wb_in = [m.sem(f"wb_in{i}") for i in range(SLOTS)]
        leads = m.sem("leads")
        h_split0 = m.sem("h_split0")
        h_lead1 = m.sem("h_lead1")
        h_split1 = m.sem("h_split1")
        wm_split = m.sem("wm_split")
        wb_split = m.sem("wb_split")
        group_done = m.sem("group_done")
        a_free = m.sem("a_free")
        m_free = m.sem("m_free")
        o_free = m.sem("o_free")
        g_sig = m.sem("g_sig")
        gated = m.sem("gated")
        y_leads = m.sem("y_leads")
        y_split = m.sem("y_split")
        gate_used = m.sem("gate_used")
        merged = m.sem("merged")
        stored = m.sem("stored")
        tick = m.sem("tick")

        wm_tiles, wb_tiles, order = [], [], []
        for br in range(BR):
            pairs = [(b, c) for b in range(KB) for c in range(2)]
            if br == 0:
                pairs[1], pairs[2] = pairs[2], pairs[1]
            base = len(wm_tiles)
            wm_tiles += [("w_gate", br * KB + b) for b in range(KB)]
            order += [("gate", base + b, br * KB + b, br, c) for b, c in pairs]
            cut = KD - 3 if br == BR - 1 else KD
            for js, cs in [([j], (0, 1)) for j in range(cut)] + [(range(cut, KD), (c,)) for c in range(2)]:
                for j in js:
                    order += [("job", len(wm_tiles), len(wb_tiles), (j, br), c) for c in cs]
                    wm_tiles.append(("w_merge", (j, br)))
                    wb_tiles.append((j, br))
        NG, NJ = (sum(o[0] == kind for o in order) for kind in ("gate", "job"))
        NM, NB_ = len(wm_tiles), len(wb_tiles)
        GROUPS_ = NG + 2 * NJ
        assert NG == 2 * NY and NM % SLOTS == 0 and NB_ % SLOTS == 0 and NJ % 2 == 0 and NG % 4 == 0
        wm_last, wb_last, h_last, br_last, block_gated = {}, {}, {}, {}, {}
        group = 0
        for n, (kind, w, b, what, c) in enumerate(order):
            if kind == "gate":
                wm_last[w] = h_last[c] = group
                group += 1
                block_gated[b] = sum(o[0] == "gate" for o in order[:n + 1])
            else:
                wm_last[w] = h_last[c] = group
                wb_last[b] = br_last[what[1]] = group + 1
                group += 2

        with nc.Block() as block:
            @block.sync
            def _(sp):
                with sp.Fori(0, 2) as i:
                    def load_h(t):
                        if t < 2:
                            wait_alone(sp, h_split1, HC * i + t + 1, tick)
                        elif t < HC + 2:
                            wait_alone(sp, h_split0, HC * i + t - 1 + 2, tick)
                        else:
                            wait_alone(sp, h_split1, HC * i + t - 1 - HC + 2, tick)
                        sp.dma_start(h_raw[:, t % 2, :, :], a["hT"][i * HT + t].rearrange("p (k t) -> p k t", t=P)).then_inc(h_in[t % 2], 16)

                    def load_wm(n):
                        wait_alone(sp, wm_split, NM * i + n + 1, tick)
                        name, at = wm_tiles[n]
                        sp.dma_start(wm_raw[:, n % SLOTS, :, :], a[name][at]).then_inc(wm_in[n % SLOTS], 16)

                    def load_wb(n):
                        wait_alone(sp, wb_split, NB_ * i + n + 1, tick)
                        sp.dma_start(wb_raw[:, n % SLOTS, :, :], a["w_branch"][wb_tiles[n]]).then_inc(wb_in[n % SLOTS], 16)

                    def load_y(b):
                        if b >= 2:
                            wait_alone(sp, gated, NG * (i + 1) + block_gated[b - 2], tick)
                        else:
                            wait_alone(sp, gated, NG * i + block_gated[NY - 2 + b], tick)
                        if b < 8:
                            src = a["yT"].rearrange("x (j e) d t -> (x j) (e d) t", e=2)[b]
                        else:
                            src = a["zT"][b - 8]
                        sp.dma_start(y_raw[:, b % 2, :], src[:, bass.ds(i * HS, HS)]).then_inc(y_in[b % 2], 16)

                    for t in range(HC):
                        load_h(t)
                    n_b = n_y = 0
                    for n, (name, at) in enumerate(wm_tiles):
                        load_wm(n)
                        if name == "w_gate":
                            load_y(n_y)
                            n_y += 1
                        else:
                            load_wb(n_b)
                            n_b += 1
                        if n == 1:
                            for t in range(HC, HT):
                                load_h(t)

            @block.gpsimd
            def _(pool):
                pool.sem_inc(h_split0, 2)
                pool.sem_inc(wm_split, SLOTS)
                pool.sem_inc(wb_split, SLOTS)
                PER_TURN = HC + NM + NB_
                with pool.Fori(0, 2) as i:
                    n_split = 0

                    def reuse(last, this_turn):
                        wait_alone(pool, group_done, GROUPS_ * (i + (1 if this_turn else 0)) + last + 1, tick)

                    reuse(h_last[0], False)
                    for t in range(HC):
                        wait_alone(pool, h_in[t % 2], 16 * (HT // 2) * i + 16 * (t // 2) + 16, tick)
                        ts = slice(t * P, (t + 1) * P)
                        split_on_pool(pool, h_raw[:, t % 2, :, :], h_lead[:, :, ts], h_rest[:, :, ts], leads, h_split0,
                                      PER_TURN * i + n_split, tick)
                        n_split += 1

                    n_b = 0
                    for n, (name, at) in enumerate(wm_tiles):
                        s = n % SLOTS
                        wait_alone(pool, wm_in[s], 16 * (NM // SLOTS) * i + 16 * (n // SLOTS) + 16, tick)
                        reuse(wm_last[(n - SLOTS) % NM], n >= SLOTS)
                        split_on_pool(pool, wm_raw[:, s, :, :], wm_lead[:, s, :, :], wm_rest[:, s, :, :], leads, wm_split,
                                      PER_TURN * i + n_split, tick)
                        n_split += 1
                        if name == "w_merge":
                            s = n_b % SLOTS
                            wait_alone(pool, wb_in[s], 16 * (NB_ // SLOTS) * i + 16 * (n_b // SLOTS) + 16, tick)
                            reuse(wb_last[(n_b - SLOTS) % NB_], n_b >= SLOTS)
                            split_on_pool(pool, wb_raw[:, s, :, :], wb_lead[:, s, :, :], wb_rest[:, s, :, :], leads, wb_split,
                                          PER_TURN * i + n_split, tick)
                            n_split += 1
                            n_b += 1

            @block.tensor
            def _(pe):
                def product(bank, w, w_at, v, cs, blocks):
                    for k in range(blocks):
                        first, second = w[0][:, w_at, k, :], w[1][:, w_at, k, :]
                        nc.tensor.matmul(bank[:, :], first, v[1][:, k, cs], start=k == 0, stop=False)
                        nc.tensor.matmul(bank[:, :], first, v[0][:, k, cs], start=False, stop=False)
                        last = nc.tensor.matmul(bank[:, :], second, v[0][:, k, cs], start=False, stop=k == blocks - 1)
                    last.then_inc(group_done, 1)

                pe.sem_inc(group_done, GROUPS_)
                with pe.Fori(0, 2) as i:
                    n_a = n_m = 0
                    for kind, w, b, what, c in order:
                        cs = slice(c * CH, (c + 1) * CH)
                        if n_a + n_m in (0, 2) and kind == "gate":
                            pe.wait_ge((h_split0, h_split1)[c], HC * i + HC + 2)
                        pe.wait_ge(wm_split, NM * i + w + 1 + SLOTS)
                        if kind == "gate":
                            pe.wait_ge(a_free, NG * i + n_a + 1)
                            product(a_ps[n_a % 4], (wm_lead, wm_rest), w % SLOTS, (h_lead, h_rest), cs, KD)
                            n_a += 1
                        else:
                            pe.wait_ge(m_free, NJ * i + n_m + 1)
                            product(m_ps[n_m % 2], (wm_lead, wm_rest), w % SLOTS, (h_lead, h_rest), cs, KD)
                            if what[0] == 0 and c == 0:
                                pe.wait_ge(y_split, NG * i + 2 * KB * (what[1] + 1))
                            pe.wait_ge(wb_split, NB_ * i + b + 1 + SLOTS)
                            pe.wait_ge(o_free, NJ * i + n_m + 1)
                            product(o_ps[n_m % 2], (wb_lead, wb_rest), b % SLOTS, (y_lead, y_rest), cs, KB)
                            n_m += 1

            @block.scalar
            def _(act):
                act.sem_inc(m_free, 2)
                act.sem_inc(stored, 1)
                with act.Fori(0, 2) as i:
                    for t in range(HC, HT):
                        act.wait_ge(h_in[t % 2], 16 * (HT // 2) * i + 16 * (t // 2) + 16)
                        ts = slice(t * P, (t + 1) * P)
                        if t == HC:
                            act.wait_ge(group_done, GROUPS_ * i + h_last[1] + 1)
                        nc.scalar.activation(h_lead[:, :, ts], h_raw[:, t % 2, :, :], ACT.Copy).then_inc(h_lead1, 1)
                    n_g = n_a = n_m = group = 0
                    waiting = []

                    def sigmoid(src, done):
                        act.wait_ge(gate_used, (NG + NJ) * i + n_g + 1)
                        nc.scalar.activation(gate[:, n_g % 2, :], src, ACT.Sigmoid).then_inc(done, 1)

                    def lead_of_y(n, b, c, g):
                        act.wait_ge(gated, NG * (i + 1) + n + 1)
                        if n % (2 * KB) == 0:
                            br = n // (2 * KB)
                            act.wait_ge(group_done, GROUPS_ * (i + (1 if br else 0)) + br_last[(br - 1) % BR] + 1)
                        nc.scalar.activation(y_lead[:, b % KB, c * CH:(c + 1) * CH], gate[:, g % 2, :], ACT.Copy).then_inc(y_leads, 1)

                    def store(n, j, c):
                        act.wait_ge(merged, NJ * i + n + 1)
                        cs = slice(c * CH, (c + 1) * CH)
                        act.dma_start(a["both"][2 * i + c][:, j, :], both[:, j, cs]).then_inc(stored, 16)

                    late = None
                    for kind, w, b, what, c in order:
                        act.wait_ge(group_done, GROUPS_ * (i + 1) + group + 1)
                        if kind == "gate":
                            sigmoid(a_ps[n_a % 4][:, :], g_sig)
                            if late:
                                lead_of_y(*late)
                            late = (n_a, b, c, n_g)
                            n_a += 1
                            group += 1
                            if n_a % (2 * KB) == 0:
                                lead_of_y(*late)
                                late = None
                        else:
                            sigmoid(m_ps[n_m % 2][:, :], m_free)
                            if what[1] == BR - 1:
                                waiting.append((n_m, what[0], c))
                            if len(waiting) > 2:
                                store(*waiting.pop(0))
                            n_m += 1
                            group += 2
                        n_g += 1
                    while waiting:
                        store(*waiting.pop(0))
                act.wait_ge(stored, 16 * 2 * 2 * KD + 1)

            @block.vector
            def _(dve):
                dve.sem_inc(h_split1, 2)
                dve.sem_inc(a_free, 4)
                dve.sem_inc(o_free, 2)
                dve.sem_inc(gate_used, 2)
                dve.sem_inc(gated, NG)
                tt = nc.vector.tensor_tensor
                with dve.Fori(0, 2) as i:
                    for t in range(HC, HT):
                        ts = slice(t * P, (t + 1) * P)
                        dve.wait_ge(h_lead1, HC * i + t - HC + 1)
                        tt(h_rest[:, :, ts], h_raw[:, t % 2, :, :], h_lead[:, :, ts].bitcast(F32), ALU.subtract).then_inc(h_split1, 1)

                    def rest_of_y(n, b, c, g):
                        dve.wait_ge(y_leads, NG * i + n + 1)
                        at = (b % KB, slice(c * CH, (c + 1) * CH))
                        tt(y_rest[:, at[0], at[1]], gate[:, g % 2, :], y_lead[:, at[0], at[1]].bitcast(F32),
                           ALU.subtract).then_inc(y_split, 1)
                        dve.wait_ge(y_split, NG * i + n + 1)
                        dve.sem_inc(gate_used, 1)

                    n_g = n_a = n_m = group = 0
                    late = None
                    for kind, w, b, what, c in order:
                        g, cs = gate[:, n_g % 2, :], slice(c * CH, (c + 1) * CH)
                        if kind == "gate":
                            dve.wait_ge(g_sig, NG * i + n_a + 1)
                            tt(g, a_ps[n_a % 4][:, :], g, ALU.mult).then_inc(a_free, 1)
                            dve.wait_ge(y_in[b % 2], 16 * (NY // 2) * i + 16 * (b // 2) + 16)
                            dve.wait_ge(a_free, NG * i + n_a + 1 + 4)
                            tt(g, y_raw[:, b % 2, cs], g, ALU.mult).then_inc(gated, 1)
                            if late:
                                rest_of_y(*late)
                            late = (n_a, b, c, n_g)
                            n_a += 1
                            group += 1
                            if n_a % (2 * KB) == 0:
                                rest_of_y(*late)
                                late = None
                        else:
                            j, br = what
                            dve.wait_ge(m_free, NJ * i + n_m + 1 + 2)
                            dve.wait_ge(group_done, GROUPS_ * (i + 1) + group + 2)
                            dst, o = both[:, j, cs], o_ps[n_m % 2][:, :]
                            if br == 0:
                                if n_m == 0:
                                    dve.wait_ge(stored, 16 * 2 * KD * i + 1)
                                tt(dst, o, g, ALU.mult).then_inc(merged, 1)
                                dve.wait_ge(merged, NJ * i + n_m + 1)
                                dve.sem_inc(o_free, 1)
                            else:
                                dve.wait_ge(merged, NJ * i + n_m)
                                tt(part[:, :], o, g, ALU.mult).then_inc(o_free, 1)
                                dve.wait_ge(o_free, NJ * i + n_m + 1 + 2)
                                tt(dst, dst, part[:, :], ALU.add).then_inc(merged, 1)
                            dve.sem_inc(gate_used, 1)
                            n_m += 1
                            group += 2
                        n_g += 1


def output(nc, a, keep):
    SLOTS = 4
    with ExitStack() as ctx:
        m = Mem(nc, ctx, "ou")
        w_raw = m.sb("w_raw", [P, KD, D])
        w_lead = m.sb("w_lead", [P, KD, D], F32R)
        w_rest = m.sb("w_rest", [P, KD, D], F32R)
        b_raw = m.sb("b_raw", [P, SLOTS, KD, P])
        b_lead = m.sb("b_lead", [P, SLOTS, KD, P], F32R)
        b_rest = m.sb("b_rest", [P, SLOTS, KD, P], F32R)
        x_in = m.sb("x_in", [P, SLOTS, D])
        out = m.sb("out", [P, 2, D])
        ps = [m.ps(f"ps{i}", [P, CH]) for i in range(4)]

        w_in = [m.sem(f"w_in{k}") for k in range(2)]
        w_leads = m.sem("w_leads")
        w_split = m.sem("w_split")
        b_in = [m.sem(f"b_in{s}") for s in range(SLOTS)]
        x_loaded = [m.sem(f"x_loaded{s}") for s in range(SLOTS)]
        leads = m.sem("leads")
        b_split = m.sem("b_split")
        full = m.sem("full")
        added = m.sem("added")
        stored = [m.sem(f"stored{s}") for s in range(2)]
        tick = m.sem("tick")

        with nc.Block() as block:
            @block.sync
            def _(sp):
                sp.sem_inc(full, 2 * SLOTS)
                sp.sem_inc(added, 2 * SLOTS)

                with sp.Fori(0, NT // SLOTS) as i:
                    for s in range(SLOTS):
                        wait_alone(sp, full, 2 * SLOTS * i + 2 * s + 2, tick)
                        sp.dma_start(b_raw[:, s, :, :], a["both"][i][:, :, s * P:(s + 1) * P]).then_inc(b_in[s], 16)
                        wait_alone(sp, added, 2 * SLOTS * i + 2 * s + 2, tick)
                        sp.dma_start(x_in[:, s, :], a["x"][i * SLOTS + s]).then_inc(x_loaded[s], 16)

            @block.gpsimd
            def _(pool):
                with pool.Fori(0, NT // SLOTS) as i:
                    for s in range(SLOTS):
                        wait_alone(pool, b_in[s], 16 * i + 16, tick)
                        split_on_pool(pool, b_raw[:, s, :, :], b_lead[:, s, :, :], b_rest[:, s, :, :], leads, b_split,
                                      SLOTS * i + s, tick)

            @block.scalar
            def _(act):
                for k in range(KD):
                    act.dma_start(w_raw[:, k, :], a["w_out"][:, k, :]).then_inc(w_in[k // 4], 16)
                for k in range(KD):
                    act.wait_ge(w_in[k // 4], 64)
                    nc.scalar.activation(w_lead[:, k, :], w_raw[:, k, :], ACT.Copy).then_inc(w_leads, 1)
                for s in range(2):
                    act.sem_inc(stored[s], 1)
                with act.Fori(0, NT // SLOTS) as i:
                    for s in range(SLOTS):
                        act.wait_ge(added, 2 * SLOTS * (i + 1) + 2 * s + 2)
                        act.dma_start(a["out"][i * SLOTS + s], out[:, s % 2, :]).then_inc(stored[s % 2], 16)
                for s in range(2):
                    act.wait_ge(stored[s], 16 * (NT // 2) + 1)

            @block.tensor
            def _(pe):
                with pe.Fori(0, NT // SLOTS) as i:
                    for s in range(SLOTS):
                        pe.wait_ge(b_split, SLOTS * i + s + 1)
                        for c in range(2):
                            n = 2 * s + c
                            cs = slice(c * CH, (c + 1) * CH)
                            pe.wait_ge(added, 2 * SLOTS * i + n + 5)
                            for k in range(KD):
                                if n == 0:
                                    pe.wait_ge(w_split, k + 1)
                                nc.tensor.matmul(ps[n % 4][:, :], b_lead[:, s, k, :], w_rest[:, k, cs], start=k == 0, stop=False)
                                nc.tensor.matmul(ps[n % 4][:, :], b_lead[:, s, k, :], w_lead[:, k, cs], start=False, stop=False)
                                last = nc.tensor.matmul(ps[n % 4][:, :], b_rest[:, s, k, :], w_lead[:, k, cs],
                                                        start=False, stop=k == KD - 1)
                            last.then_inc(full, 1)

            @block.vector
            def _(dve):
                for k in range(KD):
                    dve.wait_ge(w_leads, k + 1)
                    nc.vector.tensor_tensor(w_rest[:, k, :], w_raw[:, k, :], w_lead[:, k, :].bitcast(F32),
                                            ALU.subtract).then_inc(w_split, 1)
                with dve.Fori(0, NT // SLOTS) as i:
                    for s in range(SLOTS):
                        dve.wait_ge(x_loaded[s], 16 * i + 16)
                        dve.wait_ge(stored[s % 2], 16 * (2 * i + s // 2) + 1)
                        for c in range(2):
                            n = 2 * s + c
                            cs = slice(c * CH, (c + 1) * CH)
                            dve.wait_ge(full, 2 * SLOTS * (i + 1) + n + 1)
                            nc.vector.tensor_tensor(out[:, s % 2, cs], ps[n % 4][:, :], x_in[:, s, cs], ALU.add).then_inc(added, 1)


def build(nc, a):
    scratch = {"hT": (NT, P, D), "mqT": (H, MQ, S), "mkT": (H, MQ, S), "fqT": (H, FQ, S), "fkT": (H, FQ, S),
               "mv": (NT, P, WIDTH), "fv": (NT, P, WIDTH), "u": (NT, P, WIDTH), "yT": (2, H, HD, S), "row_sum": (2, H, 1, S),
               "row_inv": (2, H, 1, S), "both": (NT // 4, P, KD, CH),
               "zT": (WIDTH // P, P, S)}
    a = dict(a)
    for name, shape in scratch.items():
        a[name] = nc.dram_tensor(f"scratch_{name}", shape, F32).ap()
    with ExitStack() as ctx:
        keep = {"ident": ctx.enter_context(nc.sbuf_tensor("ident", [P, P], F32)),
                "cum": ctx.enter_context(nc.sbuf_tensor("cum", [P, NT, H, 2], F32))}
        norm_x(nc, a, keep)
        project(nc, a, keep)
        s5(nc, a, keep)
        attend(nc, a, keep)
        merge(nc, a, keep)
        output(nc, a, keep)


def layout(inputs):
    f = {k: np.asarray(v) for k, v in inputs.items()}
    one = {k: v[0] for k, v in f.items() if k not in ("positions",)}
    rows = lambda w: w.reshape(-1, P, w.shape[-1]).transpose(1, 0, 2)
    w = one["w_in"]
    cut = np.cumsum([0, Q_RANK, KV_RANK, ROPE, WIDTH, WIDTH, WIDTH, H, WIDTH, WIDTH, WIDTH, WIDTH, D, D, D])
    cols = lambda i, j: w[:, cut[i]:cut[j]]

    def tiles(w):
        k, j = w.shape[0] // P, w.shape[1] // P
        return w.reshape(k, P, j, P).transpose(2, 1, 0, 3)

    stack = lambda x, y: np.concatenate([x, y], axis=0)
    state = lambda x: x.transpose(1, 0)
    br, bi = (one[k].transpose(1, 0, 2) for k in ("s5_b_re", "s5_b_im"))
    cr, ci = (one[k].transpose(2, 0, 1) for k in ("s5_c_re", "s5_c_im"))
    merge_w = tiles(cols(11, 14)).reshape(3, KD, P, KD, P).transpose(1, 0, 2, 3, 4)
    branch_w = np.stack([tiles(one["w_branch_out"][b * WIDTH:(b + 1) * WIDTH]) for b in range(3)], axis=1)
    col = lambda v: v.reshape(-1, 1)
    out = {
        "x": one["x"].reshape(NT, P, D),
        "positions": f["positions"].reshape(NT, P).transpose(1, 0),
        "inv_freq": np.broadcast_to((1.0 / (np.float32(10000.0) ** (np.arange(0, ROPE, 2, dtype=np.float32) / np.float32(ROPE)))).astype(np.float32), (P, ROPE // 2)),
        "norm_g": one["norm_g"].reshape(KD, P).transpose(1, 0),
        "w_ff": rows(cols(6, 7)), "fox_b_f": one["fox_b_f"],
        "w_lora": rows(cols(0, 3)), "w_fox": rows(cols(3, 6)), "w_u": rows(cols(7, 8)),
        "w_q_up": rows(one["mla_w_q_up"]), "w_kv_up": one["mla_w_kv_up"],
        "gain_lora": np.concatenate([one["mla_q_a_norm"], one["mla_kv_a_norm"]]).reshape(3, P).transpose(1, 0),
        "fox_q_norm": col(one["fox_q_norm"]), "fox_k_norm": col(one["fox_k_norm"]),
        "mla_q_norm": col(one["mla_q_norm"]), "mla_k_norm": col(one["mla_k_norm"]),
        "s5_lr": stack(state(one["s5_lambda_re"]), state(one["s5_lambda_re"])),
        "s5_li": stack(state(one["s5_lambda_im"]), state(one["s5_lambda_im"])),
        "s5_log_dt": np.broadcast_to(one["s5_log_dt"], (P, GROUPS)),
        "s5_b_ri": stack(br, bi), "s5_b_ir": stack(bi, br), "s5_c_ri": stack(cr, ci), "s5_c_ir": stack(ci, cr),
        "s5_d": one["s5_d"], "s5_w_glu": rows(one["s5_w_glu"]), "s5_b_glu": one["s5_b_glu"].reshape(-1, P).transpose(1, 0),
        "w_gate": tiles(cols(8, 11)), "w_merge": merge_w, "w_branch": branch_w, "w_out": rows(one["w_out"]),
    }
    return {k: np.ascontiguousarray(v) for k, v in out.items()}


def kernel(**inputs):
    import concourse.bacc as bacc
    from concourse.bass_utils import run_bass_kernel_spmd

    nc = bacc.Bacc("TRN2", target_bir_lowering=False, num_devices=1)
    arrays = {f"in_{k}": v for k, v in layout(inputs).items()}
    a = {k[3:]: nc.dram_tensor(k, v.shape, mybir.dt.from_np(v.dtype), kind="ExternalInput").ap() for k, v in arrays.items()}
    a["out"] = nc.dram_tensor("out", (NT, P, D), F32, kind="ExternalOutput").ap()
    build(nc, a)
    result = run_bass_kernel_spmd(nc, [arrays], core_ids=[0])
    return result.results[0]["out"].reshape(1, S, D)
```

```python
import math
from contextlib import ExitStack

import numpy as np

import concourse.bass as bass
from concourse import mybir

P = 128
F32 = mybir.dt.float32
F32R = mybir.dt.float32r
BF16 = mybir.dt.bfloat16
I32 = mybir.dt.int32
ALU = mybir.AluOpType
ACT = mybir.ActivationFunctionType
AX = mybir.AxisListType

D = 1024
S = 2048
KD = D // P
NT = S // P
H = 8
Q_RANK, KV_RANK, ROPE, NOPE, HD = 256, 128, 32, 64, 64
MQ = NOPE + ROPE
FQ = HD + 5
WIDTH = H * HD
LQ = Q_RANK + KV_RANK + ROPE + WIDTH
GROUPS, GC, NS = 32, 16, 64
EPS = 1e-6
CH = 512
STEP = 8
NC_ = S // STEP
GB = 8
NB = GROUPS // GB
MAGIC = 1.5 * 2.0 ** 23
TWO_PI = 2.0 * math.pi
C1 = 6.28125
C2 = float(np.float32(math.floor((TWO_PI - C1) * 2 ** 20) / 2 ** 20))
C3 = TWO_PI - C1 - C2
PI_F32 = 3.1415925
MASKED = -1.0e30


class Steps:

    def __init__(self, eng, sem, base=0):
        self.eng, self.sem, self.base, self.n = eng, sem, base, 0

    def do(self, ins):
        ins.then_inc(self.sem, 1)
        self.n += 1

    def join(self):
        self.eng.wait_ge(self.sem, self.base + self.n)

    def then(self, ins):
        self.do(ins)
        self.join()


def wait_alone(eng, sem, value, tick):
    eng.wait_ge(sem, value)
    eng.sem_inc(tick, 1)


class Mem:

    def __init__(self, nc, ctx, tag):
        self.nc, self.ctx, self.tag = nc, ctx, tag

    def sb(self, name, shape, dt=F32):
        return self.ctx.enter_context(self.nc.sbuf_tensor(f"{self.tag}_{name}", shape, dt))

    def ps(self, name, shape, dt=F32):
        return self.ctx.enter_context(self.nc.psum_tensor(f"{self.tag}_{name}", shape, dt))

    def sem(self, name):
        return self.ctx.enter_context(self.nc.semaphore(f"{self.tag}_{name}"))


def norm_x(nc, a, keep):
    with ExitStack() as ctx:
        m = Mem(nc, ctx, "nx")
        x_in = m.sb("x_in", [P, 2, D])
        square = m.sb("square", [P, D])
        h = m.sb("h", [P, 2, D])
        hT = m.sb("hT", [P, 2, KD, P])
        h_lead = m.sb("h_lead", [P, 2, KD, P], F32R)
        h_rest = m.sb("h_rest", [P, 2, KD, P], F32R)
        w_raw = m.sb("w_raw", [P, 3, D])
        w_lead = m.sb("w_lead", [P, KD, D], F32R)
        w_rest = m.sb("w_rest", [P, KD, D], F32R)
        vu_out = m.sb("vu_out", [P, 2, 2, CH])
        gain = m.sb("gain", [P, KD])
        w_ff = m.sb("w_ff", [P, KD, H])
        ff = m.sb("ff", [P, NT, H])
        b_f = m.sb("b_f", [P, H])
        stat = m.sb("stat", [P, 2, 3])
        lf = m.sb("lf", [P, 4, NT * H])
        tri = m.sb("tri", [P, P])
        ones = m.sb("ones", [P, P])
        total = m.sb("total", [P, NT, H])
        cum_lead = m.sb("cum_lead", [P, NT * H], F32R)
        ident = keep["ident"]
        t_ps = [m.ps(f"t{i}", [P, 4, P]) for i in range(4)]
        ff_ps = [m.ps(f"ff{i}", [P, CH]) for i in range(2)]
        vu_ps = [m.ps(f"vu{i}", [P, CH]) for i in range(2)]

        params_in = m.sem("params_in")
        x_loaded = [m.sem(f"x_loaded{b}") for b in range(2)]
        w_in = [m.sem(f"w_in{s}") for s in range(3)]
        w_leads = m.sem("w_leads")
        w_split = m.sem("w_split")
        consts_set = m.sem("consts_set")
        squared = m.sem("squared")
        mean_ready = m.sem("mean_ready")
        root_ready = m.sem("root_ready")
        h_done = m.sem("h_done")
        transposed = m.sem("transposed")
        hT_copied = m.sem("hT_copied")
        hT_stored = [m.sem(f"hT_stored{b}") for b in range(2)]
        h_leads = m.sem("h_leads")
        h_split = m.sem("h_split")
        products = m.sem("products")
        evacuated = m.sem("evacuated")
        vu_stored = [m.sem(f"vu_stored{b}") for b in range(2)]
        logs = m.sem("logs")
        summed = m.sem("summed")
        own = m.sem("own")
        tick = keep["tick"]
        LOOP = NT // 2 - 1

        def iterations(eng, body):
            with eng.Fori(0, LOOP) as i:
                for b in range(2):
                    body(2 * i + b, b, i)
            for b in range(2):
                body(NT - 2 + b, b, LOOP)

        with nc.Block() as block:
            @block.sync
            def _(sp):
                def load_x(t, b):
                    sp.dma_start(x_in[:, b, :], a["x"][t]).then_inc(x_loaded[b], 16)

                def store_hT(t, b):
                    wait_alone(sp, hT_copied, 2 * t + 2, tick)
                    sp.dma_start(a["hT"][t], hT[:, b, :, :].rearrange("p k t -> p (k t)")).then_inc(hT_stored[b], 16)

                load_x(0, 0)
                load_x(1, 1)
                sp.dma_start(gain[:, :], a["norm_g"]).then_inc(params_in, 16)
                sp.dma_start(w_ff[:, :, :], a["w_ff"]).then_inc(params_in, 16)
                sp.dma_start(b_f[:, :], a["fox_b_f"].partition_broadcast(P)).then_inc(params_in, 16)
                for b in range(2):
                    sp.sem_inc(hT_stored[b], 1)
                    sp.sem_inc(vu_stored[b], 1)
                store_hT(0, 0)

                def body(t, b, i):
                    if i is not LOOP:
                        wait_alone(sp, h_done, t + 1, tick)
                        load_x(t + 2, b)
                    if not (i is LOOP and b):
                        store_hT(t + 1, 1 - b)
                    wait_alone(sp, evacuated, 3 * t + 3 + 6, tick)
                    sp.dma_start(a["fv"][t], vu_out[:, b, 0, :]).then_inc(vu_stored[b], 16)
                    sp.dma_start(a["u"][t], vu_out[:, b, 1, :]).then_inc(vu_stored[b], 16)

                iterations(sp, body)
                for b in range(2):
                    sp.wait_ge(hT_stored[b], 16 * (NT // 2) + 1)
                    sp.wait_ge(vu_stored[b], 32 * (NT // 2) + 1)

            @block.gpsimd
            def _(pool):
                def load_w(n):
                    name, k = ("w_vu", n) if n < KD else ("w_lq", n - KD)
                    width = D if n < KD else LQ
                    pool.dma_start(w_raw[:, n % 3, 0:width], a[name][:, k, :]).then_inc(w_in[n % 3], 16)

                for n in range(3):
                    load_w(n)
                pool.memset(ones[:, :], 1.0).then_inc(consts_set, 1)
                pool.memset(ident[:, :], 0.0).then_inc(consts_set, 1)
                pool.wait_ge(consts_set, 2)
                pool.affine_select(out=ident[:, :], in_=ident[:, :], compare_op=ALU.not_equal, fill=1.0,
                                   base=0, pattern=[[-1, P]], channel_multiplier=1).then_inc(consts_set, 1)
                pool.affine_select(out=tri[:, :], in_=ones[:, :], compare_op=ALU.is_ge, fill=0.0,
                                   base=0, pattern=[[1, P]], channel_multiplier=-1).then_inc(consts_set, 1)
                pool.sem_inc(h_split, 2)

                def split_w(n):
                    if n >= KD:
                        raw = w_raw[:, n % 3, 0:LQ]
                        first, second = (keep[key][:, n - KD, :] for key in ("wq_lead", "wq_rest"))
                        pool.wait_ge(w_in[n % 3], 16 * (n // 3) + 16)
                        pool.tensor_scalar(first, raw, 1.0, 0.0, ALU.mult, ALU.add).then_inc(w_leads, 1)
                        pool.wait_ge(w_leads, n + 1)
                        pool.wait_ge(w_split, n)
                        pool.tensor_tensor(second, raw, first.bitcast(F32), ALU.subtract).then_inc(w_split, 1)
                    if n + 3 < 2 * KD:
                        pool.wait_ge(w_split, n + 1)
                        load_w(n + 3)

                def rest_of_h(t, b):
                    wait_alone(pool, h_leads, t + 1, tick)
                    wait_alone(pool, products, 3 * t + 3, tick)
                    pool.tensor_tensor(h_rest[:, b, :, :], hT[:, b, :, :], h_lead[:, b, :, :].bitcast(F32),
                                       ALU.subtract).then_inc(h_split, 1)

                for n in range(KD):
                    split_w(n)
                rest_of_h(0, 0)
                for n in range(KD, 2 * KD):
                    rest_of_h(n - KD + 1, (n - KD + 1) % 2)
                    split_w(n)
                with pool.Fori(KD // 2, NT // 2 - 1) as i:
                    for b in range(2):
                        rest_of_h(2 * i + 1 + b, 1 - b)
                rest_of_h(NT - 1, 1)

            @block.scalar
            def _(act):
                def norm(t, b, i):
                    act.wait_ge(x_loaded[b], 16 * i + 16)
                    act.wait_ge(mean_ready, t + 1)
                    nc.scalar.activation(square[:, :], x_in[:, b, :], ACT.Square,
                                         accum_out=stat[:, b, 0:1]).then_inc(squared, 1)
                    act.wait_ge(mean_ready, t + 2)
                    nc.scalar.activation(stat[:, b, 2:3], stat[:, b, 1:2], ACT.Sqrt).then_inc(root_ready, 1)

                def lead_of_h(t, b):
                    act.wait_ge(hT_copied, 2 * t + 2)
                    act.wait_ge(products, 3 * t + 3)
                    nc.scalar.activation(h_lead[:, b, :, :], hT[:, b, :, :], ACT.Copy).then_inc(h_leads, 1)

                act.sem_inc(evacuated, 6)
                norm(0, 0, 0)
                norm(1, 1, 0)
                for k in range(KD):
                    act.wait_ge(w_in[k % 3], 16 * (k // 3) + 16)
                    nc.scalar.activation(w_lead[:, k, :], w_raw[:, k % 3, :], ACT.Copy).then_inc(w_leads, 1)
                lead_of_h(0, 0)

                def body(t, b, i):
                    if i is not LOOP:
                        norm(t + 2, b, i + 1)
                    if not (i is LOOP and b):
                        lead_of_h(t + 1, 1 - b)
                    act.wait_ge(products, 3 * t + 1 + 6)
                    nc.scalar.activation(ff[:, t, :], ff_ps[b][:, 0:H], ACT.Copy).then_inc(evacuated, 1)
                    act.wait_ge(vu_stored[b], 32 * i + 1)
                    for n in range(2):
                        act.wait_ge(products, 3 * t + n + 2 + 6)
                        nc.scalar.activation(vu_out[:, b, n, :], vu_ps[n][:, :], ACT.Copy).then_inc(evacuated, 1)

                iterations(act, body)
                act.wait_ge(logs, 1)
                nc.scalar.activation(lf[:, 2, :], lf[:, 1, :], ACT.Exp, scale=-1.0).then_inc(logs, 1)
                act.wait_ge(logs, 3)
                nc.scalar.activation(lf[:, 3, :], lf[:, 2, :], ACT.Ln).then_inc(logs, 1)

            @block.vector
            def _(dve):
                dve.sem_inc(mean_ready, 1)

                def norm(t, b):
                    dve.wait_ge(squared, t + 1)
                    nc.vector.tensor_scalar(stat[:, b, 1:2], stat[:, b, 0:1], 1.0 / D, EPS,
                                            ALU.mult, ALU.add).then_inc(mean_ready, 1)
                    dve.wait_ge(root_ready, t + 1)
                    Steps(nc.vector, own, base=t).then(nc.vector.reciprocal(stat[:, b, 1:2], stat[:, b, 2:3]))
                    dve.wait_ge(transposed, 2 * t + 2)
                    nc.vector.tensor_scalar(h[:, b, :], x_in[:, b, :], stat[:, b, 1:2], None, ALU.mult).then_inc(h_done, 1)

                def scale(t, b, i):
                    dve.wait_ge(hT_stored[b], 16 * i + 1)
                    dve.wait_ge(h_split, t + 1)
                    dve.wait_ge(products, 3 * t + 1)
                    for half in range(2):
                        dve.wait_ge(transposed, 2 * t + half + 5)
                        ks = slice(4 * half, 4 * half + 4)
                        nc.vector.tensor_tensor(hT[:, b, ks, :], t_ps[2 * b + half][:, :, :],
                                                gain[:, ks].unsqueeze(2).to_broadcast([P, 4, P]),
                                                ALU.mult).then_inc(hT_copied, 1)

                norm(0, 0)
                norm(1, 1)
                dve.wait_ge(params_in, 48)
                scale(0, 0, 0)
                for k in range(KD):
                    dve.wait_ge(w_leads, k + 1)
                    nc.vector.tensor_tensor(w_rest[:, k, :], w_raw[:, k % 3, :], w_lead[:, k, :].bitcast(F32),
                                            ALU.subtract).then_inc(w_split, 1)

                def body(t, b, i):
                    if i is not LOOP:
                        norm(t + 2, b)
                    if not (i is LOOP and b):
                        scale(t + 1, 1 - b, i + b)

                iterations(dve, body)
                dve.wait_ge(evacuated, 3 * NT + 6)
                ff_all = ff[:, :, :].rearrange("p t h -> p (t h)")
                own2 = Steps(nc.vector, own, base=NT)
                own2.then(nc.vector.tensor_tensor(ff[:, :, :], ff[:, :, :], b_f[:, :].unsqueeze(1).to_broadcast([P, NT, H]), ALU.add))
                own2.then(nc.vector.tensor_scalar(lf[:, 0, :], ff_all, -1.0, None, ALU.mult))
                nc.vector.tensor_tensor(lf[:, 1, :], lf[:, 0, :], ff_all, ALU.max).then_inc(logs, 1)
                dve.wait_ge(logs, 2)
                own2.do(nc.vector.tensor_scalar(lf[:, 0, :], ff_all, 0.0, None, ALU.min))
                nc.vector.tensor_scalar(lf[:, 2, :], lf[:, 2, :], 1.0, None, ALU.add).then_inc(logs, 1)
                dve.wait_ge(logs, 4)
                own2.join()
                nc.vector.tensor_tensor(lf[:, 0, :], lf[:, 0, :], lf[:, 3, :], ALU.subtract).then_inc(logs, 1)
                dve.wait_ge(summed, 1)
                cum_ps, tot_ps = (bank[:, 0:NT * H] for bank in vu_ps)
                own2.then(nc.vector.memset(total[:, 0, :], 0.0))
                for t in range(1, NT):
                    own2.then(nc.vector.tensor_tensor(total[:, t, :], total[:, t - 1, :],
                                                      tot_ps[:, (t - 1) * H:t * H], ALU.add))
                flat = total[:, :, :].rearrange("p t h -> p (t h)")
                lead, rest = (keep["cum"][:, :, :, n].rearrange("p t h -> p (t h)") for n in range(2))
                own2.then(nc.vector.tensor_tensor(flat, cum_ps, flat, ALU.add))
                own2.then(nc.vector.tensor_copy(cum_lead[:, :], flat))
                own2.do(nc.vector.tensor_copy(lead, cum_lead[:, :].bitcast(F32)))
                own2.then(nc.vector.tensor_tensor(rest, flat, cum_lead[:, :].bitcast(F32), ALU.subtract))

            @block.tensor
            def _(pe):
                pe.sem_inc(transposed, 4)
                pe.sem_inc(products, 6)

                def transposes(t, b):
                    pe.wait_ge(h_done, t + 1)
                    for half in range(2):
                        for k in range(4 * half, 4 * half + 4):
                            last = nc.tensor.transpose(t_ps[2 * b + half][:, k % 4, :], h[:, b, k * P:(k + 1) * P], ident[:, :])
                        last.then_inc(transposed, 1)

                pe.wait_ge(consts_set, 4)
                transposes(0, 0)
                pe.wait_ge(params_in, 48)

                def body(t, b, i):
                    if not (i is LOOP and b):
                        transposes(t + 1, 1 - b)
                    pe.wait_ge(hT_copied, 2 * t + 2)
                    pe.wait_ge(evacuated, 3 * t + 1)
                    for k in range(KD):
                        last = nc.tensor.matmul(ff_ps[b][:, 0:H], hT[:, b, k, :], w_ff[:, k, :],
                                                start=(k == 0), stop=(k == KD - 1))
                    last.then_inc(products, 1)
                    pe.wait_ge(h_split, t + 1 + 2)
                    pe.wait_ge(w_split, KD)
                    for n in range(2):
                        pe.wait_ge(evacuated, 3 * t + n + 2 + 3)
                        ns = slice(n * CH, (n + 1) * CH)
                        for k in range(KD):
                            nc.tensor.matmul(vu_ps[n][:, :], h_lead[:, b, k, :], w_rest[:, k, ns], start=k == 0, stop=False)
                            nc.tensor.matmul(vu_ps[n][:, :], h_lead[:, b, k, :], w_lead[:, k, ns], start=False, stop=False)
                            last = nc.tensor.matmul(vu_ps[n][:, :], h_rest[:, b, k, :], w_lead[:, k, ns],
                                                    start=False, stop=k == KD - 1)
                        last.then_inc(products, 1)

                iterations(pe, body)
                pe.wait_ge(evacuated, 3 * NT + 6)
                pe.wait_ge(logs, 5)
                nc.tensor.matmul(vu_ps[0][:, 0:NT * H], tri[:, :], lf[:, 0, :], start=True, stop=True)
                nc.tensor.matmul(vu_ps[1][:, 0:NT * H], ones[:, :], lf[:, 0, :], start=True, stop=True).then_inc(summed, 1)


def reduce_angle(nc, st, angle, k):
    st.then(nc.vector.tensor_scalar(k, angle, 1.0 / TWO_PI, MAGIC, ALU.mult, ALU.add))
    st.then(nc.vector.tensor_scalar(k, k, MAGIC, None, ALU.subtract))
    for part in (C1, C2, C3):
        st.then(nc.vector.scalar_tensor_tensor(out=angle, in0=k, scalar=-part, in1=angle,
                                               op0=ALU.mult, op1=ALU.add))
    st.then(nc.vector.tensor_scalar(angle, angle, PI_F32, -PI_F32, ALU.min, ALU.max))


def project(nc, a, keep):
    with ExitStack() as ctx:
        m = Mem(nc, ctx, "pr")
        wq = (keep["wq_lead"], keep["wq_rest"])
        wk = [m.sb(f"wk_{x}", [P, KD, WIDTH], F32R) for x in ("lead", "rest")]
        w_q_up = [m.sb(f"w_q_up_{x}", [P, 2, H * MQ], F32R) for x in ("lead", "rest")]
        w_kv_up = [m.sb(f"w_kv_up_{x}", [P, H * P], F32R) for x in ("lead", "rest")]
        w_raw = m.sb("w_raw", [P, 2, D])
        hT = m.sb("hT", [P, KD * P])
        h_lead = m.sb("h_lead", [P, KD, P], F32R)
        h_rest = m.sb("h_rest", [P, KD, P], F32R)
        lora = m.sb("lora", [P, 416])
        lora_n = m.sb("lora_n", [P, 384])
        loraT = m.sb("loraT", [P, 3, P])
        loraT_lead = m.sb("loraT_lead", [P, 3, P], F32R)
        loraT_rest = m.sb("loraT_rest", [P, 3, P], F32R)
        fox = m.sb("fox", [P, 2 * WIDTH])
        q_raw = m.sb("q_raw", [P, H * MQ])
        kv_raw = m.sb("kv_raw", [P, H * P])
        mv_out = m.sb("mv_out", [P, 2, WIDTH])
        junk = m.sb("junk", [P, 2 * WIDTH])
        rope = m.sb("rope", [P, 4, H * ROPE // 2])
        kpe = m.sb("kpe", [P, ROPE])
        fqk = m.sb("fqk", [P, 2 * H, FQ])
        mqk = m.sb("mqk", [P, 2 * H, MQ])
        gain_f = m.sb("gain_f", [FQ, 2])
        gain_m = m.sb("gain_m", [MQ, 2])
        gain_lora = m.sb("gain_lora", [P, 3])
        st_l = m.sb("st_l", [P, 7])
        st_f = m.sb("st_f", [P, 3, 2 * H])
        st_m = m.sb("st_m", [P, 3, 2 * H])
        stage_f = m.sb("stage_f", [FQ, 2, 2 * H, P])
        stage_m = m.sb("stage_m", [MQ, 2, 2 * H, P])
        pos_i = m.sb("pos_i", [P, NT], I32)
        pos = m.sb("pos", [P, NT])
        inv = m.sb("inv", [P, ROPE // 2])
        sin_t = m.sb("sin_t", [P, NT, ROPE // 2])
        cos_t = m.sb("cos_t", [P, NT, ROPE // 2])
        angle = m.sb("angle", [P, NT * ROPE // 2])
        turns = m.sb("turns", [P, NT * ROPE // 2])
        ident, cum = keep["ident"], keep["cum"]
        pj = [m.ps(f"pj{i}", [P, CH]) for i in range(5)]
        tp = [m.ps(f"tp{i}", [P, 4, P]) for i in range(3)]

        w_in = [m.sem(f"w_in{b}") for b in range(2)]
        w_leads = m.sem("w_leads")
        w_split = m.sem("w_split")
        small_in = m.sem("small_in")
        hT_in = m.sem("hT_in")
        h_leads = m.sem("h_leads")
        h_split = m.sem("h_split")
        h_used = m.sem("h_used")
        projected = m.sem("projected")
        evacuated = m.sem("evacuated")
        turned = m.sem("turned")
        turn_out = m.sem("turn_out")
        sums = m.sem("sums")
        roots = m.sem("roots")
        lora_ready = m.sem("lora_ready")
        lora_split = m.sem("lora_split")
        heads_ready = m.sem("heads_ready")
        raw_used = m.sem("raw_used")
        mv_ready = m.sem("mv_ready")
        stored_f, stored_m, stored_v = ([m.sem(f"stored_{x}{b}") for b in range(2)] for x in "fmv")
        tables = m.sem("tables")
        own = m.sem("own")
        tick = keep["tick"]
        FIRST = 0
        PJ, TP = 7, 9
        BANK = (0, 1, 2, 3, 4, 0, 1)
        LAST = [max(u for u in range(n - PJ, n) if BANK[u % PJ] == BANK[n]) for n in range(PJ)]

        def tiles(eng, body):
            body(FIRST, 0, 0)
            with eng.Fori(0, NT // 2 - 1) as i:
                body(2 * i + 1, 1, i)
                body(2 * i + 2, 0, i + 1)
            body(NT - 1, 1, NT // 2 - 1)

        pieces = [(a["w_fk"][:, k:k + 2, :], [w[:, k:k + 2, :] for w in wk], (2, WIDTH)) for k in range(0, KD, 2)]
        pieces += [(a["w_q_up"][:, k:k + 1, :], [w[:, k:k + 1, :] for w in w_q_up], (1, H * MQ)) for k in range(2)]
        pieces += [(a["w_kv_up"], [w[:, :] for w in w_kv_up], (H * P,))]

        def piece(n):
            shape = pieces[n][2]
            flat = w_raw[:, n % 2, 0:int(np.prod(shape))]
            return flat if len(shape) == 1 else flat.rearrange("p (k c) -> p k c", k=shape[0])

        with nc.Block() as block:
            @block.sync
            def _(sp):
                for b in range(2):
                    for sem in (stored_f, stored_m, stored_v):
                        sp.sem_inc(sem[b], 1)

                def store(names, src, tok, done):
                    for j, name in enumerate(names):
                        sp.dma_start(a[name][:, :, tok].rearrange("h d t -> d h t"), src[:, j * H:(j + 1) * H, :]).then_inc(done, 16)

                def heads(t, b):
                    tok = bass.ds((t - 1) * P, P)
                    wait_alone(sp, turn_out, TP * t + 5 + 3, tick)
                    store(("fqT", "fkT"), stage_f[:, b, :, :], tok, stored_f[b])
                    wait_alone(sp, turn_out, TP * t + TP + 3, tick)
                    store(("mqT", "mkT"), stage_m[:, b, :, :], tok, stored_m[b])

                def body(t, b, q):
                    if t is not FIRST:
                        heads(t, 1 - b)
                    wait_alone(sp, mv_ready, t + 1, tick)
                    sp.dma_start(a["mv"][t], mv_out[:, b, :]).then_inc(stored_v[b], 16)

                tiles(sp, body)
                heads(NT, 1)
                for b in range(2):
                    sp.wait_ge(stored_f[b], 32 * (NT // 2) + 1)
                    sp.wait_ge(stored_m[b], 32 * (NT // 2) + 1)
                    sp.wait_ge(stored_v[b], 16 * (NT // 2) + 1)

            @block.gpsimd
            def _(pool):
                def load(t):
                    pool.dma_start(hT[:, :], a["hT"][t]).then_inc(hT_in, 16)

                def load_w(n):
                    pool.dma_start(piece(n), pieces[n][0]).then_inc(w_in[n % 2], 16)

                load(0)
                for n in range(2):
                    load_w(n)
                pool.memset(gain_f[:, :], 1.0).then_inc(tables, 1)
                pool.memset(fqk[:, :, HD:FQ], 1.0).then_inc(tables, 1)
                pool.wait_ge(tables, 1)
                for dst, name in ((pos_i[:, :], "positions"), (inv[:, :], "inv_freq"), (gain_lora[:, :], "gain_lora"),
                                  (gain_f[0:HD, 0:1], "fox_q_norm"), (gain_f[0:HD, 1:2], "fox_k_norm"),
                                  (gain_m[:, 0:1], "mla_q_norm"), (gain_m[:, 1:2], "mla_k_norm")):
                    pool.dma_start(dst, a[name]).then_inc(small_in, 16)
                pool.sem_inc(h_used, 1)

                def split_h(t):
                    wait_alone(pool, hT_in, 16 * t + 16, tick)
                    wait_alone(pool, h_used, t + 1, tick)
                    whole = hT[:, :].rearrange("p (k t) -> p k t", t=P)
                    pool.tensor_scalar(h_lead[:, :, :], whole, 1.0, 0.0, ALU.mult, ALU.add).then_inc(h_leads, 1)
                    wait_alone(pool, h_leads, t + 1, tick)
                    pool.tensor_tensor(h_rest[:, :, :], whole, h_lead[:, :, :].bitcast(F32), ALU.subtract).then_inc(h_split, 1)

                split_h(0)
                pool.wait_ge(h_split, 1)
                load(1)
                for n in range(len(pieces)):
                    pool.wait_ge(w_leads, n + 1)
                    first, second = pieces[n][1]
                    pool.tensor_tensor(second, piece(n), first.bitcast(F32), ALU.subtract).then_inc(w_split, 1)
                    if n + 2 < len(pieces):
                        pool.wait_ge(w_split, n + 1)
                        load_w(n + 2)
                with pool.Fori(0, NT - 2) as i:
                    split_h(i + 1)
                    wait_alone(pool, h_split, i + 2, tick)
                    load(i + 2)
                split_h(NT - 1)

            @block.tensor
            def _(pe):
                def bank(t, n):
                    pe.wait_ge(evacuated, PJ * t + LAST[n] + 1 + PJ)
                    return pj[BANK[n]]

                def product(out, v, w, blocks):
                    for k in range(blocks):
                        nc.tensor.matmul(out, v[0](k), w[1](k), start=k == 0, stop=False)
                        nc.tensor.matmul(out, v[0](k), w[0](k), start=False, stop=False)
                        last = nc.tensor.matmul(out, v[1](k), w[0](k), start=False, stop=k == blocks - 1)
                    last.then_inc(projected, 1)

                def turn(t, n, blocks, rows):
                    pe.wait_ge(turn_out, TP * t + n + 1)
                    for j, src in enumerate(blocks):
                        last = nc.tensor.transpose(tp[n % 3][0:rows, j, :], src, ident[:, :])
                    last.then_inc(turned, 1)

                def turn_heads(t):
                    for n in range(4):
                        turn(t, 1 + n, [fqk[:, 4 * n + j, :] for j in range(4)], FQ)
                    for n in range(4):
                        turn(t, 5 + n, [mqk[:, 4 * n + j, :] for j in range(4)], MQ)

                h = [lambda k: h_lead[:, k, :], lambda k: h_rest[:, k, :]]

                def body(t, b, q):
                    pe.wait_ge(h_split, t + 1)
                    product(bank(t, 0)[:, 0:416], h, [lambda k, w=w: w[:, k, 0:416] for w in wq], KD)
                    product(bank(t, 1)[:, :], h, [lambda k, w=w: w[:, k, 416:LQ] for w in wq], KD)
                    if t is FIRST:
                        pe.wait_ge(w_split, KD // 2)
                    product(bank(t, 2)[:, :], h, [lambda k, w=w: w[:, k, :] for w in wk], KD)
                    pe.wait_ge(lora_ready, t + 1)
                    turn(t, 0, [lora_n[:, j * P:(j + 1) * P] for j in range(3)], P)
                    if t is FIRST:
                        pe.wait_ge(turned, 1)
                        pe.sem_inc(turned, TP - 1)
                    else:
                        pe.wait_ge(heads_ready, 2 * t)
                        turn_heads(t)
                    pe.wait_ge(projected, PJ * t + 3)
                    pe.sem_inc(h_used, 1)
                    pe.wait_ge(lora_split, t + 1)
                    if t is FIRST:
                        pe.wait_ge(w_split, len(pieces))
                    for n, (lo, hi) in enumerate(((0, CH), (CH, H * MQ))):
                        product(bank(t, 3 + n)[:, 0:hi - lo], [lambda k, x=x: x[:, k, :] for x in (loraT_lead, loraT_rest)],
                                [lambda k, w=w: w[:, k, lo:hi] for w in w_q_up], 2)
                    for n, lo in enumerate((0, CH)):
                        product(bank(t, 5 + n)[:, :], [lambda k, x=x: x[:, 2, :] for x in (loraT_lead, loraT_rest)],
                                [lambda k, w=w: w[:, lo:lo + CH] for w in w_kv_up], 1)

                tiles(pe, body)
                pe.wait_ge(heads_ready, 2 * NT)
                pe.wait_ge(turned, TP * NT)
                pe.sem_inc(turned, 1)
                turn_heads(NT)

            @block.scalar
            def _(act):
                act.wait_ge(tables, 3)
                nc.scalar.activation(sin_t[:, :, :].rearrange("p t f -> p (t f)"), angle[:, :], ACT.Sin).then_inc(tables, 1)
                nc.scalar.activation(cos_t[:, :, :].rearrange("p t f -> p (t f)"), angle[:, :], ACT.Sin,
                                     scale=0.5).then_inc(tables, 1)
                act.sem_inc(evacuated, PJ)
                for n, (src, parts, shape) in enumerate(pieces):
                    act.wait_ge(w_in[n % 2], 16 * (n // 2) + 16)
                    nc.scalar.activation(parts[0], piece(n), ACT.Copy).then_inc(w_leads, 1)

                def body(t, b, q):
                    use = [0]

                    def evacuate(dst, width):
                        n = use[0]
                        use[0] += 1
                        act.wait_ge(projected, PJ * t + n + 1)
                        nc.scalar.activation(dst, pj[BANK[n]][:, 0:width], ACT.Copy).then_inc(evacuated, 1)

                    def root(st, n):
                        act.wait_ge(sums, 3 * t + n + 1)
                        nc.scalar.activation(st[1], st[0], ACT.Sqrt).then_inc(roots, 1)

                    act.wait_ge(raw_used, 3 * t + 1)
                    evacuate(lora[:, :], 416)
                    root((st_l[:, 2:4], st_l[:, 4:6]), 0)
                    act.wait_ge(raw_used, 3 * t + 2)
                    evacuate(fox[:, 0:WIDTH], WIDTH)
                    evacuate(fox[:, WIDTH:], WIDTH)
                    act.wait_ge(raw_used, 3 * t + 3)
                    root((st_f[:, 1, :], st_f[:, 2, :]), 1)
                    evacuate(q_raw[:, 0:CH], CH)
                    evacuate(q_raw[:, CH:], H * MQ - CH)
                    evacuate(kv_raw[:, 0:CH], CH)
                    evacuate(kv_raw[:, CH:], CH)
                    root((st_m[:, 1, :], st_m[:, 2, :]), 2)

                tiles(act, body)

            @block.vector
            def _(dve):
                st = Steps(nc.vector, own)
                dve.wait_ge(small_in, 16 * 7)
                dve.wait_ge(tables, 2)
                st.do(nc.vector.memset(fqk[:, 0:H, HD:HD + 1], 0.0))
                st.do(nc.vector.tensor_scalar(gain_f[0:HD, 0:1], gain_f[0:HD, 0:1], HD ** -0.5, None, ALU.mult))
                st.do(nc.vector.tensor_scalar(gain_m[:, 0:1], gain_m[:, 0:1], MQ ** -0.5, None, ALU.mult))
                st.then(nc.vector.tensor_copy(pos[:, :], pos_i[:, :]))
                st.then(nc.vector.tensor_tensor(
                    angle[:, :].rearrange("p (t f) -> p t f", t=NT), pos[:, :].unsqueeze(2).to_broadcast([P, NT, ROPE // 2]),
                    inv[:, :].unsqueeze(1).to_broadcast([P, NT, ROPE // 2]), ALU.mult))
                reduce_angle(nc, st, angle[:, :], turns[:, :])
                dve.sem_inc(tables, 1)
                dve.wait_ge(tables, 5)
                cos_flat = cos_t[:, :, :].rearrange("p t f -> p (t f)")
                st.then(nc.vector.tensor_tensor(cos_flat, cos_flat, cos_flat, ALU.mult))
                st.then(nc.vector.tensor_scalar(cos_flat, cos_flat, -2.0, 1.0, ALU.mult, ALU.add))
                before = st.n
                per_tile = 33
                dve.sem_inc(raw_used, 3)
                dve.sem_inc(turn_out, 3)

                def turn_to(t, n, dst, gain, rows):
                    dve.wait_ge(turned, TP * t + n + 1)
                    nc.vector.tensor_scalar(dst, tp[n % 3][0:rows, :, :], gain, None, ALU.mult).then_inc(turn_out, 1)

                def heads_out(t, b, q):
                    dve.wait_ge(stored_f[b], 32 * q + 1)
                    for n in range(4):
                        turn_to(t, 1 + n, stage_f[:, b, 4 * n:4 * n + 4, :], gain_f[:, n // 2:n // 2 + 1], FQ)
                    dve.wait_ge(stored_m[b], 32 * q + 1)
                    for n in range(4):
                        turn_to(t, 5 + n, stage_m[:, b, 4 * n:4 * n + 4, :], gain_m[:, n // 2:n // 2 + 1], MQ)

                def body(t, b, q):
                    st = Steps(nc.vector, own, base=t * per_tile + before)

                    def arrived(n):
                        dve.wait_ge(evacuated, PJ * (t + 1) + n + 1)

                    def sum_squares(lo, hi, out):
                        st.do(nc.vector.tensor_tensor_reduce(out=junk[:, lo:hi], in0=lora[:, lo:hi], in1=lora[:, lo:hi],
                                                             scale=1.0, scalar=0.0, op0=ALU.mult, op1=ALU.add,
                                                             accum_out=out))

                    arrived(0)
                    sum_squares(0, Q_RANK, st_l[:, 0:1])
                    sum_squares(Q_RANK, 384, st_l[:, 1:2])
                    sum_squares(384, 416, st_l[:, 6:7])
                    st.join()
                    st.do(nc.vector.tensor_scalar(st_l[:, 2:3], st_l[:, 0:1], 1.0 / Q_RANK, EPS, ALU.mult, ALU.add))
                    nc.vector.tensor_scalar(st_l[:, 3:4], st_l[:, 1:2], 1.0 / KV_RANK, EPS,
                                            ALU.mult, ALU.add).then_inc(sums, 1)
                    dve.wait_ge(roots, 3 * t + 1)
                    st.then(nc.vector.reciprocal(st_l[:, 4:6], st_l[:, 4:6]))
                    st.do(nc.vector.tensor_scalar(lora_n[:, 0:Q_RANK], lora[:, 0:Q_RANK], st_l[:, 4:5], None, ALU.mult))
                    nc.vector.tensor_scalar(lora_n[:, Q_RANK:], lora[:, Q_RANK:384], st_l[:, 5:6], None,
                                            ALU.mult).then_inc(lora_ready, 1)
                    dve.wait_ge(turned, TP * t + 1)
                    nc.vector.tensor_tensor(loraT[:, :, :], tp[0][:, 0:3, :],
                                            gain_lora[:, :].unsqueeze(2).to_broadcast([P, 3, P]),
                                            ALU.mult).then_inc(turn_out, 1)
                    dve.wait_ge(turn_out, TP * t + 1 + 3)
                    st.then(nc.vector.tensor_copy(loraT_lead[:, :, :], loraT[:, :, :]))
                    nc.vector.tensor_tensor(loraT_rest[:, :, :], loraT[:, :, :], loraT_lead[:, :, :].bitcast(F32),
                                            ALU.subtract).then_inc(lora_split, 1)
                    cos1, sin1 = cos_t[:, t, :], sin_t[:, t, :]
                    half = ROPE // 2
                    x1, x2 = lora[:, 384:384 + half], lora[:, 384 + half:416]
                    for j, (x, w) in enumerate(((x1, cos1), (x2, sin1), (x1, sin1), (x2, cos1))):
                        st.do(nc.vector.tensor_tensor(rope[:, j, 0:half], x, w, ALU.mult))
                    st.join()
                    st.do(nc.vector.tensor_tensor(kpe[:, 0:half], rope[:, 0, 0:half], rope[:, 1, 0:half], ALU.subtract))
                    st.do(nc.vector.tensor_tensor(kpe[:, half:], rope[:, 2, 0:half], rope[:, 3, 0:half], ALU.add))
                    st.join()
                    dve.sem_inc(raw_used, 1)
                    if t is FIRST:
                        dve.sem_inc(turn_out, TP - 1)
                    else:
                        heads_out(t, 1 - b, q if b else q - 1)
                    arrived(2)
                    st.then(nc.vector.tensor_tensor(junk[:, :], fox[:, :], fox[:, :], ALU.mult))
                    st.then(nc.vector.tensor_reduce(st_f[:, 0, :], junk[:, :].rearrange("p (h d) -> p h d", d=HD),
                                                    AX.X, ALU.add))
                    nc.vector.tensor_scalar(st_f[:, 1, :], st_f[:, 0, :], 1.0 / HD, EPS, ALU.mult, ALU.add).then_inc(sums, 1)
                    dve.wait_ge(roots, 3 * t + 2)
                    st.then(nc.vector.reciprocal(st_f[:, 2, :], st_f[:, 2, :]))
                    st.do(nc.vector.tensor_tensor(fqk[:, :, 0:HD], fox[:, :].rearrange("p (h d) -> p h d", d=HD),
                                                  st_f[:, 2, :].unsqueeze(2).to_broadcast([P, 2 * H, HD]), ALU.mult))
                    st.do(nc.vector.tensor_copy(fqk[:, 0:H, HD + 3:FQ], cum[:, t, :, :]))
                    nc.vector.tensor_scalar(fqk[:, H:2 * H, HD + 1:HD + 3], cum[:, t, :, :], -1.0, None,
                                            ALU.mult).then_inc(heads_ready, 1)
                    dve.wait_ge(heads_ready, 2 * t + 1)
                    st.join()
                    dve.sem_inc(raw_used, 1)
                    arrived(6)
                    q3 = q_raw[:, :].rearrange("p (h d) -> p h d", d=MQ)
                    kv3 = kv_raw[:, :].rearrange("p (h d) -> p h d", d=P)
                    st.then(nc.vector.tensor_tensor(junk[:, 0:H * MQ], q_raw[:, :], q_raw[:, :], ALU.mult))
                    st.then(nc.vector.tensor_reduce(st_m[:, 0, 0:H], junk[:, 0:H * MQ].rearrange("p (h d) -> p h d", d=MQ),
                                                    AX.X, ALU.add))
                    jk = junk[:, 0:WIDTH].rearrange("p (h d) -> p h d", d=NOPE)
                    st.then(nc.vector.tensor_tensor(jk, kv3[:, :, 0:NOPE], kv3[:, :, 0:NOPE], ALU.mult))
                    st.then(nc.vector.tensor_reduce(st_m[:, 0, H:], jk, AX.X, ALU.add))
                    st.then(nc.vector.tensor_scalar(st_m[:, 0, H:], st_m[:, 0, H:], st_l[:, 6:7], None, ALU.add))
                    nc.vector.tensor_scalar(st_m[:, 1, :], st_m[:, 0, :], 1.0 / MQ, EPS, ALU.mult, ALU.add).then_inc(sums, 1)
                    cosb = cos1.unsqueeze(1).to_broadcast([P, H, half])
                    sinb = sin1.unsqueeze(1).to_broadcast([P, H, half])
                    r3 = [rope[:, j, :].rearrange("p (h d) -> p h d", d=half) for j in range(4)]
                    x1, x2 = q3[:, :, NOPE:NOPE + half], q3[:, :, NOPE + half:]
                    for j, (x, w) in enumerate(((x1, cosb), (x2, sinb), (x1, sinb), (x2, cosb))):
                        st.do(nc.vector.tensor_tensor(r3[j], x, w, ALU.mult))
                    st.join()
                    st.do(nc.vector.tensor_tensor(x1, r3[0], r3[1], ALU.subtract))
                    st.do(nc.vector.tensor_tensor(x2, r3[2], r3[3], ALU.add))
                    dve.wait_ge(roots, 3 * t + 3)
                    st.then(nc.vector.reciprocal(st_m[:, 2, :], st_m[:, 2, :]))
                    st.do(nc.vector.tensor_tensor(mqk[:, 0:H, :], q3,
                                                  st_m[:, 2, 0:H].unsqueeze(2).to_broadcast([P, H, MQ]), ALU.mult))
                    st.do(nc.vector.tensor_tensor(mqk[:, H:, 0:NOPE], kv3[:, :, 0:NOPE],
                                                  st_m[:, 2, H:].unsqueeze(2).to_broadcast([P, H, NOPE]), ALU.mult))
                    st.do(nc.vector.tensor_tensor(mqk[:, H:, NOPE:], kpe[:, :].unsqueeze(1).to_broadcast([P, H, ROPE]),
                                                  st_m[:, 2, H:].unsqueeze(2).to_broadcast([P, H, ROPE]), ALU.mult))
                    dve.wait_ge(stored_v[b], 16 * q + 1)
                    nc.vector.tensor_copy(mv_out[:, b, :].rearrange("p (h d) -> p h d", d=HD),
                                          kv3[:, :, NOPE:]).then_inc(mv_ready, 1)
                    st.join()
                    dve.sem_inc(heads_ready, 1)
                    dve.wait_ge(mv_ready, t + 1)
                    dve.sem_inc(raw_used, 1)
                    assert st.n == per_tile, st.n

                tiles(dve, body)
                dve.wait_ge(turn_out, TP * NT + 3)
                dve.sem_inc(turn_out, 1)
                heads_out(NT, 1, NT // 2 - 1)


def attend(nc, a, keep):
    G = 4
    NG = NT // G
    RING = 5
    with ExitStack() as ctx:
        m = Mem(nc, ctx, "at")
        widths = (MQ + 1, FQ)
        max_row = (MQ, HD)
        raw = [[m.sb(f"raw_{n}{x}", [widths[x], S]) for n in "qk"] for x in range(2)]
        lead = [[m.sb(f"lead_{n}{x}", [widths[x], S], F32R) for n in "qk"] for x in range(2)]
        rest = [[m.sb(f"rest_{n}{x}", [widths[x], S], F32R) for n in "qk"] for x in range(2)]
        v_raw = [m.sb(f"v_raw{x}", [P, NT, HD]) for x in range(2)]
        v_lead = [m.sb(f"v_lead{x}", [P, NT, 2 * HD], F32R) for x in range(2)]
        v_rest = [m.sb(f"v_rest{x}", [P, NT, 2 * HD], F32R) for x in range(2)]
        y = [m.sb(f"y{x}", [HD + 1, S]) for x in range(2)]
        sums = [m.sb(f"sums{x}", [P, S // P]) for x in range(2)]
        inv = [m.sb(f"inv{x}", [P, S // P]) for x in range(2)]
        inv_all = m.sb("inv_all", [HD, S])
        probs = m.sb("probs", [P, RING, CH])
        p_lead = m.sb("p_lead", [P, RING, CH], F32R)
        p_rest = m.sb("p_rest", [P, RING, CH], F32R)
        chunk_max = m.sb("chunk_max", [P, 2, G, NG])
        neg_max = m.sb("neg_max", [P, 2, G], F32R)
        ident_r = m.sb("ident_r", [P, P], F32R)
        ident_b = m.sb("ident_b", [P, P], BF16)
        mask = [m.sb(f"mask{x}", [P, P], BF16) for x in range(2)]
        maskT = [m.sb(f"maskT{x}", [P, P], BF16) for x in range(2)]
        s_ps = [m.ps(f"s{i}", [P, CH]) for i in range(2)]
        st_ps = [m.ps(f"st{i}", [P, CH]) for i in range(4)]
        o_ps = [m.ps(f"o{i}", [P, CH]) for i in range(2)]

        raw_in = [m.sem(f"raw_in{x}") for x in range(2)]
        raw_used = [m.sem(f"raw_used{x}") for x in range(2)]
        split = [m.sem(f"split{x}") for x in range(2)]
        head_used = [m.sem(f"head_used{x}") for x in range(2)]
        y_done = m.sem("y_done")
        in_dram = m.sem("in_dram")
        sums_in = [m.sem(f"sums_in{x}") for x in range(2)]
        inverted = [m.sem(f"inverted{x}") for x in range(2)]
        inv_in = m.sem("inv_in")
        normalised = m.sem("normalised")
        y_stored = [m.sem(f"y_stored{x}") for x in range(2)]
        masks_set = m.sem("masks_set")
        scored = m.sem("scored")
        score_out = m.sem("score_out")
        max_ready = m.sem("max_ready")
        scoredT = m.sem("scoredT")
        exped = m.sem("exped")
        lead_ready = m.sem("lead_ready")
        rest_ready = m.sem("rest_ready")
        weighted = m.sem("weighted")
        own = m.sem("own")
        tick = keep["tick"]

        steps = [(x, g) for x in range(2) for g in range(NG)]
        order = []

        ROW_AHEAD = 2

        def max_jobs(n):
            return [("max", n, r, c) for r in range(G) for c in range(steps[n][1] + 1)] + [("row", n, 0, 0)]

        blocks = [(n, kt) for n, (x, g) in enumerate(steps) for kt in range(G * (g + 1))]
        LAG = 4
        for b in range(len(blocks) + LAG):
            if b < len(blocks):
                n, kt = blocks[b]
                KT = G * (steps[n][1] + 1)
                order.append(("score", n, kt, 0))
                ahead = max_jobs((n + 1) % len(steps))
                jobs = len(ahead) - 1
                at = [-(-jobs * min(k, KT - 2) // (KT - 2)) for k in (kt, kt + 1)]
                order += ahead[at[0]:at[1]]
                if kt == KT - ROW_AHEAD:
                    order.append(ahead[-1])
            if 1 <= b <= len(blocks):
                order.append(("rest", *blocks[b - 1], 0))
            if b >= LAG:
                order.append(("weigh", *blocks[b - LAG], 0))
        S_USES = sum(o[0] in ("max", "row") for o in order)
        ST_USES = sum(o[0] == "score" for o in order)
        assert S_USES % 2 == 0 and ST_USES % 4 == 0 and ST_USES % RING == 0
        s_jobs = [o for o in order if o[0] in ("max", "row")]
        row_done = {o[1]: s_jobs.index(o) + 1 for o in s_jobs if o[0] == "row"}
        row_done[0] -= S_USES
        S_FIRST = len(max_jobs(0))

        PARTS = 10

        def block(n, kt):
            g = steps[n][1]
            lo = max(kt, G * g) - G * g
            return lo, G - lo

        with nc.Block() as program:
            @program.sync
            def _(sp):
                def load(i, x):
                    wait_alone(sp, raw_used[x], i + 1, tick)
                    for t, name in zip(raw[x], (("mqT", "mkT"), ("fqT", "fkT"))[x]):
                        rows = (MQ, FQ)[x]
                        sp.dma_start(t[0:rows, :], a[name][i]).then_inc(raw_in[x], 16)
                    sp.dma_start(v_raw[x][:, :, :], a[("mv", "fv")[x]][:, :, bass.ds(i * HD, HD)].rearrange("t p d -> p t d")).then_inc(raw_in[x], 16)

                def sums_of(i, x):
                    wait_alone(sp, y_done, len(steps) * i + NG * (x + 1) + 2, tick)
                    sp.dma_start(a["row_sum"][x, i], y[x][HD:HD + 1, :]).then_inc(in_dram, 16)

                def store(i, x):
                    wait_alone(sp, in_dram, 32 * (2 * i + x) + 16, tick)
                    if x == 1:
                        wait_alone(sp, inverted[1], i + 1, tick)
                    sp.dma_start(sums[x][:, :], a["row_sum"][x, i].rearrange("r (p c) -> (r p) c", p=P)).then_inc(sums_in[x], 16)
                    wait_alone(sp, inverted[x], i + 1 + x, tick)
                    sp.dma_start(a["row_inv"][x, i].rearrange("r (p c) -> (r p) c", p=P), inv[x][:, :]).then_inc(in_dram, 16)
                    wait_alone(sp, in_dram, 32 * (2 * i + x) + 32, tick)
                    wait_alone(sp, normalised, 2 * i + x + 1, tick)
                    sp.dma_start(inv_all[:, :], a["row_inv"][x, i].to_broadcast([HD, S])).then_inc(inv_in, 16)
                    wait_alone(sp, normalised, 2 * i + x + 2, tick)
                    sp.dma_start(a["yT"][x, i], y[x][0:HD, :]).then_inc(y_stored[x], 16)

                for x in range(2):
                    sp.sem_inc(y_stored[x], 1)
                sp.wait_ge(masks_set, 16)
                for x in range(2):
                    load(0, x)
                with sp.Fori(0, H - 1) as i:
                    for x in range(2):
                        sums_of(i, x)
                        load(i + 1, x)
                        store(i, x)
                for x in range(2):
                    sums_of(H - 1, x)
                    store(H - 1, x)
                for x in range(2):
                    sp.wait_ge(y_stored[x], 16 * H + 1)

            @program.gpsimd
            def _(pool):
                for x in range(2):
                    pool.sem_inc(raw_used[x], 1)
                pool.memset(ident_b[:, :], 0.0).then_inc(masks_set, 1)
                for x in range(2):
                    pool.memset(mask[x][:, :], 0.0).then_inc(masks_set, 1)
                    pool.memset(maskT[x][:, :], 0.0).then_inc(masks_set, 1)
                    any_finite = keep["ident"][:, 0:HD].unsqueeze(1).to_broadcast([P, NT, HD])
                    pool.tensor_scalar(v_lead[x][:, :, HD:], any_finite, 0.0, 1.0, ALU.mult, ALU.add).then_inc(masks_set, 1)
                    pool.tensor_scalar(v_rest[x][:, :, HD:], any_finite, 0.0, 0.0, ALU.mult, ALU.add).then_inc(masks_set, 1)
                pool.wait_ge(masks_set, 9)
                pool.memset(raw[0][0][MQ:MQ + 1, :], 0.0).then_inc(masks_set, 1)
                pool.wait_ge(masks_set, 10)
                pool.memset(raw[0][1][MQ:MQ + 1, :], 1.0).then_inc(masks_set, 1)
                pool.wait_ge(masks_set, 11)
                pool.affine_select(out=ident_b[:, :], in_=ident_b[:, :], compare_op=ALU.not_equal, fill=1.0,
                                   base=0, pattern=[[-1, P]], channel_multiplier=1).then_inc(masks_set, 1)
                pool.wait_ge(masks_set, 12)
                pool.memset(mask[0][0:P // 2, P // 2:P], MASKED).then_inc(masks_set, 1)
                pool.wait_ge(masks_set, 13)
                pool.memset(maskT[0][P // 2:P, 0:P // 2], MASKED).then_inc(masks_set, 1)
                pool.wait_ge(masks_set, 14)
                pool.affine_select(out=mask[1][:, :], in_=mask[1][:, :], compare_op=ALU.is_ge, fill=MASKED,
                                   base=0, pattern=[[-1, P]], channel_multiplier=1).then_inc(masks_set, 1)
                pool.affine_select(out=maskT[1][:, :], in_=maskT[1][:, :], compare_op=ALU.is_ge, fill=MASKED,
                                   base=0, pattern=[[1, P]], channel_multiplier=-1).then_inc(masks_set, 1)
                def split_head(i, x):
                    wait_alone(pool, raw_in[x], 48 * i + 48, tick)
                    wait_alone(pool, head_used[x], i + 1, tick)
                    parts = [(raw[x][n][:, c:c + CH], lead[x][n][:, c:c + CH], rest[x][n][:, c:c + CH])
                             for n in range(2) for c in range(0, S, CH)]
                    parts += [(v_raw[x][:, c:c + 8, :], v_lead[x][:, c:c + 8, 0:HD], v_rest[x][:, c:c + 8, 0:HD])
                              for c in range(0, NT, 8)]
                    assert len(parts) == PARTS
                    for whole, first, second in parts:
                        pool.tensor_scalar(first, whole, 1.0, 0.0, ALU.mult, ALU.add).then_inc(split[x], 1)
                    wait_alone(pool, split[x], 2 * PARTS * i + PARTS, tick)
                    for whole, first, second in parts:
                        pool.tensor_tensor(second, whole, first.bitcast(F32), ALU.subtract).then_inc(split[x], 1)
                    wait_alone(pool, split[x], 2 * PARTS * (i + 1), tick)
                    pool.sem_inc(raw_used[x], 1)

                def normalise(i, x):
                    wait_alone(pool, inv_in, 16 * (2 * i + x + 1), tick)
                    pool.tensor_tensor(y[x][0:HD, :], y[x][0:HD, :], inv_all[:, :], ALU.mult).then_inc(normalised, 1)

                pool.sem_inc(normalised, 1)
                for x in range(2):
                    split_head(0, x)
                with pool.Fori(0, H - 1) as i:
                    for x in range(2):
                        split_head(i + 1, x)
                        normalise(i, x)
                pool.sem_inc(split[0], 2 * PARTS)
                for x in range(2):
                    normalise(H - 1, x)

            @program.tensor
            def _(pe):
                pe.sem_inc(weighted, RING)
                for x in range(2):
                    pe.sem_inc(head_used[x], 1)
                pe.wait_ge(masks_set, 18)
                def maximum(head, n, r, c, at):
                    x, g = steps[n]
                    t, lo = G * g + r, G * c
                    hi = min(lo + 4, t + 1)
                    if g == 0 and r == 0:
                        pe.wait_ge(split[x], 2 * PARTS * head + PARTS)
                    pe.wait_ge(score_out, at[0] + 1)
                    bank = s_ps[at[1] % 2]
                    diagonal = hi == t + 1
                    last = nc.tensor.matmul(bank[:, 0:(hi - lo) * P], lead[x][0][:, t * P:(t + 1) * P],
                                            lead[x][1][:, lo * P:hi * P], start=True, stop=not diagonal)
                    if diagonal:
                        last = nc.tensor.matmul(bank[:, (t - lo) * P:(hi - lo) * P], ident_b[:, :], mask[x][:, :],
                                                start=False, stop=True)
                    last.then_inc(scored, 1)

                def row(step_number, n, at):
                    pe.wait_ge(score_out, at[0] + 1)
                    pe.wait_ge(max_ready, G * step_number + G)
                    for r in range(G):
                        last = nc.tensor.matmul(s_ps[at[1] % 2][:, r * P:(r + 1) * P],
                                                neg_max[:, n % 2, r:r + 1].to_broadcast([P, P]), ident_r[:, :],
                                                start=True, stop=True)
                    last.then_inc(scored, 1)

                for n_s, (kind, n, p1, p2) in enumerate(max_jobs(0)):
                    if kind == "max":
                        maximum(0, n, p1, p2, (n_s, n_s))
                    else:
                        row(0, n, (n_s, n_s))
                with pe.Fori(0, H) as i:
                    n_s, n_st, n_w = S_FIRST, 0, 0
                    for kind, n, p1, p2 in order:
                        x, g = steps[n]
                        (q_lead, k_lead), (q_rest, k_rest) = lead[x], rest[x]
                        if kind == "max":
                            maximum(i + (1 if n == 0 else 0), n, p1, p2, (S_USES * i + n_s, n_s))
                            n_s += 1
                        elif kind == "row":
                            row(len(steps) * (i + (1 if n == 0 else 0)) + n, n, (S_USES * i + n_s, n_s))
                            n_s += 1
                        elif kind == "score":
                            kt = p1
                            lo, width = block(n, kt)
                            if g == 0 and kt == 0:
                                pe.wait_ge(split[x], 2 * PARTS * (i + 1))
                            if kt == 0:
                                pe.wait_ge(score_out, S_USES * i + S_FIRST + row_done[n] + 2)
                            pe.wait_ge(exped, ST_USES * i + n_st + 1)
                            bank = st_ps[n_st % 4][:, 0:width * P]
                            ks = slice(kt * P, (kt + 1) * P)
                            qs = slice((G * g + lo) * P, (G * g + G) * P)
                            nc.tensor.matmul(bank, k_lead[:, ks], q_rest[:, qs], start=True, stop=False)
                            nc.tensor.matmul(bank, k_rest[:, ks], q_lead[:, qs], start=False, stop=False)
                            diagonal = kt >= G * g
                            last = nc.tensor.matmul(bank, k_lead[:, ks], q_lead[:, qs], start=False, stop=not diagonal)
                            if diagonal:
                                last = nc.tensor.matmul(st_ps[n_st % 4][:, 0:P], ident_b[:, :], maskT[x][:, :],
                                                        start=False, stop=True)
                            last.then_inc(scoredT, 1)
                            n_st += 1
                        elif kind == "weigh":
                            kt = p1
                            lo, width = block(n, kt)
                            pe.wait_ge(rest_ready, ST_USES * i + n_w + 1)
                            if kt == 0:
                                pe.wait_ge(y_done, len(steps) * i + n + 1)
                            out = o_ps[n % 2][:, lo * P:CH]
                            ws = slice(0, width * P)
                            last_kt = kt == G * g + G - 1
                            nc.tensor.matmul(out, v_rest[x][:, kt, :], p_lead[:, n_w % RING, ws], start=kt == 0, stop=False)
                            nc.tensor.matmul(out, v_lead[x][:, kt, :], p_rest[:, n_w % RING, ws], start=False, stop=False)
                            last = nc.tensor.matmul(out, v_lead[x][:, kt, :], p_lead[:, n_w % RING, ws], start=False, stop=last_kt)
                            last.then_inc(weighted, 1)
                            n_w += 1
                            if g == NG - 1 and kt == NT - 1:
                                pe.wait_ge(weighted, ST_USES * i + n_w + RING)
                                pe.sem_inc(head_used[x], 1)

            @program.scalar
            def _(act):
                act.sem_inc(exped, 4)
                with act.Fori(0, H) as i:
                    def lead_of(b):
                        width = block(*blocks[b])[1] * P
                        act.wait_ge(exped, ST_USES * i + b + 1 + 4)
                        nc.scalar.activation(p_lead[:, b % RING, 0:width], probs[:, b % RING, 0:width], ACT.Copy).then_inc(lead_ready, 1)

                    for b, (n, kt) in enumerate(blocks):
                        width = block(n, kt)[1] * P
                        act.wait_ge(scoredT, ST_USES * i + b + 1)
                        act.wait_ge(weighted, ST_USES * i + b + 1)
                        nc.scalar.activation(probs[:, b % RING, 0:width], st_ps[b % 4][:, 0:width], ACT.Exp).then_inc(exped, 1)
                        if b >= 1:
                            lead_of(b - 1)
                    lead_of(len(blocks) - 1)

            @program.vector
            def _(dve):
                dve.sem_inc(score_out, 2)
                dve.sem_inc(y_done, 2)
                dve.sem_inc(sums_in[1], 1)
                dve.wait_ge(masks_set, 16)
                nc.vector.tensor_copy(ident_r[:, :], keep["ident"][:, :]).then_inc(masks_set, 1)
                nc.vector.memset(sums[1][:, :], 1.0).then_inc(masks_set, 1)
                dve.wait_ge(masks_set, 18)
                def maximum(n, r, c, at):
                    g = steps[n][1]
                    t, lo = G * g + r, G * c
                    hi = min(lo + 4, t + 1)
                    dve.wait_ge(scored, at[0] + 1)
                    nc.vector.tensor_reduce(chunk_max[:, n % 2, r, c:c + 1], s_ps[at[1] % 2][:, 0:(hi - lo) * P],
                                            AX.X, ALU.max).then_inc(score_out, 1)
                    if hi == t + 1:
                        dve.wait_ge(score_out, at[0] + 1 + 2)
                        nc.vector.tensor_reduce(neg_max[:, n % 2, r:r + 1], chunk_max[:, n % 2, r, 0:g + 1],
                                                AX.X, ALU.max, negate=True).then_inc(max_ready, 1)

                def row_to_q(head, n, at):
                    x, g = steps[n]
                    dve.wait_ge(scored, at[0] + 1)
                    if g == 0:
                        dve.wait_ge(split[x], 2 * PARTS * (head + 1))
                    rows = slice(max_row[x], max_row[x] + 1)
                    nc.vector.tensor_copy(lead[x][0][rows, g * CH:(g + 1) * CH], s_ps[at[1] % 2][rows, :]).then_inc(score_out, 1)

                def invert(x, value):
                    dve.wait_ge(sums_in[x], value)
                    nc.vector.reciprocal(inv[x][:, :], sums[x][:, :]).then_inc(inverted[x], 1)

                for n_s, (kind, n, p1, p2) in enumerate(max_jobs(0)):
                    if kind == "max":
                        maximum(n, p1, p2, (n_s, n_s))
                    else:
                        row_to_q(0, n, (n_s, n_s))
                with dve.Fori(0, H) as i:
                    n_s, n_w, n_r = S_FIRST, 0, 0
                    for kind, n, p1, p2 in order:
                        x, g = steps[n]
                        if kind == "max":
                            maximum(n, p1, p2, (S_USES * i + n_s, n_s))
                            n_s += 1
                        elif kind == "row":
                            row_to_q(i + (1 if n == 0 else 0), n, (S_USES * i + n_s, n_s))
                            n_s += 1
                        elif kind == "rest":
                            width = block(n, p1)[1] * P
                            dve.wait_ge(lead_ready, ST_USES * i + n_r + 1)
                            nc.vector.tensor_tensor(p_rest[:, n_r % RING, 0:width], probs[:, n_r % RING, 0:width],
                                                    p_lead[:, n_r % RING, 0:width].bitcast(F32), ALU.subtract).then_inc(rest_ready, 1)
                            n_r += 1
                            if (n, p1) == (2, 8):
                                invert(1, 16 * i + 1)
                            if (n, p1) == (6, 8):
                                invert(0, 16 * i + 16)
                        elif kind == "weigh":
                            n_w += 1
                            if p1 == G * (g + 1) - 1:
                                b = n % 2
                                dve.wait_ge(weighted, ST_USES * i + n_w + RING)
                                if g == 0:
                                    dve.wait_ge(y_stored[x], 16 * i + 1)
                                nc.vector.tensor_copy(y[x][:, g * CH:(g + 1) * CH], o_ps[b][0:HD + 1, :]).then_inc(y_done, 1)
                invert(1, 16 * H + 1)


def s5(nc, a, keep):
    TC = NC_ + 1
    with ExitStack() as ctx:
        m = Mem(nc, ctx, "s5")
        lr = m.sb("lr", [P, GROUPS])
        li = m.sb("li", [P, GROUPS])
        dt = m.sb("dt", [P, GROUPS])
        w = m.sb("w", [P, 12, GROUPS])
        pr = m.sb("pr", [P, GROUPS, STEP + 1])
        pi = m.sb("pi", [P, GROUPS, STEP + 1])
        back_r = m.sb("back_r", [P, GROUPS, STEP])
        back_i = m.sb("back_i", [P, GROUPS, STEP])
        mag8 = m.sb("mag8", [P, GROUPS])
        turn8 = m.sb("turn8", [P, GROUPS])
        b1 = m.sb("b1", [P, GROUPS, GC])
        b2 = m.sb("b2", [P, GROUPS, GC])
        c1 = m.sb("c1", [P, GROUPS, GC])
        c2 = m.sb("c2", [P, GROUPS, GC])
        bb1 = m.sb("bb1", [P, GROUPS, GC])
        bb2 = m.sb("bb2", [P, GROUPS, GC])
        skip = m.sb("skip", [GC, GROUPS, GC])
        step_i = m.sb("step_i", [P, TC], I32)
        step_no = m.sb("step_no", [P, TC])
        u_in = m.sb("u_in", [P, 2, STEP, P])
        u_grp = m.sb("u_grp", [P, 2, GB, P])
        uT = m.sb("uT", [P, GB, 2, P])
        tmp = m.sb("tmp", [P, GB, (STEP + 1) * GC])
        tmp2 = m.sb("tmp2", [P, GB, (STEP + 1) * GC])
        h_rows = m.sb("h_rows", [P, 2, GB, P])
        hT = m.sb("hT", [P, 2, GB, P])
        ca1 = m.sb("ca1", [P, GROUPS, (STEP + 1) * GC])
        g2 = m.sb("g2", [P, GROUPS, STEP * GC])
        k_out = m.sb("k_out", [GC, GB, P])
        toep = m.sb("toep", [P, GB, P])
        arg = m.sb("arg", [P, GB, TC])
        whole = m.sb("whole", [P, GB, TC])
        sin_t = m.sb("sin_t", [P, GB, TC])
        cos_t = m.sb("cos_t", [P, GB, TC])
        drive = m.sb("drive", [P, NC_])
        drive2 = m.sb("drive2", [P, NC_])
        z = m.sb("z", [P, NC_ + 1])
        xc = m.sb("xc", [P, 2, GB, NC_])
        y_tok = m.sb("y_tok", [P, 2, STEP, P])
        gel = m.sb("gel", [P, WIDTH // P, S])
        ident = keep["ident"]
        q = [m.ps(f"q{i}", [P, CH]) for i in range(8)]

        params_in = m.sem("params_in")
        consts = m.sem("consts")
        params_act = m.sem("params_act")
        params_ready = m.sem("params_ready")
        turns_ready = m.sem("turns_ready")
        u_loaded = m.sem("u_loaded")
        u_grouped = m.sem("u_grouped")
        u_turned = m.sem("u_turned")
        u_ready = m.sem("u_ready")
        rows_ready = m.sem("rows_ready")
        angles = m.sem("angles")
        waves_ready = m.sem("waves_ready")
        h_turned = m.sem("h_turned")
        h_ready = m.sem("h_ready")
        k_done = m.sem("k_done")
        k_copied = m.sem("k_copied")
        k_ready = m.sem("k_ready")
        shifted = m.sem("shifted")
        driven = m.sem("driven")
        drive_used = m.sem("drive_used")
        x_ready = m.sem("x_ready")
        y_done = m.sem("y_done")
        y_copied = m.sem("y_copied")
        y_turned = m.sem("y_turned")
        gelu_done = m.sem("gelu_done")
        own = m.sem("own")
        tick = keep["tick"]

        with nc.Block() as block:
            @block.gpsimd
            def _(pool):
                pool.iota(step_i[:, :], pattern=[[1, TC]], base=-1, channel_multiplier=0).then_inc(consts, 1)
                pool.memset(toep[:, :, :], 0.0).then_inc(consts, 1)
                pool.memset(z[:, 0:1], 0.0).then_inc(consts, 1)
                for dst, name in ((lr[:, :], "s5_lr"), (li[:, :], "s5_li"), (dt[:, :], "s5_log_dt"),
                                  (b1[:, :, :], "s5_b_ri"), (b2[:, :, :], "s5_b_ir"),
                                  (c1[:, :, :], "s5_c_ri"), (c2[:, :, :], "s5_c_ir")):
                    pool.dma_start(dst, a[name]).then_inc(params_in, 16)
                pool.dma_start(skip[:, :, :].rearrange("c g o -> c (g o)"), a["s5_d"].partition_broadcast(GC)).then_inc(params_in, 16)
                pool.wait_ge(params_in, 16 * 8)
                pool.affine_select(out=skip[:, :, :], in_=skip[:, :, :], compare_op=ALU.is_equal, fill=0.0, base=0,
                                   pattern=[[0, GROUPS], [-1, GC]], channel_multiplier=1).then_inc(consts, 1)

                def prepare(i):
                    for half in range(2):
                        src = a["u"].rearrange("(h t) p n -> h (t p) n", h=2)[half].rearrange("(c s) n -> c s n", s=STEP)
                        pool.dma_start(u_in[:, half, :, :], src[:, :, bass.ds(i * P, P)]).then_inc(u_loaded, 16)
                    wait_alone(pool, u_loaded, 32 * i + 32, tick)
                    wait_alone(pool, u_turned, 4 * i + 4, tick)
                    for half in range(2):
                        pool.tensor_copy(u_grp[:, half, :, :].rearrange("c g (s o) -> c g s o", o=GC),
                                         u_in[:, half, :, :].rearrange("c s (g o) -> c g s o", o=GC)).then_inc(u_grouped, 1)
                    gs = bass.ds(i * GB, GB)
                    full = [P, GB, TC]
                    wait_alone(pool, waves_ready, 2 * i + 2, tick)
                    pool.wait_ge(turns_ready, 1)
                    pool.tensor_tensor(arg[:, :, :], turn8[:, gs].unsqueeze(2).to_broadcast(full),
                                       step_no[:, :].unsqueeze(1).to_broadcast(full), ALU.mult).then_inc(angles, 1)
                    wait_alone(pool, angles, 4 * i + 1, tick)
                    pool.tensor_scalar(whole[:, :, :], arg[:, :, :], MAGIC, 0.0, ALU.add, ALU.add).then_inc(angles, 1)
                    wait_alone(pool, angles, 4 * i + 2, tick)
                    pool.tensor_scalar(whole[:, :, :], whole[:, :, :], MAGIC, 0.0, ALU.subtract, ALU.add).then_inc(angles, 1)
                    wait_alone(pool, angles, 4 * i + 3, tick)
                    pool.tensor_tensor(arg[:, :, :], arg[:, :, :], whole[:, :, :], ALU.subtract).then_inc(angles, 1)

                prepare(0)
                with pool.Fori(1, NB) as i:
                    wait_alone(pool, u_grouped, 2 * i, tick)
                    prepare(i)

            @block.sync
            def _(sp):
                sp.wait_ge(consts, 4)
                sp.sem_inc(shifted, 1)
                with sp.Fori(0, NB) as i:
                    wait_alone(sp, k_ready, i + 1, tick)
                    wait_alone(sp, y_done, 4 * i + 4, tick)
                    for s in range(STEP):
                        sp.dma_start(toep[s * GC:(s + 1) * GC, :, s * GC:P], k_out[:, :, 0:P - s * GC]).then_inc(shifted, 16)

            @block.scalar
            def _(act):
                act.sem_inc(waves_ready, 2)
                act.wait_ge(params_in, 16 * 8)
                nc.scalar.activation(dt[:, :], dt[:, :], ACT.Exp).then_inc(params_act, 1)
                act.wait_ge(params_ready, 1)
                nc.scalar.activation(w[:, 0, :], w[:, 4, :], ACT.Exp).then_inc(params_act, 1)
                nc.scalar.activation(mag8[:, :], w[:, 4, :], ACT.Exp, scale=float(STEP)).then_inc(params_act, 1)
                nc.scalar.activation(w[:, 1, :], w[:, 5, :], ACT.Sin).then_inc(params_act, 1)
                nc.scalar.activation(w[:, 2, :], w[:, 5, :], ACT.Sin, scale=0.5).then_inc(params_act, 1)

                def front(i):
                    for j in range(4):
                        act.wait_ge(u_turned, 4 * i + j + 1 + 4)
                        nc.scalar.activation(uT[:, 2 * j:2 * j + 2, :, :].rearrange("p g h c -> p (g h c)"), q[4 + j][:, :],
                                             ACT.Copy).then_inc(u_ready, 1)

                def front2(i):
                    for j in range(4):
                        act.wait_ge(h_turned, 4 * i + j + 1)
                        nc.scalar.activation(hT[:, j // 2, 4 * (j % 2):4 * (j % 2) + 4, :].rearrange("p g n -> p (g n)"),
                                             q[4 + j][:, :], ACT.Copy).then_inc(h_ready, 1)
                    act.wait_ge(k_done, i + 1)
                    for j in range(2):
                        nc.scalar.activation(k_out[:, 4 * j:4 * j + 4, :].rearrange("p g n -> p (g n)"), q[4 + j][0:GC, :],
                                             ACT.Copy).then_inc(k_copied, 1)
                    act.wait_ge(angles, 4 * i + 4)
                    act.wait_ge(x_ready, 2 * GB * i + 1)
                    nc.scalar.activation(sin_t[:, :, :], arg[:, :, :], ACT.Sin, scale=6.283185).then_inc(waves_ready, 1)
                    nc.scalar.activation(cos_t[:, :, :], arg[:, :, :], ACT.Sin, scale=3.1415925).then_inc(waves_ready, 1)

                def y_copies(i):
                    for j in range(4):
                        half, g4 = divmod(j, 2)
                        act.wait_ge(y_done, 4 * i + 4 + 4)
                        nc.scalar.activation(
                            y_tok[:, half, :, 64 * g4:64 * g4 + 64].rearrange("p s (g o) -> p g s o", o=GC),
                            q[j][:, :].rearrange("p (g s o) -> p g s o", g=4, o=GC), ACT.Copy).then_inc(y_copied, 1)

                def gelu(i, at):
                    gel_b = gel[:, at, :].rearrange("p (h c s) -> p h s c", h=2, s=STEP)
                    for j in range(4):
                        half, s4 = divmod(j, 2)
                        act.wait_ge(y_turned, 4 * i + j + 1)
                        nc.scalar.activation(gel_b[:, half, 4 * s4:4 * s4 + 4, :],
                                             q[j][:, :].rearrange("p (s c) -> p s c", s=4),
                                             ACT.Gelu_apprx_tanh).then_inc(gelu_done, 1)

                front(0)
                front2(0)
                with act.Fori(0, NB - 1) as i:
                    y_copies(i)
                    front(i + 1)
                    gelu(i, i)
                    front2(i + 1)
                y_copies(NB - 1)
                gelu(NB - 1, NB - 1)

            @block.tensor
            def _(pe):
                pe.sem_inc(drive_used, 4)
                pe.sem_inc(u_turned, 4)
                pe.sem_inc(y_done, 4)

                def front(i):
                    pe.wait_ge(u_grouped, 2 * i + 2)
                    pe.wait_ge(drive_used, GB * i + 4)
                    for g in range(GB):
                        for half in range(2):
                            last = nc.tensor.transpose(q[4 + g // 2][:, (g % 2) * 256 + half * P:(g % 2) * 256 + half * P + P],
                                                       u_grp[:, half, g, :], ident[:, :])
                        if g % 2:
                            last.then_inc(u_turned, 1)

                def front2(i):
                    pe.wait_ge(rows_ready, 2 * i + 1)
                    for j in range(4):
                        pe.wait_ge(u_ready, 4 * i + j + 1)
                        for g in range(4):
                            last = nc.tensor.transpose(q[4 + j][:, g * P:(g + 1) * P], h_rows[:, j // 2, 4 * (j % 2) + g, :],
                                                       ident[:, :])
                        last.then_inc(h_turned, 1)
                    pe.wait_ge(rows_ready, 2 * i + 2)
                    pe.wait_ge(h_ready, 4 * i + 4)
                    for g in range(GB):
                        last = nc.tensor.matmul(q[4 + g // 4][0:GC, (g % 4) * P:(g % 4 + 1) * P], h_rows[:, 0, g, P - GC:P],
                                                ca1[:, bass.ds(i * GB + g, 1), 0:P], start=True, stop=True)
                    last.then_inc(k_done, 1)

                def drive_of(i, g):
                    pe.wait_ge(drive_used, GB * i + g + 1)
                    for j in range(2):
                        last = nc.tensor.matmul(q[4 + g % 4][:, j * NC_:(j + 1) * NC_], hT[:, j, g, :],
                                                uT[:, g, :, :].rearrange("p h c -> p (h c)"), start=True, stop=True)
                    last.then_inc(driven, 1)

                def scan_and_outputs(i):
                    pe.wait_ge(k_copied, 2 * i + 2)
                    for g in range(4):
                        drive_of(i, g)
                    pe.wait_ge(shifted, 16 * STEP * i + 16 * STEP + 1)
                    for g in range(GB):
                        pe.wait_ge(x_ready, 2 * GB * i + 2 * g + 2 + 1)
                        for half in range(2):
                            cs = slice(half * P, half * P + P)
                            out = q[2 * half + g // 4][:, (g % 4) * P:(g % 4 + 1) * P]
                            nc.tensor.matmul(out, uT[:, g, half, :], toep[:, g, :], start=True, stop=False)
                            nc.tensor.matmul(out, xc[:, 0, g, cs], ca1[:, bass.ds(i * GB + g, 1), GC:P + GC], start=False, stop=False)
                            last = nc.tensor.matmul(out, xc[:, 1, g, cs], g2[:, bass.ds(i * GB + g, 1), :], start=False, stop=True)
                            if g % 4 == 3:
                                last.then_inc(y_done, 1)
                        if g + 4 < GB:
                            drive_of(i, g + 4)

                def turn_outputs(i):
                    pe.wait_ge(y_copied, 4 * i + 4)
                    for j in range(4):
                        half, s4 = divmod(j, 2)
                        for s in range(4):
                            last = nc.tensor.transpose(q[j][:, s * P:(s + 1) * P], y_tok[:, half, 4 * s4 + s, :], ident[:, :])
                        last.then_inc(y_turned, 1)

                front(0)
                front2(0)
                with pe.Fori(0, NB - 1) as i:
                    scan_and_outputs(i)
                    front(i + 1)
                    turn_outputs(i)
                    front2(i + 1)
                    pe.wait_ge(gelu_done, 4 * i + 4)
                scan_and_outputs(NB - 1)
                turn_outputs(NB - 1)

            @block.vector
            def _(dve):
                st = Steps(nc.vector, own)
                v, tt, ts = nc.vector, nc.vector.tensor_tensor, nc.vector.tensor_scalar
                W = lambda n: w[:, n, :]
                dve.wait_ge(consts, 4)
                dve.wait_ge(params_in, 16 * 8)
                dve.wait_ge(params_act, 1)
                st.do(ts(b2[0:NS, :, :], b2[0:NS, :, :], -1.0, None, ALU.mult))
                st.do(ts(c1[NS:P, :, :], c1[NS:P, :, :], -1.0, None, ALU.mult))
                st.do(ts(c2[:, :, :], c2[:, :, :], -1.0, None, ALU.mult))
                st.do(v.tensor_copy(step_no[:, :], step_i[:, :]))
                st.do(tt(W(4), lr[:, :], dt[:, :], ALU.mult))
                st.then(tt(W(5), li[:, :], dt[:, :], ALU.mult))
                reduce_angle(nc, st, W(5), W(6))
                dve.sem_inc(params_ready, 1)
                st.then(ts(turn8[:, :], W(5), STEP / TWO_PI, None, ALU.mult))
                st.then(ts(W(6), turn8[:, :], MAGIC, None, ALU.add))
                st.then(ts(W(6), W(6), MAGIC, None, ALU.subtract))
                tt(turn8[:, :], turn8[:, :], W(6), ALU.subtract).then_inc(turns_ready, 1)
                st.do(tt(W(7), lr[:, :], lr[:, :], ALU.mult))
                st.then(tt(W(8), li[:, :], li[:, :], ALU.mult))
                st.then(tt(W(7), W(7), W(8), ALU.add))
                st.do(v.reciprocal(W(7), W(7)))
                dve.wait_ge(params_act, 5)
                st.then(tt(W(2), W(2), W(2), ALU.mult))
                st.then(ts(W(2), W(2), -2.0, 1.0, ALU.mult, ALU.add))
                a_re, a_im = pr[:, :, 1], pi[:, :, 1]
                st.do(tt(a_re, W(0), W(2), ALU.mult))
                st.do(tt(a_im, W(0), W(1), ALU.mult))
                st.do(v.memset(pr[:, :, 0], 1.0))
                st.then(v.memset(pi[:, :, 0], 0.0))
                st.then(ts(W(3), a_re, 1.0, None, ALU.subtract))
                for n, (x, y) in enumerate(((W(3), lr), (a_im, li), (a_im, lr), (W(3), li))):
                    st.do(tt(W(8 + n), x, y[:, :], ALU.mult))
                st.join()
                st.do(tt(W(8), W(8), W(9), ALU.add))
                st.then(tt(W(10), W(10), W(11), ALU.subtract))
                st.do(tt(W(8), W(8), W(7), ALU.mult))
                st.then(tt(W(10), W(10), W(7), ALU.mult))
                for d in range(2, STEP + 1):
                    for n, (x, y) in enumerate(((pr, a_re), (pi, a_im), (pr, a_im), (pi, a_re))):
                        st.do(tt(W((0, 1, 2, 4)[n]), x[:, :, d - 1], y, ALU.mult))
                    st.join()
                    st.do(tt(pr[:, :, d], W(0), W(1), ALU.subtract))
                    st.then(tt(pi[:, :, d], W(2), W(4), ALU.add))
                for d in range(STEP):
                    st.do(v.tensor_copy(back_r[:, :, STEP - 1 - d], pr[:, :, d]))
                    st.do(v.tensor_copy(back_i[:, :, STEP - 1 - d], pi[:, :, d]))
                wide = lambda x: x.unsqueeze(2).to_broadcast([P, GROUPS, GC])
                flat = lambda x: x[:, :, :].rearrange("p g c -> p (g c)")
                ta = tmp[:, 0:4, :].rearrange("p g c -> p (g c)")[:, 0:GROUPS * GC].rearrange("p (g c) -> p g c", c=GC)
                tb = tmp2[:, 0:4, :].rearrange("p g c -> p (g c)")[:, 0:GROUPS * GC].rearrange("p (g c) -> p g c", c=GC)
                for out, x, y, op in ((bb1, b1, b2, ALU.add), (bb2, b2, b1, ALU.subtract)):
                    st.do(tt(ta, x[:, :, :], wide(W(8)), ALU.mult))
                    st.then(tt(tb, y[:, :, :], wide(W(10)), ALU.mult))
                    st.then(tt(out[:, :, :], ta, tb, op))
                before = st.n
                FRONT, per_batch = 12, 36
                dve.sem_inc(x_ready, 1)

                def front(i):
                    st = Steps(nc.vector, own, base=i * per_batch + before)
                    gs = bass.ds(i * GB, GB)

                    def rows(out, powers_r, powers_i, n, x, y, op, done=None):
                        shape = [P, GB, n, GC]
                        sr, si = (s[:, :, :].unsqueeze(3).to_broadcast(shape) for s in (powers_r, powers_i))
                        bx, by = (s[:, gs, :].unsqueeze(2).to_broadcast(shape) for s in (x, y))
                        t1, t2 = (s[:, :, 0:n * GC].rearrange("p g (s c) -> p g s c", c=GC) for s in (tmp, tmp2))
                        st.do(tt(t1, sr, bx, ALU.mult))
                        st.then(tt(t2, si, by, ALU.mult))
                        ins = tt(out.rearrange("p g (s c) -> p g s c", c=GC), t1, t2, op)
                        if done is None:
                            st.then(ins)
                        else:
                            ins.then_inc(done, 1)

                    br, bi = back_r[:, gs, :], back_i[:, gs, :]
                    rows(h_rows[:, 0, :, :], br, bi, STEP, bb1, bb2, ALU.add)
                    rows(h_rows[:, 1, :, :], bi, br, STEP, bb1, bb2, ALU.subtract, rows_ready)
                    dve.wait_ge(rows_ready, 2 * i + 1)
                    rows(g2[:, gs, :], pr[:, gs, 1:], pi[:, gs, 1:], STEP, c2, c1, ALU.subtract)
                    rows(ca1[:, gs, :], pr[:, gs, :], pi[:, gs, :], STEP + 1, c1, c2, ALU.add, rows_ready)
                    dve.wait_ge(waves_ready, 2 * i + 2 + 2)
                    st.then(tt(cos_t[:, :, :], cos_t[:, :, :], cos_t[:, :, :], ALU.mult))
                    st.then(ts(cos_t[:, :, :], cos_t[:, :, :], -2.0, 1.0, ALU.mult, ALU.add))
                    dve.wait_ge(k_copied, 2 * i + 2)
                    tt(k_out[:, :, 0:GC], k_out[:, :, 0:GC], skip[:, gs, :], ALU.add).then_inc(k_ready, 1)
                    assert st.n == FRONT, st.n

                def scan(i):
                    st = Steps(nc.vector, own, base=i * per_batch + before + FRONT)
                    for g in range(GB):
                        dve.wait_ge(driven, GB * i + g + 1)
                        st.do(tt(drive[:, :], q[4 + g % 4][:, 0:NC_], cos_t[:, g, 1:TC], ALU.mult))
                        tt(drive2[:, :], q[4 + g % 4][:, NC_:], sin_t[:, g, 1:TC], ALU.mult).then_inc(drive_used, 1)
                        dve.wait_ge(drive_used, GB * i + g + 1 + 4)
                        st.join()
                        st.then(tt(drive[:, :], drive[:, :], drive2[:, :], ALU.add))
                        st.then(v.tensor_tensor_scan(z[:, 1:NC_ + 1], mag8[:, bass.ds(i * GB + g, 1)].to_broadcast([P, NC_]),
                                                     drive[:, :], 0.0, ALU.mult, ALU.add))
                        tt(xc[:, 0, g, :], z[:, 0:NC_], cos_t[:, g, 0:NC_], ALU.mult).then_inc(x_ready, 1)
                        tt(xc[:, 1, g, :], z[:, 0:NC_], sin_t[:, g, 0:NC_], ALU.mult).then_inc(x_ready, 1)
                    assert FRONT + st.n == per_batch, st.n

                front(0)
                with dve.Fori(0, NB - 1) as i:
                    scan(i)
                    front(i + 1)
                scan(NB - 1)

        with ExitStack() as glu_ctx:
            m = Mem(nc, glu_ctx, "gl")
            over = lambda tile, k, n: tile[:, :, :].rearrange("p g c -> p (g c)")[:, 0:k * n].rearrange("p (k n) -> p k n", k=k)
            w_glu = over(arg, WIDTH // P, WIDTH)
            b_glu = m.sb("b_glu", [P, WIDTH // P])
            gate = over(whole, 2, CH)
            out = over(sin_t, 2, CH)
            loaded, mixed, gated, multiplied = m.sem("loaded"), m.sem("mixed"), m.sem("gated"), m.sem("multiplied")
            z_stored = [m.sem(f"z_stored{i}") for i in range(2)]
            NJ = WIDTH // P
            with nc.Block() as block:
                @block.sync
                def _(sp):
                    sp.dma_start(w_glu[:, :, :], a["s5_w_glu"]).then_inc(loaded, 16)
                    sp.dma_start(b_glu[:, :], a["s5_b_glu"]).then_inc(loaded, 16)
                    for n in range(4 * NJ):
                        j, c = divmod(n, 4)
                        sp.wait_ge(multiplied, n + 1)
                        sp.dma_start(a["zT"][j, :, c * CH:(c + 1) * CH], out[:, n % 2, :]).then_inc(z_stored[n % 2], 16)
                    for i in range(2):
                        sp.wait_ge(z_stored[i], 32 * NJ)

                @block.tensor
                def _(pe):
                    pe.wait_ge(loaded, 32)
                    for n in range(4 * NJ):
                        j, c = divmod(n, 4)
                        if n >= 4:
                            pe.wait_ge(gated, n - 3)
                        for k in range(NJ):
                            last = nc.tensor.matmul(q[n % 4][:, :], w_glu[:, k, j * P:(j + 1) * P],
                                                    gel[:, k, c * CH:(c + 1) * CH], start=(k == 0), stop=(k == NJ - 1))
                        last.then_inc(mixed, 1)

                @block.scalar
                def _(act):
                    act.wait_ge(loaded, 32)
                    for n in range(4 * NJ):
                        j, c = divmod(n, 4)
                        act.wait_ge(mixed, n + 1)
                        if n >= 2:
                            act.wait_ge(multiplied, n - 1)
                        nc.scalar.activation(gate[:, n % 2, :], q[n % 4][:, :], ACT.Sigmoid,
                                             bias=b_glu[:, j:j + 1]).then_inc(gated, 1)

                @block.vector
                def _(dve):
                    for n in range(4 * NJ):
                        j, c = divmod(n, 4)
                        dve.wait_ge(gated, n + 1)
                        if n >= 2:
                            dve.wait_ge(z_stored[n % 2], 16 * (n // 2))
                        nc.vector.tensor_tensor(out[:, n % 2, :], gel[:, j, c * CH:(c + 1) * CH], gate[:, n % 2, :],
                                                ALU.mult).then_inc(multiplied, 1)


def split_on_pool(pool, whole, lead, rest, leads, done, count, tick):
    pool.tensor_scalar(lead, whole, 1.0, 0.0, ALU.mult, ALU.add).then_inc(leads, 1)
    wait_alone(pool, leads, count + 1, tick)
    pool.tensor_tensor(rest, whole, lead.bitcast(F32), ALU.subtract).then_inc(done, 1)


def merge(nc, a, keep):
    HT = NT // 2
    HC = HT // 2
    HS = S // 2
    BR = 3
    KB = WIDTH // P
    NY = BR * KB
    SLOTS = 3
    with ExitStack() as ctx:
        m = Mem(nc, ctx, "me")
        h_raw = m.sb("h_raw", [P, 2, KD, P])
        h_lead = m.sb("h_lead", [P, KD, HS], F32R)
        h_rest = m.sb("h_rest", [P, KD, HS], F32R)
        y_raw = m.sb("y_raw", [P, 2, HS])
        y_lead = m.sb("y_lead", [P, KB, HS], F32R)
        y_rest = m.sb("y_rest", [P, KB, HS], F32R)
        wm_raw = m.sb("wm_raw", [P, SLOTS, KD, P])
        wm_lead = m.sb("wm_lead", [P, SLOTS, KD, P], F32R)
        wm_rest = m.sb("wm_rest", [P, SLOTS, KD, P], F32R)
        wb_raw = m.sb("wb_raw", [P, SLOTS, KB, P])
        wb_lead = m.sb("wb_lead", [P, SLOTS, KB, P], F32R)
        wb_rest = m.sb("wb_rest", [P, SLOTS, KB, P], F32R)
        gate = m.sb("gate", [P, 2, CH])
        part = m.sb("part", [P, CH])
        both = m.sb("both", [P, KD, HS])
        a_ps = [m.ps(f"a{i}", [P, CH]) for i in range(4)]
        m_ps = [m.ps(f"m{i}", [P, CH]) for i in range(2)]
        o_ps = [m.ps(f"o{i}", [P, CH]) for i in range(2)]

        h_in = [m.sem(f"h_in{b}") for b in range(2)]
        y_in = [m.sem(f"y_in{b}") for b in range(2)]
        wm_in = [m.sem(f"wm_in{i}") for i in range(SLOTS)]
        wb_in = [m.sem(f"wb_in{i}") for i in range(SLOTS)]
        leads = m.sem("leads")
        h_split0 = m.sem("h_split0")
        h_lead1 = m.sem("h_lead1")
        h_split1 = m.sem("h_split1")
        wm_split = m.sem("wm_split")
        wb_split = m.sem("wb_split")
        group_done = m.sem("group_done")
        a_free = m.sem("a_free")
        m_free = m.sem("m_free")
        o_free = m.sem("o_free")
        g_sig = m.sem("g_sig")
        gated = m.sem("gated")
        y_leads = m.sem("y_leads")
        y_split = m.sem("y_split")
        gate_used = m.sem("gate_used")
        merged = m.sem("merged")
        stored = m.sem("stored")
        tick = keep["tick"]

        wm_tiles, wb_tiles, order = [], [], []
        for br in range(BR):
            pairs = [(b, c) for b in range(KB) for c in range(2)]
            if br == 0:
                pairs[1], pairs[2] = pairs[2], pairs[1]
            base = len(wm_tiles)
            wm_tiles += [("w_gate", br * KB + b) for b in range(KB)]
            order += [("gate", base + b, br * KB + b, br, c) for b, c in pairs]
            cut = KD - 3 if br == BR - 1 else KD
            for js, cs in [([j], (0, 1)) for j in range(cut)] + [(range(cut, KD), (c,)) for c in range(2)]:
                for j in js:
                    order += [("job", len(wm_tiles), len(wb_tiles), (j, br), c) for c in cs]
                    wm_tiles.append(("w_merge", (j, br)))
                    wb_tiles.append((j, br))
        NG, NJ = (sum(o[0] == kind for o in order) for kind in ("gate", "job"))
        NM, NB_ = len(wm_tiles), len(wb_tiles)
        GROUPS_ = NG + 2 * NJ
        assert NG == 2 * NY and NM % SLOTS == 0 and NB_ % SLOTS == 0 and NJ % 2 == 0 and NG % 4 == 0
        wm_last, wb_last, h_last, br_last, block_gated = {}, {}, {}, {}, {}
        group = 0
        for n, (kind, w, b, what, c) in enumerate(order):
            if kind == "gate":
                wm_last[w] = h_last[c] = group
                group += 1
                block_gated[b] = sum(o[0] == "gate" for o in order[:n + 1])
            else:
                wm_last[w] = h_last[c] = group
                wb_last[b] = br_last[what[1]] = group + 1
                group += 2

        with nc.Block() as block:
            @block.sync
            def _(sp):
                with sp.Fori(0, 2) as i:
                    def load_h(t):
                        if t < 2:
                            wait_alone(sp, h_split1, HC * i + t + 1, tick)
                        elif t < HC + 2:
                            wait_alone(sp, h_split0, HC * i + t - 1 + 2, tick)
                        else:
                            wait_alone(sp, h_split1, HC * i + t - 1 - HC + 2, tick)
                        sp.dma_start(h_raw[:, t % 2, :, :], a["hT"][i * HT + t].rearrange("p (k t) -> p k t", t=P)).then_inc(h_in[t % 2], 16)

                    def load_wm(n):
                        wait_alone(sp, wm_split, NM * i + n + 1, tick)
                        name, at = wm_tiles[n]
                        sp.dma_start(wm_raw[:, n % SLOTS, :, :], a[name][at]).then_inc(wm_in[n % SLOTS], 16)

                    def load_wb(n):
                        wait_alone(sp, wb_split, NB_ * i + n + 1, tick)
                        sp.dma_start(wb_raw[:, n % SLOTS, :, :], a["w_branch"][wb_tiles[n]]).then_inc(wb_in[n % SLOTS], 16)

                    def load_y(b):
                        if b >= 2:
                            wait_alone(sp, gated, NG * (i + 1) + block_gated[b - 2], tick)
                        else:
                            wait_alone(sp, gated, NG * i + block_gated[NY - 2 + b], tick)
                        if b < 8:
                            src = a["yT"].rearrange("x (j e) d t -> (x j) (e d) t", e=2)[b]
                        else:
                            src = a["zT"][b - 8]
                        sp.dma_start(y_raw[:, b % 2, :], src[:, bass.ds(i * HS, HS)]).then_inc(y_in[b % 2], 16)

                    for t in range(HC):
                        load_h(t)
                    n_b = n_y = 0
                    for n, (name, at) in enumerate(wm_tiles):
                        load_wm(n)
                        if name == "w_gate":
                            load_y(n_y)
                            n_y += 1
                        else:
                            load_wb(n_b)
                            n_b += 1
                        if n == 1:
                            for t in range(HC, HT):
                                load_h(t)

            @block.gpsimd
            def _(pool):
                pool.sem_inc(h_split0, 2)
                pool.sem_inc(wm_split, SLOTS)
                pool.sem_inc(wb_split, SLOTS)
                PER_TURN = HC + NM + NB_
                with pool.Fori(0, 2) as i:
                    n_split = 0

                    def reuse(last, this_turn):
                        wait_alone(pool, group_done, GROUPS_ * (i + (1 if this_turn else 0)) + last + 1, tick)

                    reuse(h_last[0], False)
                    for t in range(HC):
                        wait_alone(pool, h_in[t % 2], 16 * (HT // 2) * i + 16 * (t // 2) + 16, tick)
                        ts = slice(t * P, (t + 1) * P)
                        split_on_pool(pool, h_raw[:, t % 2, :, :], h_lead[:, :, ts], h_rest[:, :, ts], leads, h_split0,
                                      PER_TURN * i + n_split, tick)
                        n_split += 1

                    n_b = 0
                    for n, (name, at) in enumerate(wm_tiles):
                        s = n % SLOTS
                        wait_alone(pool, wm_in[s], 16 * (NM // SLOTS) * i + 16 * (n // SLOTS) + 16, tick)
                        reuse(wm_last[(n - SLOTS) % NM], n >= SLOTS)
                        split_on_pool(pool, wm_raw[:, s, :, :], wm_lead[:, s, :, :], wm_rest[:, s, :, :], leads, wm_split,
                                      PER_TURN * i + n_split, tick)
                        n_split += 1
                        if name == "w_merge":
                            s = n_b % SLOTS
                            wait_alone(pool, wb_in[s], 16 * (NB_ // SLOTS) * i + 16 * (n_b // SLOTS) + 16, tick)
                            reuse(wb_last[(n_b - SLOTS) % NB_], n_b >= SLOTS)
                            split_on_pool(pool, wb_raw[:, s, :, :], wb_lead[:, s, :, :], wb_rest[:, s, :, :], leads, wb_split,
                                          PER_TURN * i + n_split, tick)
                            n_split += 1
                            n_b += 1

            @block.tensor
            def _(pe):
                def product(bank, w, w_at, v, cs, blocks):
                    for k in range(blocks):
                        first, second = w[0][:, w_at, k, :], w[1][:, w_at, k, :]
                        nc.tensor.matmul(bank[:, :], first, v[1][:, k, cs], start=k == 0, stop=False)
                        nc.tensor.matmul(bank[:, :], first, v[0][:, k, cs], start=False, stop=False)
                        last = nc.tensor.matmul(bank[:, :], second, v[0][:, k, cs], start=False, stop=k == blocks - 1)
                    last.then_inc(group_done, 1)

                pe.sem_inc(group_done, GROUPS_)
                with pe.Fori(0, 2) as i:
                    n_a = n_m = 0
                    for kind, w, b, what, c in order:
                        cs = slice(c * CH, (c + 1) * CH)
                        if n_a + n_m in (0, 2) and kind == "gate":
                            pe.wait_ge((h_split0, h_split1)[c], HC * i + HC + 2)
                        pe.wait_ge(wm_split, NM * i + w + 1 + SLOTS)
                        if kind == "gate":
                            pe.wait_ge(a_free, NG * i + n_a + 1)
                            product(a_ps[n_a % 4], (wm_lead, wm_rest), w % SLOTS, (h_lead, h_rest), cs, KD)
                            n_a += 1
                        else:
                            pe.wait_ge(m_free, NJ * i + n_m + 1)
                            product(m_ps[n_m % 2], (wm_lead, wm_rest), w % SLOTS, (h_lead, h_rest), cs, KD)
                            if what[0] == 0 and c == 0:
                                pe.wait_ge(y_split, NG * i + 2 * KB * (what[1] + 1))
                            pe.wait_ge(wb_split, NB_ * i + b + 1 + SLOTS)
                            pe.wait_ge(o_free, NJ * i + n_m + 1)
                            product(o_ps[n_m % 2], (wb_lead, wb_rest), b % SLOTS, (y_lead, y_rest), cs, KB)
                            n_m += 1

            @block.scalar
            def _(act):
                act.sem_inc(m_free, 2)
                act.sem_inc(stored, 1)
                with act.Fori(0, 2) as i:
                    for t in range(HC, HT):
                        act.wait_ge(h_in[t % 2], 16 * (HT // 2) * i + 16 * (t // 2) + 16)
                        ts = slice(t * P, (t + 1) * P)
                        if t == HC:
                            act.wait_ge(group_done, GROUPS_ * i + h_last[1] + 1)
                        nc.scalar.activation(h_lead[:, :, ts], h_raw[:, t % 2, :, :], ACT.Copy).then_inc(h_lead1, 1)
                    n_g = n_a = n_m = group = 0
                    waiting = []

                    def sigmoid(src, done):
                        act.wait_ge(gate_used, (NG + NJ) * i + n_g + 1)
                        nc.scalar.activation(gate[:, n_g % 2, :], src, ACT.Sigmoid).then_inc(done, 1)

                    def lead_of_y(n, b, c, g):
                        act.wait_ge(gated, NG * (i + 1) + n + 1)
                        if n % (2 * KB) == 0:
                            br = n // (2 * KB)
                            act.wait_ge(group_done, GROUPS_ * (i + (1 if br else 0)) + br_last[(br - 1) % BR] + 1)
                        nc.scalar.activation(y_lead[:, b % KB, c * CH:(c + 1) * CH], gate[:, g % 2, :], ACT.Copy).then_inc(y_leads, 1)

                    def store(n, j, c):
                        act.wait_ge(merged, NJ * i + n + 1)
                        cs = slice(c * CH, (c + 1) * CH)
                        act.dma_start(a["both"][2 * i + c][:, j, :], both[:, j, cs]).then_inc(stored, 16)

                    late = None
                    for kind, w, b, what, c in order:
                        act.wait_ge(group_done, GROUPS_ * (i + 1) + group + 1)
                        if kind == "gate":
                            sigmoid(a_ps[n_a % 4][:, :], g_sig)
                            if late:
                                lead_of_y(*late)
                            late = (n_a, b, c, n_g)
                            n_a += 1
                            group += 1
                            if n_a % (2 * KB) == 0:
                                lead_of_y(*late)
                                late = None
                        else:
                            sigmoid(m_ps[n_m % 2][:, :], m_free)
                            if what[1] == BR - 1:
                                waiting.append((n_m, what[0], c))
                            if len(waiting) > 2:
                                store(*waiting.pop(0))
                            n_m += 1
                            group += 2
                        n_g += 1
                    while waiting:
                        store(*waiting.pop(0))
                act.wait_ge(stored, 16 * 2 * 2 * KD + 1)

            @block.vector
            def _(dve):
                dve.sem_inc(h_split1, 2)
                dve.sem_inc(a_free, 4)
                dve.sem_inc(o_free, 2)
                dve.sem_inc(gate_used, 2)
                dve.sem_inc(gated, NG)
                tt = nc.vector.tensor_tensor
                with dve.Fori(0, 2) as i:
                    for t in range(HC, HT):
                        ts = slice(t * P, (t + 1) * P)
                        dve.wait_ge(h_lead1, HC * i + t - HC + 1)
                        tt(h_rest[:, :, ts], h_raw[:, t % 2, :, :], h_lead[:, :, ts].bitcast(F32), ALU.subtract).then_inc(h_split1, 1)

                    def rest_of_y(n, b, c, g):
                        dve.wait_ge(y_leads, NG * i + n + 1)
                        at = (b % KB, slice(c * CH, (c + 1) * CH))
                        tt(y_rest[:, at[0], at[1]], gate[:, g % 2, :], y_lead[:, at[0], at[1]].bitcast(F32),
                           ALU.subtract).then_inc(y_split, 1)
                        dve.wait_ge(y_split, NG * i + n + 1)
                        dve.sem_inc(gate_used, 1)

                    n_g = n_a = n_m = group = 0
                    late = None
                    for kind, w, b, what, c in order:
                        g, cs = gate[:, n_g % 2, :], slice(c * CH, (c + 1) * CH)
                        if kind == "gate":
                            dve.wait_ge(g_sig, NG * i + n_a + 1)
                            tt(g, a_ps[n_a % 4][:, :], g, ALU.mult).then_inc(a_free, 1)
                            dve.wait_ge(y_in[b % 2], 16 * (NY // 2) * i + 16 * (b // 2) + 16)
                            dve.wait_ge(a_free, NG * i + n_a + 1 + 4)
                            tt(g, y_raw[:, b % 2, cs], g, ALU.mult).then_inc(gated, 1)
                            if late:
                                rest_of_y(*late)
                            late = (n_a, b, c, n_g)
                            n_a += 1
                            group += 1
                            if n_a % (2 * KB) == 0:
                                rest_of_y(*late)
                                late = None
                        else:
                            j, br = what
                            dve.wait_ge(m_free, NJ * i + n_m + 1 + 2)
                            dve.wait_ge(group_done, GROUPS_ * (i + 1) + group + 2)
                            dst, o = both[:, j, cs], o_ps[n_m % 2][:, :]
                            if br == 0:
                                if n_m == 0:
                                    dve.wait_ge(stored, 16 * 2 * KD * i + 1)
                                tt(dst, o, g, ALU.mult).then_inc(merged, 1)
                                dve.wait_ge(merged, NJ * i + n_m + 1)
                                dve.sem_inc(o_free, 1)
                            else:
                                dve.wait_ge(merged, NJ * i + n_m)
                                tt(part[:, :], o, g, ALU.mult).then_inc(o_free, 1)
                                dve.wait_ge(o_free, NJ * i + n_m + 1 + 2)
                                tt(dst, dst, part[:, :], ALU.add).then_inc(merged, 1)
                            dve.sem_inc(gate_used, 1)
                            n_m += 1
                            group += 2
                        n_g += 1


def output(nc, a, keep):
    SLOTS = 4
    with ExitStack() as ctx:
        m = Mem(nc, ctx, "ou")
        w_raw = m.sb("w_raw", [P, KD, D])
        w_lead = m.sb("w_lead", [P, KD, D], F32R)
        w_rest = m.sb("w_rest", [P, KD, D], F32R)
        b_raw = m.sb("b_raw", [P, SLOTS, KD, P])
        b_lead = m.sb("b_lead", [P, SLOTS, KD, P], F32R)
        b_rest = m.sb("b_rest", [P, SLOTS, KD, P], F32R)
        x_in = m.sb("x_in", [P, SLOTS, D])
        out = m.sb("out", [P, 2, D])
        ps = [m.ps(f"ps{i}", [P, CH]) for i in range(4)]

        w_in = [m.sem(f"w_in{c}") for c in range(2)]
        w_leads = m.sem("w_leads")
        w_split = m.sem("w_split")
        tile_in = [m.sem(f"tile_in{s}") for s in range(SLOTS)]
        leads = m.sem("leads")
        b_split = m.sem("b_split")
        full = m.sem("full")
        added = m.sem("added")
        stored = [m.sem(f"stored{s}") for s in range(2)]
        tick = keep["tick"]

        with nc.Block() as block:
            @block.sync
            def _(sp):
                sp.sem_inc(full, 2 * SLOTS)
                sp.sem_inc(added, 2 * SLOTS)

                with sp.Fori(0, NT // SLOTS) as i:
                    for s in range(SLOTS):
                        wait_alone(sp, full, 2 * SLOTS * i + 2 * s + 2, tick)
                        sp.dma_start(b_raw[:, s, :, :], a["both"][i][:, :, s * P:(s + 1) * P]).then_inc(tile_in[s], 16)
                        wait_alone(sp, added, 2 * SLOTS * i + 2 * s + 2, tick)
                        sp.dma_start(x_in[:, s, :], a["x"][i * SLOTS + s]).then_inc(tile_in[s], 16)

            @block.gpsimd
            def _(pool):
                with pool.Fori(0, NT // SLOTS) as i:
                    for s in range(SLOTS):
                        wait_alone(pool, tile_in[s], 32 * i + 32, tick)
                        split_on_pool(pool, b_raw[:, s, :, :], b_lead[:, s, :, :], b_rest[:, s, :, :], leads, b_split,
                                      SLOTS * i + s, tick)

            @block.scalar
            def _(act):
                for c in range(2):
                    act.dma_start(w_raw[:, :, c * CH:(c + 1) * CH], a["w_out"][:, :, c * CH:(c + 1) * CH]).then_inc(w_in[c], 16)
                for c, k in ((c, k) for c in range(2) for k in range(0, KD, 2)):
                    act.wait_ge(w_in[c], 16)
                    at = (slice(None), slice(k, k + 2), slice(c * CH, (c + 1) * CH))
                    nc.scalar.activation(w_lead[at], w_raw[at], ACT.Copy).then_inc(w_leads, 1)
                for s in range(2):
                    act.sem_inc(stored[s], 1)
                with act.Fori(0, NT // SLOTS) as i:
                    for s in range(SLOTS):
                        act.wait_ge(added, 2 * SLOTS * (i + 1) + 2 * s + 2)
                        act.dma_start(a["out"][i * SLOTS + s], out[:, s % 2, :]).then_inc(stored[s % 2], 16)
                for s in range(2):
                    act.wait_ge(stored[s], 16 * (NT // 2) + 1)

            @block.tensor
            def _(pe):
                with pe.Fori(0, NT // SLOTS) as i:
                    for s in range(SLOTS):
                        pe.wait_ge(b_split, SLOTS * i + s + 1)
                        for c in range(2):
                            n = 2 * s + c
                            cs = slice(c * CH, (c + 1) * CH)
                            pe.wait_ge(added, 2 * SLOTS * i + n + 5)
                            for k in range(KD):
                                if n < 2 and k % 2 == 0:
                                    pe.wait_ge(w_split, n * (KD // 2) + k // 2 + 1)
                                nc.tensor.matmul(ps[n % 4][:, :], b_lead[:, s, k, :], w_rest[:, k, cs], start=k == 0, stop=False)
                                nc.tensor.matmul(ps[n % 4][:, :], b_lead[:, s, k, :], w_lead[:, k, cs], start=False, stop=False)
                                last = nc.tensor.matmul(ps[n % 4][:, :], b_rest[:, s, k, :], w_lead[:, k, cs],
                                                        start=False, stop=k == KD - 1)
                            last.then_inc(full, 1)

            @block.vector
            def _(dve):
                for n in range(KD):
                    c, k = divmod(2 * n, KD)
                    at = (slice(None), slice(k, k + 2), slice(c * CH, (c + 1) * CH))
                    dve.wait_ge(w_leads, n + 1)
                    nc.vector.tensor_tensor(w_rest[at], w_raw[at], w_lead[at].bitcast(F32), ALU.subtract).then_inc(w_split, 1)
                with dve.Fori(0, NT // SLOTS) as i:
                    for s in range(SLOTS):
                        dve.wait_ge(tile_in[s], 32 * i + 32)
                        dve.wait_ge(stored[s % 2], 16 * (2 * i + s // 2) + 1)
                        for c in range(2):
                            n = 2 * s + c
                            cs = slice(c * CH, (c + 1) * CH)
                            dve.wait_ge(full, 2 * SLOTS * (i + 1) + n + 1)
                            nc.vector.tensor_tensor(out[:, s % 2, cs], ps[n % 4][:, :], x_in[:, s, cs], ALU.add).then_inc(added, 1)


def build(nc, a):
    scratch = {"hT": (NT, P, D), "mqT": (H, MQ, S), "mkT": (H, MQ, S), "fqT": (H, FQ, S), "fkT": (H, FQ, S),
               "mv": (NT, P, WIDTH), "fv": (NT, P, WIDTH), "u": (NT, P, WIDTH), "yT": (2, H, HD, S), "row_sum": (2, H, 1, S),
               "row_inv": (2, H, 1, S), "both": (NT // 4, P, KD, CH),
               "zT": (WIDTH // P, P, S)}
    a = dict(a)
    for name, shape in scratch.items():
        a[name] = nc.dram_tensor(f"scratch_{name}", shape, F32).ap()
    with ExitStack() as ctx:
        keep = {"ident": ctx.enter_context(nc.sbuf_tensor("ident", [P, P], F32)),
                "tick": ctx.enter_context(nc.semaphore("tick")),
                "cum": ctx.enter_context(nc.sbuf_tensor("cum", [P, NT, H, 2], F32))}
        with ExitStack() as weights:
            for key in ("wq_lead", "wq_rest"):
                keep[key] = weights.enter_context(nc.sbuf_tensor(key, [P, KD, LQ], F32R))
            norm_x(nc, a, keep)
            project(nc, a, keep)
        s5(nc, a, keep)
        attend(nc, a, keep)
        merge(nc, a, keep)
        output(nc, a, keep)


def layout(inputs):
    f = {k: np.asarray(v) for k, v in inputs.items()}
    one = {k: v[0] for k, v in f.items() if k not in ("positions",)}
    rows = lambda w: w.reshape(-1, P, w.shape[-1]).transpose(1, 0, 2)
    w = one["w_in"]
    cut = np.cumsum([0, Q_RANK, KV_RANK, ROPE, WIDTH, WIDTH, WIDTH, H, WIDTH, WIDTH, WIDTH, WIDTH, D, D, D])
    cols = lambda i, j: w[:, cut[i]:cut[j]]

    def tiles(w):
        k, j = w.shape[0] // P, w.shape[1] // P
        return w.reshape(k, P, j, P).transpose(2, 1, 0, 3)

    stack = lambda x, y: np.concatenate([x, y], axis=0)
    state = lambda x: x.transpose(1, 0)
    br, bi = (one[k].transpose(1, 0, 2) for k in ("s5_b_re", "s5_b_im"))
    cr, ci = (one[k].transpose(2, 0, 1) for k in ("s5_c_re", "s5_c_im"))
    merge_w = tiles(cols(11, 14)).reshape(3, KD, P, KD, P).transpose(1, 0, 2, 3, 4)
    branch_w = np.stack([tiles(one["w_branch_out"][b * WIDTH:(b + 1) * WIDTH]) for b in range(3)], axis=1)
    col = lambda v: v.reshape(-1, 1)
    out = {
        "x": one["x"].reshape(NT, P, D),
        "positions": f["positions"].reshape(NT, P).transpose(1, 0),
        "inv_freq": np.broadcast_to((1.0 / (np.float32(10000.0) ** (np.arange(0, ROPE, 2, dtype=np.float32) / np.float32(ROPE)))).astype(np.float32), (P, ROPE // 2)),
        "norm_g": one["norm_g"].reshape(KD, P).transpose(1, 0),
        "w_ff": rows(cols(6, 7)), "fox_b_f": one["fox_b_f"],
        "w_lq": rows(cols(0, 4)), "w_fk": rows(cols(4, 5)),
        "w_vu": rows(np.concatenate([cols(5, 6), cols(7, 8)], axis=1)),
        "w_q_up": rows(one["mla_w_q_up"]), "w_kv_up": one["mla_w_kv_up"],
        "gain_lora": np.concatenate([one["mla_q_a_norm"], one["mla_kv_a_norm"]]).reshape(3, P).transpose(1, 0),
        "fox_q_norm": col(one["fox_q_norm"]), "fox_k_norm": col(one["fox_k_norm"]),
        "mla_q_norm": col(one["mla_q_norm"]), "mla_k_norm": col(one["mla_k_norm"]),
        "s5_lr": stack(state(one["s5_lambda_re"]), state(one["s5_lambda_re"])),
        "s5_li": stack(state(one["s5_lambda_im"]), state(one["s5_lambda_im"])),
        "s5_log_dt": np.broadcast_to(one["s5_log_dt"], (P, GROUPS)),
        "s5_b_ri": stack(br, bi), "s5_b_ir": stack(bi, br), "s5_c_ri": stack(cr, ci), "s5_c_ir": stack(ci, cr),
        "s5_d": one["s5_d"], "s5_w_glu": rows(one["s5_w_glu"]), "s5_b_glu": one["s5_b_glu"].reshape(-1, P).transpose(1, 0),
        "w_gate": tiles(cols(8, 11)), "w_merge": merge_w, "w_branch": branch_w, "w_out": rows(one["w_out"]),
    }
    return {k: np.ascontiguousarray(v) for k, v in out.items()}


def kernel(**inputs):
    import concourse.bacc as bacc
    from concourse.bass_utils import run_bass_kernel_spmd

    nc = bacc.Bacc("TRN2", target_bir_lowering=False, num_devices=1)
    arrays = {f"in_{k}": v for k, v in layout(inputs).items()}
    a = {k[3:]: nc.dram_tensor(k, v.shape, mybir.dt.from_np(v.dtype), kind="ExternalInput").ap() for k, v in arrays.items()}
    a["out"] = nc.dram_tensor("out", (NT, P, D), F32, kind="ExternalOutput").ap()
    build(nc, a)
    result = run_bass_kernel_spmd(nc, [arrays], core_ids=[0])
    return result.results[0]["out"].reshape(1, S, D)
```
